# Optimizing a Trainium2 kernel written in Bass

```python
import math
import jax, jax.numpy as jnp
from jax import lax
import numpy as np

D_MODEL = 1024
BATCH = 1
SEQ = 512
DEPTH = 2

PLE_DIM = 256
N_A_LAYERS = DEPTH // 2
N_B_LAYERS = DEPTH - N_A_LAYERS
N_DENSE_LAYERS = (DEPTH + 1) // 2
N_MOE_LAYERS = DEPTH // 2

RWKV_HEAD = 64
RWKV_HEADS = D_MODEL // RWKV_HEAD
DECAY_LORA = 64
ICLR_LORA = 64
GATE_LORA = 128
GN_EPS = 64e-5

N_HEADS = 16
HEAD_DIM = D_MODEL // N_HEADS
N_KV_GROUPS = 4
Q_PER_GROUP = N_HEADS // N_KV_GROUPS
N_BRANCH = 3
CMP_LEN = 32
CMP_STRIDE = 16
CMP_HIDDEN = 256
SEL_BLOCK = 64
N_SEL = 8
WINDOW = 512
Q_CHUNK = 32
ROPE_THETA = 10000.0

D_FF = 2816
N_EXPERTS = 8
TOP_K = 2
D_FF_EXPERT = 1408
MOE_ROWS = 256

LN_EPS = 1e-5
DEEPNORM_ALPHA = (2.0 * DEPTH) ** 0.25
DEEPNORM_BETA = (8.0 * DEPTH) ** -0.25
NEG_INF = -1e30
FORCE_SCORE = 1e4

kernel_name = "yoco_rwkv7_nsa_moe_deepnorm"

def layer_norm(x, g, b):
    xf = x.astype(jnp.float32)
    mu = jnp.mean(xf, -1, keepdims=True)
    var = jnp.mean(jnp.square(xf - mu), -1, keepdims=True)
    return ((xf - mu) * lax.rsqrt(var + LN_EPS) * g + b).astype(x.dtype)

def rope(x, pos):
    half = x.shape[-1] // 2
    inv = ROPE_THETA ** (-jnp.arange(half, dtype=jnp.float32) / half)
    ang = pos.astype(jnp.float32)[:, None] * inv[None, :]
    cos, sin = jnp.cos(ang), jnp.sin(ang)
    xf = x.astype(jnp.float32)
    x1, x2 = xf[..., :half], xf[..., half:]
    return jnp.concatenate([x1 * cos - x2 * sin, x2 * cos + x1 * sin], -1).astype(x.dtype)

def masked_softmax(s, mask):
    s = jnp.where(mask, s.astype(jnp.float32), NEG_INF)
    p = jax.nn.softmax(s, axis=-1)
    return jnp.where(mask, p, 0.0)

def token_shift(x):
    return jnp.pad(x, ((0, 0), (1, 0), (0, 0)))[:, :-1]

def rwkv7_time_mix(x, mu, w_rkv, w0, w1, w2, a0, a1, a2, g1, g2, k_k, k_a, r_k, gn_g, gn_b, w_o):
    B, T, D = x.shape
    H, N = RWKV_HEADS, RWKV_HEAD
    xx = token_shift(x) - x
    mix = lambda i: x + xx * mu[i]
    rkv = jnp.einsum('mbtd,mde->mbte', jnp.stack([mix(0), mix(1), mix(2)]), w_rkv)
    w = -jax.nn.softplus(-(w0 + jnp.tanh(mix(3) @ w1) @ w2)) - 0.5
    a = jax.nn.sigmoid(a0 + (mix(4) @ a1) @ a2)
    g = jax.nn.sigmoid(mix(5) @ g1) @ g2
    heads = lambda z: z.reshape(B, T, H, N).astype(jnp.float32)
    r, k, v, w, a = heads(rkv[0]), heads(rkv[1]), heads(rkv[2]), heads(w), heads(a)
    kk = k * k_k.reshape(H, N).astype(jnp.float32)
    kk = kk / jnp.maximum(jnp.sqrt(jnp.sum(kk * kk, -1, keepdims=True)), 1e-12)
    k = k * (1.0 + (a - 1.0) * k_a.reshape(H, N).astype(jnp.float32))
    decay = jnp.exp(-jnp.exp(w))

    def step(S, inp):
        r_t, k_t, v_t, d_t, kk_t, a_t = inp
        sk = jnp.einsum('bhij,bhj->bhi', S, kk_t)
        S = (S * d_t[:, :, None, :] - sk[..., :, None] * (kk_t * a_t)[:, :, None, :]
             + v_t[..., :, None] * k_t[:, :, None, :])
        return S, jnp.einsum('bhij,bhj->bhi', S, r_t)

    S0 = jnp.zeros((B, H, N, N), jnp.float32)
    seq = tuple(jnp.moveaxis(z, 1, 0) for z in (r, k, v, decay, kk, a))
    _, out = lax.scan(step, S0, seq)
    out = jnp.moveaxis(out, 0, 1)
    mu_o = jnp.mean(out, -1, keepdims=True)
    var_o = jnp.mean(jnp.square(out - mu_o), -1, keepdims=True)
    out = ((out - mu_o) * lax.rsqrt(var_o + GN_EPS)).reshape(B, T, D) * gn_g + gn_b
    bonus = jnp.sum(r * k * r_k.reshape(H, N).astype(jnp.float32), -1, keepdims=True) * v
    out = out + bonus.reshape(B, T, D)
    return (out * g).astype(x.dtype) @ w_o

def nsa_shared_kv(s, w_kv, cmp_pos, phi_w1, phi_b1, phi_w2):
    B, T, _ = s.shape
    G, dh = N_KV_GROUPS, HEAD_DIM
    kv = jnp.transpose((s @ w_kv).reshape(B, T, 6, G, dh), (2, 0, 3, 1, 4))
    pos = jnp.arange(T)
    n_cmp = (T - CMP_LEN) // CMP_STRIDE + 1
    idx = jnp.arange(n_cmp)[:, None] * CMP_STRIDE + jnp.arange(CMP_LEN)[None, :]

    def compress(z, j):
        blk = z[:, :, idx, :] + cmp_pos[j]
        blk = blk.reshape(B, G, n_cmp, CMP_LEN * dh)
        return jax.nn.gelu(blk @ phi_w1[j] + phi_b1[j]) @ phi_w2[j]

    k_cmp = compress(kv[0], 0)
    v_cmp = compress(kv[1], 1)
    k_slc = rope(kv[2], pos)
    k_win = rope(kv[4], pos)
    return (k_cmp, v_cmp, k_slc, kv[3], k_win, kv[5])

def nsa_attention(h, shared, w_in, w_o):
    B, T, D = h.shape
    G, R, dh, H = N_KV_GROUPS, Q_PER_GROUP, HEAD_DIM, N_HEADS
    k_cmp, v_cmp, k_slc, v_slc, k_win, v_win = shared
    proj = h @ w_in
    q = proj[..., :H * dh].reshape(B, T, G, R, dh).transpose(0, 2, 3, 1, 4)
    gates = jax.nn.sigmoid(proj[..., H * dh:].astype(jnp.float32))
    gates = gates.reshape(B, T, G, R, N_BRANCH).transpose(0, 2, 3, 1, 4)
    pos = jnp.arange(T)
    q_rot = rope(q, pos)
    scale = HEAD_DIM ** -0.5

    n_cmp = k_cmp.shape[2]
    n_blk = T // SEL_BLOCK
    n_pick = min(N_SEL, n_blk)
    cmp_start = jnp.arange(n_cmp) * CMP_STRIDE
    cmp_end = cmp_start + CMP_LEN - 1
    blk_start = jnp.arange(n_blk) * SEL_BLOCK
    blk_ids = jnp.arange(n_blk)
    overlap = ((cmp_start[:, None] < blk_start[None, :] + SEL_BLOCK)
               & (cmp_end[:, None] >= blk_start[None, :])).astype(jnp.float32)
    k_blk = k_slc.reshape(B, G, n_blk, SEL_BLOCK, dh)
    v_blk = v_slc.reshape(B, G, n_blk, SEL_BLOCK, dh)
    k_win_pad = jnp.pad(k_win, ((0, 0), (0, 0), (WINDOW, 0), (0, 0)))
    v_win_pad = jnp.pad(v_win, ((0, 0), (0, 0), (WINDOW, 0), (0, 0)))
    bi = jnp.arange(B)[:, None, None, None]
    gi = jnp.arange(G)[None, :, None, None]
    n_chunks = T // Q_CHUNK
    span = WINDOW + Q_CHUNK

    def attend_chunk(args):
        c, q_c, qr_c, g_c = args
        t = c * Q_CHUNK + jnp.arange(Q_CHUNK)
        s = jnp.einsum('bgrqd,bgnd->bgrqn', q_c, k_cmp) * scale
        p_cmp = masked_softmax(s, cmp_end[None, :] <= t[:, None])
        o_cmp = jnp.einsum('bgrqn,bgnd->bgrqd', p_cmp.astype(v_cmp.dtype), v_cmp)
        imp = jnp.einsum('bgrqn,ns->bgqs', p_cmp, overlap)
        cur = t // SEL_BLOCK
        forced = ((blk_ids[None, :] == 0) | (blk_ids[None, :] == cur[:, None])
                  | (blk_ids[None, :] == cur[:, None] - 1))
        causal_blk = blk_start[None, :] <= t[:, None]
        imp = jnp.where(forced, FORCE_SCORE, jnp.where(causal_blk, imp, NEG_INF))
        _, sel = lax.top_k(imp, n_pick)
        k_sel = k_blk[bi, gi, sel].reshape(B, G, Q_CHUNK, n_pick * SEL_BLOCK, dh)
        v_sel = v_blk[bi, gi, sel].reshape(B, G, Q_CHUNK, n_pick * SEL_BLOCK, dh)
        key_pos = (sel[..., None] * SEL_BLOCK + jnp.arange(SEL_BLOCK)).reshape(B, G, Q_CHUNK, -1)
        s = jnp.einsum('bgrqd,bgqkd->bgrqk', qr_c, k_sel) * scale
        p = masked_softmax(s, (key_pos <= t[None, None, :, None])[:, :, None])
        o_slc = jnp.einsum('bgrqk,bgqkd->bgrqd', p.astype(v_sel.dtype), v_sel)
        kw = lax.dynamic_slice_in_dim(k_win_pad, c * Q_CHUNK, span, axis=2)
        vw = lax.dynamic_slice_in_dim(v_win_pad, c * Q_CHUNK, span, axis=2)
        s_pos = c * Q_CHUNK - WINDOW + jnp.arange(span)
        diff = t[:, None] - s_pos[None, :]
        wmask = (diff >= 0) & (diff < WINDOW) & (s_pos[None, :] >= 0)
        s = jnp.einsum('bgrqd,bgkd->bgrqk', qr_c, kw) * scale
        p = masked_softmax(s, wmask)
        o_win = jnp.einsum('bgrqk,bgkd->bgrqd', p.astype(vw.dtype), vw)
        o = g_c[..., 0:1] * o_cmp + g_c[..., 1:2] * o_slc + g_c[..., 2:3] * o_win
        return o.astype(h.dtype)

    chunked = lambda z: jnp.moveaxis(z.reshape(B, G, R, n_chunks, Q_CHUNK, z.shape[-1]), 3, 0)
    out = lax.map(attend_chunk, (jnp.arange(n_chunks), chunked(q), chunked(q_rot), chunked(gates)))
    out = jnp.transpose(out, (1, 0, 4, 2, 3, 5)).reshape(B, T, H * dh)
    return out @ w_o

def swiglu(x, w_gu, w_down):
    gt, up = jnp.split(x @ w_gu, 2, axis=-1)
    return (jax.nn.silu(gt) * up) @ w_down

def moe_swiglu(x, w_router, b_router, w_gu, w_down):
    B, T, D = x.shape
    xt = x.reshape(-1, D)
    n_tok = xt.shape[0]
    n_assign = n_tok * TOP_K
    logits = (xt @ w_router).astype(jnp.float32) + b_router
    top_logit, top_e = lax.top_k(logits, TOP_K)
    weights = jax.nn.softmax(top_logit, axis=-1)
    flat_e = top_e.reshape(-1)
    flat_tok = jnp.arange(n_assign) // TOP_K
    order = jnp.argsort(flat_e)
    e_sorted = flat_e[order]
    tok_sorted = flat_tok[order]
    w_sorted = weights.reshape(-1)[order]
    counts = jnp.bincount(flat_e, length=N_EXPERTS)
    padded = (counts + MOE_ROWS - 1) // MOE_ROWS * MOE_ROWS
    pad_end = jnp.cumsum(padded)
    pad_start = pad_end - padded
    grp_start = jnp.cumsum(counts) - counts
    dest = pad_start[e_sorted] + jnp.arange(n_assign) - grp_start[e_sorted]
    n_blocks = -(-n_assign // MOE_ROWS) + N_EXPERTS
    n_rows = n_blocks * MOE_ROWS
    row_tok = jnp.zeros((n_rows,), jnp.int32).at[dest].set(tok_sorted.astype(jnp.int32))
    block_e = jnp.minimum(jnp.searchsorted(pad_end, jnp.arange(n_blocks) * MOE_ROWS, side='right'),
                          N_EXPERTS - 1)
    xs = xt[row_tok].reshape(n_blocks, MOE_ROWS, D)

    def expert_block(args):
        xb, e = args
        gt, up = jnp.split(xb @ w_gu[e], 2, axis=-1)
        return (jax.nn.silu(gt) * up) @ w_down[e]

    ys = lax.map(expert_block, (xs, block_e)).reshape(n_rows, D)
    y_assign = ys[dest] * w_sorted[:, None].astype(ys.dtype)
    out = jax.ops.segment_sum(y_assign, tok_sorted, num_segments=n_tok)
    return out.reshape(B, T, D)

def setup_inputs(seed: int = 0) -> dict:
    key = jax.random.key(seed)
    ks = iter(jax.random.split(key, 48))
    nrm = lambda shape, sc: jax.random.normal(next(ks), shape, jnp.float32) * sc
    unif = lambda shape, lo, hi: jax.random.uniform(next(ks), shape, jnp.float32, lo, hi)
    D, NA, NB, ND, NM = D_MODEL, N_A_LAYERS, N_B_LAYERS, N_DENSE_LAYERS, N_MOE_LAYERS
    G, dh = N_KV_GROUPS, HEAD_DIM
    return {
        "x": nrm((BATCH, SEQ, D), 1.0),
        "p": nrm((DEPTH, BATCH, SEQ, PLE_DIM), 1.0),
        "a_mu": unif((NA, 6, D), 0.0, 1.0),
        "a_w_rkv": nrm((NA, 3, D, D), D ** -0.5),
        "a_w0": unif((NA, D), -6.0, -0.5),
        "a_w1": nrm((NA, D, DECAY_LORA), D ** -0.5),
        "a_w2": nrm((NA, DECAY_LORA, D), 0.5 * DECAY_LORA ** -0.5),
        "a_a0": nrm((NA, D), 0.1),
        "a_a1": nrm((NA, D, ICLR_LORA), D ** -0.5),
        "a_a2": nrm((NA, ICLR_LORA, D), 0.5 * ICLR_LORA ** -0.5),
        "a_g1": nrm((NA, D, GATE_LORA), D ** -0.5),
        "a_g2": nrm((NA, GATE_LORA, D), GATE_LORA ** -0.5),
        "a_k_k": 0.85 + nrm((NA, D), 0.05),
        "a_k_a": 1.0 + nrm((NA, D), 0.05),
        "a_r_k": nrm((NA, D), 0.1),
        "a_gn_g": 1.0 + nrm((NA, D), 0.05),
        "a_gn_b": nrm((NA, D), 0.02),
        "a_w_o": nrm((NA, D, D), DEEPNORM_BETA * D ** -0.5),
        "b_w_kv": nrm((D, 6 * G * dh), D ** -0.5),
        "b_cmp_pos": nrm((2, CMP_LEN, dh), 0.5),
        "b_phi_w1": nrm((2, CMP_LEN * dh, CMP_HIDDEN), (CMP_LEN * dh) ** -0.5),
        "b_phi_b1": nrm((2, CMP_HIDDEN), 0.02),
        "b_phi_w2": nrm((2, CMP_HIDDEN, dh), CMP_HIDDEN ** -0.5),
        "b_w_in": nrm((NB, D, N_HEADS * dh + N_BRANCH * N_HEADS), D ** -0.5),
        "b_w_o": nrm((NB, N_HEADS * dh, D), DEEPNORM_BETA * D ** -0.5),
        "f_w_gu": nrm((ND, D, 2 * D_FF), D ** -0.5),
        "f_w_down": nrm((ND, D_FF, D), DEEPNORM_BETA * D_FF ** -0.5),
        "m_w_router": nrm((NM, D, N_EXPERTS), D ** -0.5),
        "m_b_router": nrm((NM, N_EXPERTS), 0.01),
        "m_w_gu": nrm((NM, N_EXPERTS, D, 2 * D_FF_EXPERT), D ** -0.5),
        "m_w_down": nrm((NM, N_EXPERTS, D_FF_EXPERT, D), DEEPNORM_BETA * D_FF_EXPERT ** -0.5),
        "ln_g": 1.0 + nrm((DEPTH, 2, D), 0.05),
        "ln_b": nrm((DEPTH, 2, D), 0.02),
        "ple_w": nrm((DEPTH, PLE_DIM, D), PLE_DIM ** -0.5),
        "ple_gate_w": nrm((DEPTH, D, D), D ** -0.5),
        "ple_gate_b": nrm((DEPTH, D), 0.02),
    }

def reference(x, p, a_mu, a_w_rkv, a_w0, a_w1, a_w2, a_a0, a_a1, a_a2, a_g1, a_g2, a_k_k, a_k_a,
              a_r_k, a_gn_g, a_gn_b, a_w_o, b_w_kv, b_cmp_pos, b_phi_w1, b_phi_b1, b_phi_w2,
              b_w_in, b_w_o, f_w_gu, f_w_down, m_w_router, m_b_router, m_w_gu, m_w_down,
              ln_g, ln_b, ple_w, ple_gate_w, ple_gate_b):
    shared = None
    for i in range(DEPTH):
        if i < N_A_LAYERS:
            j = i
            mix = rwkv7_time_mix(x, a_mu[j], a_w_rkv[j], a_w0[j], a_w1[j], a_w2[j], a_a0[j],
                                 a_a1[j], a_a2[j], a_g1[j], a_g2[j], a_k_k[j], a_k_a[j],
                                 a_r_k[j], a_gn_g[j], a_gn_b[j], a_w_o[j])
        else:
            if shared is None:
                shared = nsa_shared_kv(x, b_w_kv, b_cmp_pos, b_phi_w1, b_phi_b1, b_phi_w2)
            j = i - N_A_LAYERS
            mix = nsa_attention(x, shared, b_w_in[j], b_w_o[j])
        x = layer_norm(DEEPNORM_ALPHA * x + mix, ln_g[i, 0], ln_b[i, 0])
        if i % 2 == 0:
            ffn = swiglu(x, f_w_gu[i // 2], f_w_down[i // 2])
        else:
            ffn = moe_swiglu(x, m_w_router[i // 2], m_b_router[i // 2], m_w_gu[i // 2], m_w_down[i // 2])
        x = layer_norm(DEEPNORM_ALPHA * x + ffn, ln_g[i, 1], ln_b[i, 1])
        x = x + (p[i] @ ple_w[i]) * jax.nn.sigmoid(x @ ple_gate_w[i] + ple_gate_b[i])
    return x


_drawn_inputs = setup_inputs


def setup_inputs(seed=0):
    import zlib

    import numpy as np

    out = dict(_drawn_inputs(seed))
    spreads = {}
    factors = {'a_w1': 8.0,
     'a_w2': 8.0,
     'a_a0': 6.171,
     'a_k_k': 7.529,
     'a_k_a': 4.939,
     'a_gn_g': 4.717,
     'a_gn_b': 8.0,
     'b_phi_b1': 8.0,
     'm_b_router': 7.361,
     'ple_gate_b': 7.269}
    for name, (base, spread) in spreads.items():
        noise = np.random.default_rng([zlib.crc32(name.encode()), seed]).standard_normal(out[name].shape)
        drawn = base * np.exp(spread * noise) if base else spread * noise
        out[name] = __import__('jax').numpy.asarray(drawn.astype(out[name].dtype))
    for name, factor in factors.items():
        out[name] = (out[name] * factor).astype(out[name].dtype)
    return out
```

```python
import math
from contextlib import ExitStack

import numpy as np
import concourse.bass as bass
from concourse import mybir

F32 = mybir.dt.float32
ALU = mybir.AluOpType
ACT = mybir.ActivationFunctionType
AX = mybir.AxisListType
ds = bass.ds

P = 128
T, D = 512, 1024
KT = D // P
MT = T // P
DH = 64
CH = 64
NCH = T // CH
GRP = 4
NG = KT // GRP
LEVELS = 5
D_FF, D_FFE, NE = 2816, 1408, 8
PLE = 256
NKV = 4
NQ = 4
CMP_LEN, CMP_STRIDE = 32, 16
NCMP = (T - CMP_LEN) // CMP_STRIDE + 1
CMPW = 32
HID = 256
DEPTH = 2
ALPHA = (2.0 * DEPTH) ** 0.25
LN_EPS, GN_EPS = 1e-5, 64e-5
EM05 = math.exp(-0.5)
NEG = -1e30
SCALE = DH ** -0.5

SLOT = 11 * 512
TILE = KT * T

CONST = {}
_at = 0
for _n, _w in (("ident", P), ("bones", P), ("strict", P), ("lev", 6 * P), ("incl", CH), ("rmat", P),
               ("causal", P), ("reset", T), ("mhalf", 1)):
    CONST[_n] = (_at, _w)
    _at += _w
NCONST = _at
VEC = ["mu0", "mu1", "mu2", "mu3", "mu4", "mu5", "w0", "a0", "k_k", "k_a", "r_k", "gn_g", "gn_b"]


class Core:

    def __init__(self, nc, ctx, io):
        self.nc, self.ctx, self.io = nc, ctx, io
        self.arena = self.sb("arena", [P, 9 * TILE])
        self.slots = [self.sb(f"slot{i}", [P, SLOT]) for i in range(2)]
        self.const = self.sb("const", [P, NCONST])
        self.vec = self.sb("vec", [P, len(VEC), KT])
        self.small = self.sb("small", [P, 1184])
        self.bank = [ctx.enter_context(nc.psum_tensor(f"bank{i}", [P, 512], F32)) for i in range(8)]
        self.phase_sems = []
        self.slab_ready = [self.kept_sem(f"slab_ready{i}") for i in range(2)]
        self.slabs = 0

    def sb(self, name, shape):
        return self.ctx.enter_context(self.nc.sbuf_tensor(name, shape, F32))

    def sem(self, name):
        h = self.nc.alloc_semaphore(name=name)
        self.phase_sems.append(h)
        return h

    def kept_sem(self, name):
        return self.ctx.enter_context(self.nc.semaphore(name))

    def clear_sems(self):
        self.nc.clear_and_free_semaphores(self.phase_sems)
        self.nc.all_engine_barrier()
        self.phase_sems = []

    def c(self, name):
        a, w = CONST[name]
        return self.const[:, a:a + w]

    def v(self, name, f):
        return self.vec[:, VEC.index(name), f:f + 1] if isinstance(f, int) else self.vec[:, VEC.index(name), ds(f, 1)]

    def region(self, i, a=0, n=TILE):
        return self.arena[:, i * TILE + a:i * TILE + a + n]

    def act(self, i):
        return self.region(i).rearrange("p (k t) -> p k t", k=KT)

    def tok(self, i):
        return self.region(i).rearrange("p (m d) -> p m d", m=MT)

    def slab(self, n, kt, cols):
        return self.slots[n % 2][:, 0:kt * cols].rearrange("p (k c) -> p k c", k=kt)


def load_slab(k, sp, slot, src):
    kt, cols = src.shape[1:]
    dst = k.slots[slot][:, 0:kt * cols].rearrange("p (k c) -> p k c", k=kt)
    sp.dma_start(dst, src).then_inc(k.slab_ready[slot], 16)


def slab_wait(k, pe, n):
    pe.wait_ge(k.slab_ready[n % 2], 16 * (n // 2 + 1))


def phase_load(k):
    nc, io = k.nc, k.io
    loaded = k.sem("loaded")
    k.loaded = loaded
    with nc.Block() as block:
        @block.sync
        def _(sp):
            sp.dma_start(k.const[:, :], io["const"]).then_inc(loaded, 16)
            sp.dma_start(k.vec[:, :, :], io["vec"].rearrange("p (n k) -> p n k", k=KT)).then_inc(loaded, 16)
            sp.dma_start(k.act(0), io["xT"].rearrange("p (k t) -> p k t", k=KT)).then_inc(loaded, 16)
            sp.dma_start(k.region(8, 0, 2048), io["lora_in"]).then_inc(loaded, 16)
            sp.dma_start(k.region(8, 2048, 2048)[0:64, :], io["lora_out"]).then_inc(loaded, 16)
            sp.wait_ge(loaded, 80)


R_XT, R_MIX, R_R, R_K, R_V, R_A, R_S, R_BON = 0, 1, 3, 4, 5, 6, 7, 8
MIX_ORDER = [3, 4, 5, 0, 1, 2]


def phase_project(k):
    nc, io = k.nc, k.io
    mixbase, mixed = k.sem("mixbase"), k.sem("mixed")
    one_minus = k.sem("one_minus_mu")
    tile_full, tile_free = k.sem("proj_full"), k.sem("proj_free")
    base = k.slabs
    k.slabs += 6
    xT = k.act(R_XT)
    mix = [k.act(R_MIX), k.act(R_MIX + 1)]
    lora_in = k.region(8, 0, 2048).rearrange("p (k c) -> p k c", k=KT)
    lora_out = k.region(8, 2048, 2048)[0:64, :].rearrange("p (i c) -> p i c", i=2)
    omu = k.small[:, 0:48].rearrange("p (m k) -> p m k", m=6)
    lhid = k.small[0:64, 48:560]
    sgate = k.small[:, 560:1072]
    k.sgate = sgate
    out = {3: R_R, 4: R_K, 5: R_V}
    first = [0, 9, 18, 19, 27, 35]

    with nc.Block() as block:
        @block.sync
        def _(sp):
            for n in range(6):
                if n >= 2:
                    sp.wait_ge(tile_full, 19 + 4 * (n - 1))
                load_slab(k, sp, n % 2, io["w_rkv"][n])

        @block.scalar
        def _(act):
            def mix_base(m):
                if m == 0:
                    act.wait_ge(one_minus, 1)
                if m >= 2:
                    act.wait_ge(tile_full, first[m - 1])
                for f in range(KT):
                    i = MIX_ORDER[m]
                    act.activation(mix[m % 2][:, f, :], xT[:, f, :], ACT.Copy,
                                   scale=omu[:, i, f:f + 1]).then_inc(mixbase, 1)

            def evacuate(n, dst, func, bias=0.0):
                act.wait_ge(tile_full, n + 1)
                act.activation(dst, k.bank[n % 8][0:dst.shape[0], :], func, bias=bias).then_inc(tile_free, 1)

            mix_base(0)
            mix_base(1)
            evacuate(0, lhid, ACT.Tanh)
            for f in range(KT):
                evacuate(1 + f, k.act(R_S)[:, f, :], ACT.Sigmoid, k.v("w0", f))
            mix_base(2)
            evacuate(9, lhid, ACT.Identity)
            for f in range(KT):
                evacuate(10 + f, k.act(R_A)[:, f, :], ACT.Sigmoid, k.v("a0", f))
            mix_base(3)
            evacuate(18, sgate, ACT.Sigmoid)
            for m in range(3, 6):
                if m < 5:
                    mix_base(m + 1)
                for f in range(KT):
                    evacuate(first[m] + f, k.act(out[m])[:, f, :], ACT.Identity)

        @block.vector
        def _(dve):
            dve.tensor_scalar(omu, k.vec[:, 0:6, :], -1.0, 1.0, ALU.mult, ALU.add).then_inc(one_minus, 1)
            for m in range(6):
                for f in range(KT):
                    i = MIX_ORDER[m]
                    dve.wait_ge(mixbase, m * KT + f + 1)
                    dst = mix[m % 2][:, f, 1:T]
                    dve.scalar_tensor_tensor(out=dst, in0=xT[:, f, 0:T - 1], scalar=k.v(f"mu{i}", f), in1=dst,
                                             op0=ALU.mult, op1=ALU.add).then_inc(mixed, 1)

        @block.tensor
        def _(pe):
            tile = [0]

            def group(lhs, rhs, ready=None):
                n = tile[0]
                tile[0] += 1
                if n >= 8:
                    pe.wait_ge(tile_free, n - 7)
                for i, (a, b) in enumerate(zip(lhs, rhs)):
                    if ready is not None:
                        pe.wait_ge(mixed, ready + i + 1)
                    last = pe.matmul(k.bank[n % 8][0:a.shape[1], :], a, b, start=i == 0, stop=i == len(lhs) - 1)
                return last

            for m in range(2):
                mx = mix[m]
                group([lora_in[:, kk, 64 * m:64 * m + 64] for kk in range(KT)], [mx[:, kk, :] for kk in range(KT)],
                      ready=m * KT).then_inc(tile_full, 1)
                pe.wait_ge(tile_free, first[m] + 1)
                for f in range(KT):
                    last = group([lora_out[:, m, f * P:(f + 1) * P]], [lhid])
                    last.then_inc(tile_full, 1)
            mx = mix[0]
            group([lora_in[:, kk, 128:256] for kk in range(KT)], [mx[:, kk, :] for kk in range(KT)],
                  ready=2 * KT).then_inc(tile_full, 1)
            for m in range(3, 6):
                for h in range(2):
                    n = 2 * (m - 3) + h
                    slab_wait(k, pe, base + n)
                    w = k.slab(n, KT, 512)
                    for o in range(4):
                        last = group([w[:, kk, o * P:(o + 1) * P] for kk in range(KT)],
                                     [mix[m % 2][:, kk, :] for kk in range(KT)],
                                     ready=m * KT if h == 0 and o == 0 else None)
                        last.then_inc(tile_full, 1)


def phase_scale(k):
    nc = k.nc
    dots, dots_full = k.sem("dots"), k.sem("dots_full")
    head_key, dec_sum, dec, dec_inv, dec_prev = (k.sem(n) for n in ("head_key", "dec_sum", "dec", "dec_inv", "dec_prev"))
    chain, ptmp, pool_done, kept = k.sem("scale_chain"), k.sem("scale_ptmp"), k.sem("scale_pool"), k.sem("decay_kept")
    newkey, tile_done = k.sem("newkey"), k.sem("scale_tile")
    Rr, Kk, Vv, Aa, Ss, Bon = (k.act(i) for i in (R_R, R_K, R_V, R_A, R_S, R_BON))
    tmp = [k.slots[j][:, 0:8 * T].rearrange("p (k t) -> p k t", k=8) for j in range(2)]
    norm = k.act(R_MIX)
    squared, summed, clamped, rooted, normed = (k.sem("norm_" + n) for n in ("squared", "summed", "clamped", "rooted", "done"))
    k.chunk_decay = k.small[:, 0:64].rearrange("p (k c) -> p k c", k=KT)
    omka = k.small[:, 1072:1080]

    with nc.Block() as block:
        @block.scalar
        def _(act):
            for f in range(KT):
                act.activation(norm[:, f, :], Kk[:, f, :], ACT.Square, scale=k.v("k_k", f)).then_inc(squared, 1)
            for f in range(KT):
                act.wait_ge(clamped, f + 1)
                act.activation(norm[:, f, :], norm[:, f, :], ACT.Sqrt).then_inc(rooted, 1)
            with act.Fori(0, KT // 2) as half:
                for j in range(2):
                    f, t = 2 * half + j, tmp[j]
                    n = f + 1
                    col = lambda name: k.v(name, f)
                    row = lambda x: x[:, ds(f, 1), :].rearrange("p a t -> p (a t)")
                    act.wait_ge(tile_done, f + 1)
                    act.wait_ge(pool_done, f + 1)
                    act.activation(t[:, 0, :], row(Kk), ACT.Copy, scale=col("k_k")).then_inc(head_key, 1)
                    act.wait_ge(dec_sum, n)
                    act.activation(t[:, 6, :], t[:, 5, :], ACT.Exp, scale=-EM05).then_inc(dec, 1)
                    act.activation(t[:, 7, :], t[:, 5, :], ACT.Exp, scale=EM05).then_inc(dec_inv, 1)
                    act.wait_ge(dec, n)
                    act.activation(k.chunk_decay[:, ds(f, 1), :].rearrange("p a c -> p (a c)"),
                                   t[:, 6, CH - 1:T:CH], ACT.Copy).then_inc(kept, 1)
                    act.wait_ge(ptmp, 3 * f + 1)
                    act.activation(t[:, 2, :], t[:, 2, :], ACT.Exp, scale=-EM05).then_inc(dec_prev, 1)

        @block.tensor
        def _(pe):
            for f in range(KT):
                pe.wait_ge(squared, f + 1)
                pe.matmul(k.bank[f][:, :], k.c("bones"), norm[:, f, :], start=True, stop=True).then_inc(summed, 1)
            pe.wait_ge(clamped, KT)
            with pe.Fori(0, KT // 2) as half:
                for j in range(2):
                    f, t = 2 * half + j, tmp[j]
                    pe.wait_ge(dots, f + 1)
                    pe.wait_ge(tile_done, f + 1)
                    pe.matmul(k.bank[2 * j + 1][:, :], k.c("bones"), t[:, 4, :], start=True,
                              stop=True).then_inc(dots_full, 1)

        @block.vector
        def _(dve):
            dve.tensor_scalar(omka, k.vec[:, VEC.index("k_a"), :], -1.0, 1.0, ALU.mult, ALU.add).then_inc(chain, 1)
            dve.wait_ge(chain, 1)
            for f in range(KT):
                dve.wait_ge(summed, f + 1)
                dve.tensor_scalar(norm[:, f, :], k.bank[f][:, :], 1e-24, None, ALU.max).then_inc(clamped, 1)
            for f in range(KT):
                dve.wait_ge(rooted, f + 1)
                dve.reciprocal(norm[:, f, :], norm[:, f, :]).then_inc(normed, 1)
            dve.wait_ge(normed, KT)
            dve.sem_inc(tile_done, 2)
            with dve.Fori(0, KT // 2) as half:
                for j in range(2):
                    f, t = 2 * half + j, tmp[j]
                    n = f + 1
                    col = lambda name: k.v(name, f)
                    row = lambda x: x[:, ds(f, 1), :].rearrange("p a t -> p (a t)")
                    dve.wait_ge(pool_done, f + 1)
                    dve.tensor_tensor_scan(t[:, 5, :], k.c("reset"), row(Ss), 0.0, ALU.mult,
                                           ALU.add).then_inc(dec_sum, 1)
                    dve.tensor_scalar(t[:, 3, :], row(Aa), col("k_a"), omka[:, ds(f, 1)], ALU.mult,
                                      ALU.add).then_inc(chain, 1)
                    dve.wait_ge(chain, 2 * f + 2)
                    dve.tensor_tensor(t[:, 3, :], t[:, 3, :], row(Kk), ALU.mult).then_inc(newkey, 1)
                    dve.wait_ge(newkey, n)
                    dve.scalar_tensor_tensor(out=t[:, 4, :], in0=row(Rr), scalar=col("r_k"), in1=t[:, 3, :],
                                             op0=ALU.mult, op1=ALU.mult).then_inc(dots, 1)
                    dve.wait_ge(head_key, n)
                    dve.tensor_tensor(t[:, 0, :], t[:, 0, :], row(norm), ALU.mult).then_inc(chain, 1)
                    dve.wait_ge(dots_full, n)
                    dve.tensor_tensor(row(Bon), k.bank[2 * j + 1][:, :], row(Vv), ALU.mult)
                    dve.wait_ge(dec, n)
                    dve.tensor_tensor(row(Rr), row(Rr), t[:, 6, :], ALU.mult)
                    dve.wait_ge(dec_prev, n)
                    dve.wait_ge(kept, n)
                    dve.wait_ge(chain, 2 * f + 3)
                    dve.tensor_tensor(row(Ss), t[:, 0, :], t[:, 2, :], ALU.mult).then_inc(tile_done, 1)

        @block.gpsimd
        def _(pool):
            pool.sem_inc(pool_done, 2)
            with pool.Fori(0, KT // 2) as half:
                for j in range(2):
                    f, t = 2 * half + j, tmp[j]
                    n = f + 1
                    row = lambda x: x[:, ds(f, 1), :].rearrange("p a t -> p (a t)")
                    pool.wait_ge(dec_sum, n)
                    pool.wait_ge(tile_done, f + 1)
                    pool.nop(nofuse=True)
                    pool.tensor_tensor(t[:, 2, :], t[:, 5, :], row(Ss), ALU.subtract).then_inc(ptmp, 1)
                    pool.wait_ge(dec_inv, n)
                    pool.wait_ge(newkey, n)
                    pool.wait_ge(dots, n)
                    pool.nop(nofuse=True)
                    pool.tensor_tensor(row(Kk), t[:, 3, :], t[:, 7, :], ALU.mult).then_inc(ptmp, 1)
                    pool.wait_ge(chain, 2 * f + 3)
                    pool.nop(nofuse=True)
                    pool.tensor_tensor(t[:, 1, :], t[:, 0, :], row(Aa), ALU.mult).then_inc(ptmp, 1)
                    pool.wait_ge(ptmp, 3 * f + 3)
                    pool.nop(nofuse=True)
                    pool.tensor_tensor(row(Aa), t[:, 1, :], t[:, 7, :], ALU.mult).then_inc(pool_done, 1)


def phase_recurrence(k):
    nc = k.nc
    S = {n: k.sem("rec_" + n) for n in (
        "ab", "ak", "rm", "tb", "tk", "tv", "ty", "p", "xp", "py", "w", "u", "o", "ds",
        "built_dve", "built_pool", "nmask", "kmask", "rmask", "btok", "ktok", "vtok", "levels", "first", "y1", "x1",
        "p_sb", "x", "y", "w_sb", "u_sb", "out", "sum", "state", "zero", "zero_state")}
    rho, kap, vv, bet, alp, out = (k.act(i) for i in (R_R, R_K, R_V, R_A, R_S, R_XT))
    W = GRP * P

    def take(pool=[k.region(1), 0, k.region(2), 0, k.slots[0][:, :], 0, k.slots[1][:, :], 0]):
        for i in range(0, len(pool), 2):
            if pool[i + 1] + W <= pool[i].shape[1]:
                a = pool[i + 1]
                pool[i + 1] += W
                return pool[i][:, a:a + W].rearrange("p (q c) -> p q c", q=GRP)
        raise MemoryError("recurrence")

    names = ["bdA", "bdB", "bdK", "bdV", "N", "AK", "RM", "btok", "ktok", "vtok", "X", "Y", "Pm", "ST"]
    B = [{n: take() for n in names + [f"lev{i + 1}" for i in range(LEVELS)]} for g in range(NG)]
    for s in B:
        s["Wm"], s["U"] = s["Pm"], s["X"]
    bk = [[k.bank[4 * g + i][:, :].rearrange("p (q c) -> p q c", q=GRP) for i in range(4)] for g in range(NG)]
    ident = k.c("ident")
    over = lambda m: m.rearrange("p (q c) -> p q c", q=1).to_broadcast([P, GRP, m.shape[1]])
    strict = over(k.c("strict"))
    levm = k.c("lev").rearrange("p (l c) -> p l c", l=6)
    lev = [over(levm[:, l, :]) for l in range(6)]
    incl = k.c("incl").rearrange("p (q c) -> p q c", q=1).to_broadcast([P, 2 * GRP, CH])
    idn = over(ident)
    both = (0, 1)

    with nc.Block() as block:
        @block.sync
        def _(sp):
            for each in S.values():
                sp.sem_inc(each, 1)

        @block.tensor
        def _(pe):
            def four(bank, lhs, rhs, sem, width=P, add=None):
                for q in range(GRP):
                    terms = [(lhs, rhs)] + (add or [])
                    for i, (a, b) in enumerate(terms):
                        last = pe.matmul(bank[:, q, 0:width] if width == P else bank[:, q, :], a(q), b(q),
                                         start=i == 0, stop=i == len(terms) - 1)
                last.then_inc(sem, 1)

            def turn(bank, src, sem):
                for q in range(GRP):
                    last = pe.transpose(bank[:, q, :], src[:, q, :], ident)
                last.then_inc(sem, 1)

            with pe.Fori(0, NCH) as c:
                for g in both:
                    n, s = 2 * c + g + 1, B[g]
                    rc = lambda q, g=g: rho[:, GRP * g + q, ds(c * CH, CH)]
                    pe.wait_ge(S["built_dve"], 8 * c + 4 * g + 4 + 1)
                    pe.wait_ge(S["out"], 2 * c + 1)
                    four(bk[g][0], lambda q: s["bdB"][:, q, :], lambda q: s["bdA"][:, q, :], S["ab"])
                    pe.wait_ge(S["built_pool"], 8 * c + 4 * g + 4 + 1)
                    pe.wait_ge(S["sum"], 2 * c + 1)
                    four(bk[g][1], lambda q: s["bdK"][:, q, :], lambda q: s["bdA"][:, q, :], S["ak"])
                    pe.wait_ge(S["w_sb"], 2 * c + 1)
                    rm = k.bank[4 * g + 2][:, :].rearrange("p (q c) -> p q c", c=CH)
                    for i, b in enumerate(("bdB", "bdK")):
                        for q in range(GRP):
                            last = pe.matmul(rm[:, GRP * i + q, :], s[b][:, q, :], rc(q), start=True, stop=True)
                    last.then_inc(S["rm"], 1)
                for g in both:
                    n, s = 2 * c + g + 1, B[g]
                    pe.wait_ge(S["u_sb"], 2 * c + 1)
                    turn(bk[g][3], s["bdB"], S["tb"])
                    pe.wait_ge(S["nmask"], n + 1)
                    turn(bk[g][0], s["bdK"], S["tk"])
                    pe.wait_ge(S["kmask"], n + 1)
                    turn(bk[g][1], s["bdV"], S["tv"])
                for g in both:
                    n, s = 2 * c + g + 1, B[g]
                    pe.wait_ge(S["y1"], n + 1)
                    pe.wait_ge(S["rmask"], n + 1)
                    turn(bk[g][2], s["Y"], S["ty"])
                for l in range(LEVELS):
                    for g in both:
                        s = B[g]
                        m = 2 * c + g + 1
                        if l == 0:
                            pe.wait_ge(S["x1"], m + 1)
                            pe.wait_ge(S["btok"], m + 1)
                        else:
                            pe.wait_ge(S["x"], 8 * c + 2 * (l - 1) + g + 1 + 1)
                        pe.wait_ge(S["levels"], 10 * c + 5 * g + l + 1 + 1)
                        four(bk[g][3], lambda q: s[f"lev{l + 1}"][:, q, :], lambda q: s["X"][:, q, :], S["p"])
                    for g in both:
                        s = B[g]
                        m = 2 * c + g + 1
                        pe.wait_ge(S["p_sb"], 10 * c + 2 * l + g + 1 + 1)
                        if l == 0:
                            pe.wait_ge(S["ktok"], m + 1)
                            pe.wait_ge(S["vtok"], m + 1)
                        else:
                            pe.wait_ge(S["y"], 10 * c + 2 * (l - 1) + g + 1 + 1)
                        if l < LEVELS - 1:
                            four(bk[g][0], lambda q: s["Y"][:, q, :], lambda q: s["Pm"][:, q, :], S["xp"])
                        four(bk[g][1], lambda q: s["Pm"][:, q, :], lambda q: s["Y"][:, q, :], S["py"])
                for g in both:
                    n, s = 2 * c + g + 1, B[g]
                    pe.wait_ge(S["zero_state"], 2 + 1)
                    pe.wait_ge(S["state"], 2 * c + 1)
                    four(bk[g][2], lambda q: s["bdA"][:, q, :], lambda q: s["ST"][:, q, :], S["w"],
                         add=[(lambda q: s["AK"][:, q, :], lambda q: s["vtok"][:, q, :])])
                for g in both:
                    n, s = 2 * c + g + 1, B[g]
                    pe.wait_ge(S["w_sb"], n + 1)
                    pe.wait_ge(S["y"], 10 * c + 2 * (LEVELS - 1) + g + 1 + 1)
                    four(bk[g][3], lambda q: s["Y"][:, q, :], lambda q: s["Wm"][:, q, :], S["u"])
                for g in both:
                    n, s = 2 * c + g + 1, B[g]
                    rc = lambda q, g=g: rho[:, GRP * g + q, ds(c * CH, CH)]
                    rmv = s["RM"].rearrange("p q c -> p (q c)").rearrange("p (r c) -> p r c", c=CH)
                    ob = k.bank[4 * g][:, 0:GRP * CH].rearrange("p (q c) -> p q c", c=CH)
                    pe.wait_ge(S["u_sb"], n + 1)
                    four(ob, lambda q: s["ST"][:, q, :], rc, S["o"], width=CH,
                         add=[(lambda q: s["U"][:, q, :], lambda q: rmv[:, q, :]),
                              (lambda q: s["vtok"][:, q, :], lambda q: rmv[:, GRP + q, :])])
                    four(bk[g][1], lambda q: s["btok"][:, q, :], lambda q: s["U"][:, q, :], S["ds"],
                         add=[(lambda q: s["ktok"][:, q, :], lambda q: s["vtok"][:, q, :])])

        def spread(eng, dst, src, g, c, sem):
            for h in range(2):
                op = eng.tensor_copy(dst[64 * h:64 * h + 64, :, 64 * h:64 * h + 64],
                                     src[64 * h:64 * h + 64, GRP * g:GRP * g + GRP, ds(c * CH, CH)]).then_inc(sem, 1)

        @block.vector
        def _(dve):
            for g in both:
                for b in ("bdA", "bdB"):
                    op = dve.memset(B[g][b], 0.0)
                op.then_inc(S["zero"], 1)
            for g in both:
                dve.memset(B[g]["ST"], 0.0).then_inc(S["zero_state"], 1)
            dve.wait_ge(S["zero"], 4 + 1)
            dve.wait_ge(S["zero_state"], 2 + 1)
            with dve.Fori(0, NCH) as c:
                for g in both:
                    dve.wait_ge(S["w"], 2 * c + 1)
                    spread(dve, B[g]["bdB"], bet, g, c, S["built_dve"])
                    spread(dve, B[g]["bdA"], alp, g, c, S["built_dve"])
                for g in both:
                    n, s = 2 * c + g + 1, B[g]
                    dve.wait_ge(S["ab"], n + 1)
                    dve.wait_ge(S["levels"], 10 * c + 1)
                    dve.tensor_tensor(s["N"], bk[g][0], strict, ALU.mult).then_inc(S["nmask"], 1)
                    dve.wait_ge(S["nmask"], n + 1)
                    dve.wait_ge(S["u"], 2 * c + 1)
                    dve.tensor_tensor(s["Y"], s["N"], lev[0], ALU.mult).then_inc(S["first"], 1)
                    dve.wait_ge(S["first"], n + 1)
                    dve.tensor_tensor(s["Y"], idn, s["Y"], ALU.subtract).then_inc(S["y1"], 1)
                    dve.wait_ge(S["ak"], n + 1)
                    dve.tensor_tensor(s["AK"], bk[g][1], strict, ALU.mult).then_inc(S["kmask"], 1)
                    dve.wait_ge(S["rm"], n + 1)
                    dve.wait_ge(S["o"], 2 * c + 1)
                    flat = lambda x: x.rearrange("p q c -> p (q c)").rearrange("p (r c) -> p r c", c=CH)
                    dve.tensor_tensor(flat(s["RM"]), flat(bk[g][2]), incl, ALU.mult).then_inc(S["rmask"], 1)
                for l in range(LEVELS):
                    for g in both:
                        s = B[g]
                        if l < LEVELS - 1:
                            dve.wait_ge(S["xp"], 8 * c + 2 * l + g + 1 + 1)
                            if l == 0:
                                dve.wait_ge(S["x1"], 2 * c + g + 1 + 1)
                            else:
                                dve.wait_ge(S["x"], 8 * c + 2 * (l - 1) + g + 1 + 1)
                            dve.tensor_tensor(s["X"], s["X"], bk[g][0], ALU.subtract).then_inc(S["x"], 1)
                        dve.wait_ge(S["py"], 10 * c + 2 * l + g + 1 + 1)
                        if l == 0:
                            dve.wait_ge(S["y1"], 2 * c + g + 1 + 1)
                        else:
                            dve.wait_ge(S["y"], 10 * c + 2 * (l - 1) + g + 1 + 1)
                        dve.tensor_tensor(s["Y"], s["Y"], bk[g][1], ALU.subtract).then_inc(S["y"], 1)
                for g in both:
                    n, s = 2 * c + g + 1, B[g]
                    dve.wait_ge(S["ds"], n + 1)
                    dve.wait_ge(S["state"], 2 * c + 1)
                    dve.tensor_tensor(s["ST"], s["ST"], bk[g][1], ALU.add).then_inc(S["sum"], 1)
                    dve.wait_ge(S["sum"], n + 1)
                    dk = k.chunk_decay[:, GRP * g:GRP * g + GRP, ds(c, 1)].to_broadcast([P, GRP, P])
                    dve.tensor_tensor(s["ST"], s["ST"], dk, ALU.mult).then_inc(S["state"], 1)

        @block.gpsimd
        def _(pool):
            for g in both:
                for b in ("bdK", "bdV"):
                    op = pool.memset(B[g][b], 0.0)
                op.then_inc(S["zero"], 1)
            pool.wait_ge(S["zero"], 4 + 1)
            with pool.Fori(0, NCH) as c:
                for g in both:
                    pool.wait_ge(S["w"], 2 * c + 1)
                    pool.nop(nofuse=True)
                    spread(pool, B[g]["bdV"], vv, g, c, S["built_pool"])
                    spread(pool, B[g]["bdK"], kap, g, c, S["built_pool"])
                    pool.wait_ge(S["built_pool"], 8 * c + 4 * g + 4 + 1)
                for g in both:
                    pool.wait_ge(S["nmask"], 2 * c + g + 1 + 1)
                    for l in range(LEVELS):
                        if l == 0:
                            pool.wait_ge(S["p"], 10 * c + 1)
                        else:
                            pool.wait_ge(S["levels"], 10 * c + 5 * g + l + 1)
                        pool.tensor_tensor(B[g][f"lev{l + 1}"], B[g]["N"], lev[l + 1], ALU.mult).then_inc(S["levels"], 1)

        @block.scalar
        def _(act):
            def take_out(dst, src, sem, scale=1.0):
                act.activation(dst, src, ACT.Copy, scale=scale).then_inc(sem, 1)

            with act.Fori(0, NCH) as c:
                for g in both:
                    n, s = 2 * c + g + 1, B[g]
                    act.wait_ge(S["tb"], n + 1)
                    act.wait_ge(S["ds"], 2 * c + 1)
                    take_out(s["btok"], bk[g][3], S["btok"])
                    act.wait_ge(S["tk"], n + 1)
                    take_out(s["ktok"], bk[g][0], S["ktok"])
                    act.wait_ge(S["tv"], n + 1)
                    take_out(s["vtok"], bk[g][1], S["vtok"])
                for g in both:
                    act.wait_ge(S["ty"], 2 * c + g + 1 + 1)
                    take_out(B[g]["X"], bk[g][2], S["x1"])
                for l in range(LEVELS):
                    for g in both:
                        act.wait_ge(S["p"], 10 * c + 2 * l + g + 1 + 1)
                        take_out(B[g]["Pm"], bk[g][3], S["p_sb"])
                for g in both:
                    act.wait_ge(S["w"], 2 * c + g + 1 + 1)
                    take_out(B[g]["Wm"], bk[g][2], S["w_sb"])
                for g in both:
                    act.wait_ge(S["u"], 2 * c + g + 1 + 1)
                    take_out(B[g]["U"], bk[g][3], S["u_sb"], scale=-1.0)
                for g in both:
                    act.wait_ge(S["o"], 2 * c + g + 1 + 1)
                    ob = k.bank[4 * g][:, 0:GRP * CH].rearrange("p (q c) -> p q c", c=CH)
                    take_out(out[:, GRP * g:GRP * g + GRP, ds(c * CH, CH)], ob, S["out"])


def phase_gate(k):
    nc, io = k.nc, k.io
    s = {n: k.sem("gn_" + n) for n in ("mean", "var", "gate", "centred", "squared", "root", "chain", "done")}
    g2_ready, eps_set = k.sem("g2_ready"), k.sem("eps_set")
    o, y, bon = k.act(R_XT), k.act(3), k.act(R_BON)
    tmp = [k.region(2, j * 2048, 2048).rearrange("p (k t) -> p k t", k=4) for j in range(2)]
    g2 = k.region(5, 0, D)
    eps = k.small[:, 1080:1081]
    k.rows = k.kept_sem("rows_ready")
    with nc.Block() as block:
        @block.sync
        def _(sp):
            sp.dma_start(g2, io["g2"]).then_inc(g2_ready, 16)
            for n in range(2):
                load_slab(k, sp, n, io["w_o_a"][n])
            sp.dma_start(k.tok(1), io["x"].rearrange("(m p) d -> p m d", p=P)).then_inc(k.rows, 16)
            rows = io["rows"].rearrange("(o r) d -> o (r d)", o=1)
            sp.dma_start(k.region(6), rows[:, 0:4 * D].to_broadcast([P, 4 * D])).then_inc(k.rows, 16)
            sp.dma_start(k.region(7), rows[:, 4 * D:8 * D].to_broadcast([P, 4 * D])).then_inc(k.rows, 16)
            sp.dma_start(k.region(5, D, D), rows[:, 8 * D:9 * D].to_broadcast([P, D])).then_inc(k.rows, 16)
            sp.dma_start(k.region(5, 2 * D, 2 * T), io["pT"][0]).then_inc(k.rows, 16)

        @block.tensor
        def _(pe):
            pe.wait_ge(g2_ready, 16)
            for f in range(KT):
                t, j = tmp[f % 2], f % 2
                if f >= 2:
                    pe.wait_ge(s["done"], f - 1)
                pe.matmul(k.bank[3 * j][:, :], k.c("bones"), o[:, f, :], start=True, stop=True).then_inc(s["mean"], 1)
                pe.matmul(k.bank[3 * j + 2][:, :], g2[:, f * P:(f + 1) * P], k.sgate, start=True,
                          stop=True).then_inc(s["gate"], 1)
                pe.wait_ge(s["squared"], f + 1)
                pe.matmul(k.bank[3 * j + 1][:, :], k.c("bones"), t[:, 1, :], start=True,
                          stop=True).then_inc(s["var"], 1)

        @block.scalar
        def _(act):
            act.wait_ge(eps_set, 1)
            for f in range(KT):
                t, j = tmp[f % 2], f % 2
                act.wait_ge(s["centred"], f + 1)
                act.activation(t[:, 1, :], t[:, 0, :], ACT.Square).then_inc(s["squared"], 1)
                act.wait_ge(s["var"], f + 1)
                act.activation(t[:, 2, :], k.bank[3 * j + 1][:, :], ACT.Sqrt, bias=eps,
                               scale=1.0 / DH).then_inc(s["root"], 1)

        @block.vector
        def _(dve):
            dve.memset(eps, GN_EPS).then_inc(eps_set, 1)

            def centre(f):
                t, j = tmp[f % 2], f % 2
                dve.wait_ge(s["mean"], f + 1)
                dve.scalar_tensor_tensor(out=t[:, 0, :], in0=k.bank[3 * j][:, :], scalar=-1.0 / DH, in1=o[:, f, :],
                                         op0=ALU.mult, op1=ALU.add).then_inc(s["centred"], 1)

            centre(0)
            for f in range(KT):
                t, j = tmp[f % 2], f % 2
                if f + 1 < KT:
                    centre(f + 1)
                dve.wait_ge(s["root"], f + 1)
                dve.reciprocal(t[:, 2, :], t[:, 2, :]).then_inc(s["chain"], 1)
                dve.wait_ge(s["chain"], 4 * f + 1)
                dve.tensor_tensor(t[:, 0, :], t[:, 0, :], t[:, 2, :], ALU.mult).then_inc(s["chain"], 1)
                dve.wait_ge(s["chain"], 4 * f + 2)
                dve.tensor_scalar(t[:, 0, :], t[:, 0, :], k.v("gn_g", f), k.v("gn_b", f), ALU.mult,
                                  ALU.add).then_inc(s["chain"], 1)
                dve.wait_ge(s["chain"], 4 * f + 3)
                dve.tensor_tensor(t[:, 0, :], t[:, 0, :], bon[:, f, :], ALU.add).then_inc(s["chain"], 1)
                dve.wait_ge(s["chain"], 4 * f + 4)
                dve.wait_ge(s["gate"], f + 1)
                dve.tensor_tensor(y[:, f, :], t[:, 0, :], k.bank[3 * j + 2][:, :], ALU.mult).then_inc(s["done"], 1)


def phase_out_norm(k, tag, lhs, weights, kts, X, gain, shift, XT=None, acc=None, nxt=()):
    nc = k.nc
    s = {n: k.sem(f"{tag}_{n}") for n in ("full", "added", "stats", "mv", "rstd", "normed", "scaled", "shifted",
                                          "turned", "copied", "eps")}
    base = k.slabs
    parts = len(kts)
    if weights is not None:
        k.slabs += 2 * parts
    stat = k.small[:, 1082:1082 + 12]
    mv = k.small[:, 1094:1094 + 8].rearrange("p (m c) -> p m c", m=MT)
    rstd = k.small[:, 1102:1106]
    srcs = list(nxt)

    with nc.Block() as block:
        @block.sync
        def _(sp):
            if weights is not None:
                for n in range(2, 2 * parts):
                    sp.wait_ge(s["full"], MT * (n - 1))
                    load_slab(k, sp, n % 2, weights[n])
            for n, src in enumerate(srcs):
                if weights is not None:
                    sp.wait_ge(s["full"], MT * (2 * parts - 1 + n))
                load_slab(k, sp, n, src)

        @block.tensor
        def _(pe):
            n = 0
            if weights is not None:
                for h in range(2):
                    k0 = 0
                    for part, kt in enumerate(kts):
                        slab_wait(k, pe, base + n)
                        w = k.slab(n, kt, 512)
                        for m in range(MT):
                            for kk in range(kt):
                                last = pe.matmul(k.bank[4 * h + m][:, :], lhs[:, k0 + kk, m * P:(m + 1) * P],
                                                 w[:, kk, :], start=k0 + kk == 0,
                                                 stop=part == parts - 1 and kk == kt - 1)
                            last.then_inc(s["full"], 1)
                        k0 += kt
                        n += 1
            if XT is not None:
                for m in range(MT):
                    pe.wait_ge(s["shifted"], m + 1)
                    if m >= 2:
                        pe.wait_ge(s["copied"], 2 * (m - 1))
                    for b in range(2):
                        bank = k.bank[2 * (m % 2) + b]
                        for q in range(4):
                            last = pe.transpose(bank[:, q * P:(q + 1) * P], X[:, m, (4 * b + q) * P:(4 * b + q + 1) * P],
                                                k.c("ident"))
                        last.then_inc(s["turned"], 1)

        @block.vector
        def _(dve):
            if gain is None:
                return
            dve.memset(k.small[:, 1106:1107], LN_EPS).then_inc(s["eps"], 1)
            if weights is not None and k.rows is not None:
                dve.wait_ge(k.rows, 16 * 5)
            for h in range(2):
                for m in range(MT):
                    row = X[:, m, h * 512:(h + 1) * 512]
                    if weights is not None:
                        dve.wait_ge(s["full"], MT * (parts * (h + 1) - 1) + m + 1)
                        src = k.bank[4 * h + m][:, :]
                    else:
                        src = acc[:, m, h * 512:(h + 1) * 512]
                    dve.scalar_tensor_tensor(out=row, in0=row, scalar=ALPHA, in1=src, op0=ALU.mult,
                                             op1=ALU.add).then_inc(s["added"], 1)
                    if h == 0:
                        continue
                    dve.wait_ge(s["added"], 5 + m)
                    if m:
                        dve.wait_ge(s["mv"], m)
                    for q in range(2):
                        dve.bn_stats(stat[:, 6 * q:6 * q + 6], X[:, m, q * 512:(q + 1) * 512]).then_inc(s["stats"], 1)
                    dve.wait_ge(s["stats"], 2 * m + 2)
                    dve.bn_aggr(mv[:, m, :], stat).then_inc(s["mv"], 1)
                    dve.wait_ge(s["rstd"], 2 * m + 2)
                    dve.tensor_scalar(X[:, m, :], X[:, m, :], mv[:, m, 0:1], rstd[:, m:m + 1], ALU.subtract,
                                      ALU.mult).then_inc(s["normed"], 1)
                    dve.wait_ge(s["normed"], m + 1)
                    dve.tensor_tensor(X[:, m, :], X[:, m, :], gain, ALU.mult).then_inc(s["scaled"], 1)
                    dve.wait_ge(s["scaled"], m + 1)
                    dve.tensor_tensor(X[:, m, :], X[:, m, :], shift, ALU.add).then_inc(s["shifted"], 1)

        @block.gpsimd
        def _(pool):
            if gain is None:
                return
            for m in range(MT):
                pool.wait_ge(s["mv"], m + 1)
                pool.tensor_scalar(rstd[:, m:m + 1], mv[:, m, 1:2], LN_EPS, None, ALU.add).then_inc(s["rstd"], 1)
                pool.wait_ge(s["rstd"], 2 * m + 1)
                pool.tensor_tensor(rstd[:, m:m + 1], rstd[:, m:m + 1], k.c("mhalf"), ALU.pow).then_inc(s["rstd"], 1)

        @block.scalar
        def _(act):
            if XT is not None:
                for m in range(MT):
                    for b in range(2):
                        act.wait_ge(s["turned"], 2 * m + b + 1)
                        act.activation(XT[:, 4 * b:4 * b + 4, m * P:(m + 1) * P],
                                       k.bank[2 * (m % 2) + b][:, :].rearrange("p (q t) -> p q t", q=4),
                                       ACT.Copy).then_inc(s["copied"], 1)


def phase_ffn_up(k, XT, H, nxt):
    nc, io = k.nc, k.io
    full, sig, part, done = (k.sem("up_" + n) for n in ("full", "sig", "part", "done"))
    base = k.slabs
    n_f = D_FF // P
    k.slabs += n_f
    tmp = k.region(8, 0, 1024).rearrange("p (j t) -> p j t", j=2)
    with nc.Block() as block:
        @block.sync
        def _(sp):
            with sp.Fori(1, n_f // 2) as i:
                for j in range(2):
                    sp.wait_ge(full, 2 * (i - 1) + j + 1)
                    load_slab(k, sp, j, io["w_up"][ds(2 * i + j, 1)].rearrange("a p k c -> (a p) k c"))
            for n, src in enumerate(nxt):
                sp.wait_ge(full, n_f - 1 + n)
                load_slab(k, sp, n, src)

        @block.tensor
        def _(pe):
            pe.sem_inc(done, 2)
            with pe.Fori(0, n_f // 2) as i:
                for j in range(2):
                    pe.wait_ge(k.slab_ready[j], 16 * i + 16 * (base // 2 + 1))
                    w = k.slab(j, KT, 256)
                    pe.wait_ge(done, 2 * i + j + 1)
                    for u in range(2):
                        for kk in range(KT):
                            last = pe.matmul(k.bank[2 * j + u][:, :], w[:, kk, u * P:(u + 1) * P], XT[:, kk, :],
                                             start=kk == 0, stop=kk == KT - 1)
                    last.then_inc(full, 1)

        @block.scalar
        def _(act):
            with act.Fori(0, n_f // 2) as i:
                for j in range(2):
                    act.wait_ge(full, 2 * i + j + 1)
                    act.wait_ge(done, 2 * i + j + 1)
                    act.activation(tmp[:, j, :], k.bank[2 * j][:, :], ACT.Sigmoid).then_inc(sig, 1)

        @block.vector
        def _(dve):
            with dve.Fori(0, n_f // 2) as i:
                for j in range(2):
                    n = 2 * i + j
                    dve.wait_ge(sig, n + 1)
                    dve.tensor_tensor(tmp[:, j, :], tmp[:, j, :], k.bank[2 * j][:, :], ALU.mult).then_inc(part, 1)
                    dve.wait_ge(part, n + 1)
                    dve.tensor_tensor(H[:, ds(n, 1), :].rearrange("p a t -> p (a t)"), tmp[:, j, :],
                                      k.bank[2 * j + 1][:, :], ALU.mult).then_inc(done, 1)


def phase_ple(k, tag, X, XT, pT, bias, tmp, weights, turn, nxt, rows):
    nc, io = k.nc, k.io
    s = {n: k.sem(f"{tag}_{n}") for n in ("ple", "gate", "biased", "sig", "mul", "added", "turned", "copied", "stored")}
    base = k.slabs
    k.slabs += 4
    with nc.Block() as block:
        @block.sync
        def _(sp):
            for n in (2, 3):
                sp.wait_ge(s["ple" if n == 2 else "gate"], MT)
                load_slab(k, sp, n % 2, weights(n))
            for n, src in enumerate(nxt):
                sp.wait_ge(s["ple" if n == 0 else "gate"], 2 * MT)
                load_slab(k, sp, n, src)
            if not turn:
                for m in range(MT):
                    sp.wait_ge(s["added"], MT + m + 1)
                    sp.dma_start(io["out"][0, m * P:(m + 1) * P, :], X[:, m, :]).then_inc(s["stored"], 16)
                sp.wait_ge(s["stored"], 16 * MT)

        @block.tensor
        def _(pe):
            pe.wait_ge(k.rows, rows)
            for h in range(2):
                slab_wait(k, pe, base + 2 * h)
                w = k.slab(0, 2, 512)
                for m in range(MT):
                    if h:
                        pe.wait_ge(s["mul"], m + 1)
                    for kk in range(2):
                        last = pe.matmul(k.bank[4 + m][:, :], pT[:, kk, m * P:(m + 1) * P], w[:, kk, :],
                                         start=kk == 0, stop=kk == 1)
                    last.then_inc(s["ple"], 1)
                slab_wait(k, pe, base + 2 * h + 1)
                w = k.slab(1, KT, 512)
                for m in range(MT):
                    for kk in range(KT):
                        last = pe.matmul(k.bank[m][:, :], XT[:, kk, m * P:(m + 1) * P], w[:, kk, :],
                                         start=kk == 0, stop=kk == KT - 1)
                    last.then_inc(s["gate"], 1)
            if turn:
                for m in range(MT):
                    pe.wait_ge(s["added"], MT + m + 1)
                    if m >= 2:
                        pe.wait_ge(s["copied"], 2 * (m - 1))
                    else:
                        pe.wait_ge(s["mul"], 2 * MT)
                    pe.wait_ge(s["biased"], 2 * MT)
                    for b in range(2):
                        bank = k.bank[4 + 2 * (m % 2) + b]
                        for q in range(4):
                            last = pe.transpose(bank[:, q * P:(q + 1) * P], X[:, m, (4 * b + q) * P:(4 * b + q + 1) * P],
                                                k.c("ident"))
                        last.then_inc(s["turned"], 1)

        @block.scalar
        def _(act):
            for n in range(2 * MT):
                act.wait_ge(s["biased"], n + 1)
                act.activation(tmp[:, n % 4, :], tmp[:, n % 4, :], ACT.Sigmoid).then_inc(s["sig"], 1)
            if turn:
                for m in range(MT):
                    for b in range(2):
                        act.wait_ge(s["turned"], 2 * m + b + 1)
                        act.activation(XT[:, 4 * b:4 * b + 4, m * P:(m + 1) * P],
                                       k.bank[4 + 2 * (m % 2) + b][:, :].rearrange("p (q t) -> p q t", q=4),
                                       ACT.Copy).then_inc(s["copied"], 1)

        @block.vector
        def _(dve):
            dve.wait_ge(k.rows, rows)
            for n in range(2 * MT):
                h, m = n // MT, n % MT
                cols = slice(h * 512, (h + 1) * 512)
                dve.wait_ge(s["gate"], n + 1)
                if h:
                    dve.wait_ge(s["added"], m + 1)
                dve.tensor_tensor(tmp[:, m, :], k.bank[m][:, :], bias[:, cols], ALU.add).then_inc(s["biased"], 1)
                dve.wait_ge(s["sig"], n + 1)
                dve.wait_ge(s["ple"], n + 1)
                dve.tensor_tensor(tmp[:, m, :], tmp[:, m, :], k.bank[4 + m][:, :], ALU.mult).then_inc(s["mul"], 1)
                dve.wait_ge(s["mul"], n + 1)
                dve.tensor_tensor(X[:, m, cols], X[:, m, cols], tmp[:, m, :], ALU.add).then_inc(s["added"], 1)


SM_GATEW, SM_PHI2, SM_PHI2V, SM_B1, SM_POS, SM_ROUTER, SM_BR = 0, 384, 640, 768, 772, 804, 868
SM_GATES, SM_WEIGHTS, SM_MISC = 876, 1108, 1140
R8_VS, R8_VW, R8_ROT, R8_CMPM, R8_RANK, R8_KC, R8_VC = 0, 1024, 2048, 3072, 3328, 3392, 3456


def phase_kv_q(k, XT, nxt):
    nc, io = k.nc, k.io
    s = {n: k.sem("kvq_" + n) for n in ("tables", "full", "free", "rot", "cos", "sin", "done", "twins")}
    base = k.slabs
    k.slabs += 8
    qn, qr = k.act(2), k.act(3)
    four = lambda r, a, n: k.region(r, a, n * T).rearrange("p (k t) -> p k t", t=T)
    z = [four(4, 0, 2), four(4, 2 * T, 2)]
    ks, kw = four(4, 4 * T, 2), four(4, 6 * T, 2)
    vs = k.region(8, R8_VS, 1024).rearrange("p (m c) -> p m c", m=MT)
    vw = k.region(8, R8_VW, 1024).rearrange("p (m c) -> p m c", m=MT)
    rot = k.region(8, R8_ROT, 1024).rearrange("p (i t) -> p i t", i=2)
    z2 = k.region(6).rearrange("p (j a e t) -> p j a e t", j=2, a=2, e=2)
    gw = k.small[:, SM_GATEW:SM_GATEW + 384].rearrange("p (k c) -> p k c", k=KT)
    gates = k.small[:, SM_GATES:SM_GATES + 192]
    tmp = four(5, 0, 2)
    dst = [z[0][:, a, :] for a in range(2)] + [z[1][:, a, :] for a in range(2)] + [ks[:, a, :] for a in range(2)]
    dst += [vs[:, m, :] for m in range(MT)] + [kw[:, a, :] for a in range(2)] + [vw[:, m, :] for m in range(MT)]
    dst += [qn[:, f, :] for f in range(KT)]
    first = [0, 2, 4, 6, 10, 12, 16, 20, 24]
    turns = [(4 + a, ks[:, a, :], ks[:, a, :]) for a in range(2)] + [(10 + a, kw[:, a, :], kw[:, a, :]) for a in range(2)]
    turns += [(16 + f, qn[:, f, :], qr[:, f, :]) for f in range(KT)]

    with nc.Block() as block:
        @block.sync
        def _(sp):
            sp.dma_start(k.region(8, R8_ROT, 1024 + 256 + 64), io["tables"]).then_inc(s["tables"], 16)
            sp.dma_start(k.small[:, 0:SM_BR], io["nsa_small"]).then_inc(s["tables"], 16)
            sp.dma_start(k.small[:, SM_BR:SM_BR + NE], io["router_b"].to_broadcast([P, NE])).then_inc(s["tables"], 16)
            for n in range(2, 8):
                sp.wait_ge(s["full"], first[n - 1])
                load_slab(k, sp, n % 2, io["w_kv"][n] if n < 6 else io["w_q"][n - 6])
            for n, src in enumerate(nxt):
                sp.wait_ge(s["full"], first[7 + n])
                load_slab(k, sp, n, src)
            for j in range(2):
                sp.wait_ge(s["free"], 2 * j + 2)
                for e in range(2):
                    part = z[j][64 * e:64 * e + 64, :, :]
                    sp.dma_start(z2[0:64, j, :, e, :], part).then_inc(s["twins"], 16)
                    sp.dma_start(z2[64:128, j, :, e, 0:T - 1], part[:, :, 1:T]).then_inc(s["twins"], 16)
            sp.wait_ge(s["twins"], 16 * 8)

        @block.tensor
        def _(pe):
            n = [0, 0]

            def room():
                if n[0] >= 4:
                    pe.wait_ge(s["free"], n[0] - 3)
                n[0] += 1
                return k.bank[(n[0] - 1) % 4]

            def rotate(count):
                for _ in range(count):
                    t = n[1]
                    n[1] += 1
                    pe.wait_ge(s["free"], turns[t][0] + 1)
                    if t >= 4:
                        pe.wait_ge(s["sin"], t - 3)
                    pe.matmul(k.bank[4 + t % 4][:, :], k.c("rmat"), turns[t][1], start=True,
                              stop=True).then_inc(s["rot"], 1)

            for i in range(8):
                slab_wait(k, pe, base + i)
                if i in (3, 5):
                    w = k.slab(i, KT, 256)
                    for m in range(MT):
                        bank = room()
                        for kk in range(KT):
                            last = pe.matmul(bank[:, 0:256], XT[:, kk, m * P:(m + 1) * P], w[:, kk, :],
                                             start=kk == 0, stop=kk == KT - 1)
                        last.then_inc(s["full"], 1)
                    rotate(2)
                    continue
                cols = 256 if i < 6 else 512
                w = k.slab(i, KT, cols)
                for o in range(cols // P):
                    bank = room()
                    for kk in range(KT):
                        last = pe.matmul(bank[:, :], w[:, kk, o * P:(o + 1) * P], XT[:, kk, :],
                                         start=kk == 0, stop=kk == KT - 1)
                    last.then_inc(s["full"], 1)
                if i == 7:
                    rotate(4)
            bank = room()
            pe.wait_ge(s["tables"], 48)
            for m in range(MT):
                for kk in range(KT):
                    last = pe.matmul(bank[:, m * 48:(m + 1) * 48], XT[:, kk, m * P:(m + 1) * P], gw[:, kk, :],
                                     start=kk == 0, stop=kk == KT - 1)
            last.then_inc(s["full"], 1)
            rotate(4)

        @block.scalar
        def _(act):
            for t, d in enumerate(dst):
                act.wait_ge(s["full"], t + 1)
                act.activation(d, k.bank[t % 4][:, 0:d.shape[1]], ACT.Copy).then_inc(s["free"], 1)
            act.wait_ge(s["full"], len(dst) + 1)
            act.wait_ge(s["tables"], 48)
            act.activation(gates, k.bank[len(dst) % 4][:, 0:192], ACT.Sigmoid).then_inc(s["free"], 1)

        @block.vector
        def _(dve):
            dve.wait_ge(s["tables"], 48)
            for t, (tile, src, out) in enumerate(turns):
                dve.wait_ge(s["rot"], t + 1)
                if t >= 2:
                    dve.wait_ge(s["done"], t - 1)
                dve.tensor_tensor(tmp[:, t % 2, :], k.bank[4 + t % 4][:, :], rot[:, 1, :], ALU.mult).then_inc(s["sin"], 1)
                dve.wait_ge(s["free"], tile + 1)
                dve.tensor_tensor(out, src, rot[:, 0, :], ALU.mult).then_inc(s["cos"], 1)
                dve.wait_ge(s["sin"], t + 1)
                dve.wait_ge(s["cos"], t + 1)
                dve.tensor_tensor(out, out, tmp[:, t % 2, :], ALU.add).then_inc(s["done"], 1)


def phase_compress(k, nxt):
    nc = k.nc
    s = {n: k.sem("cmp_" + n) for n in ("hidden", "pos", "bias", "u", "sq", "cube", "tanh", "half", "act", "keys",
                                        "values", "zero", "out")}
    base = k.slabs
    k.slabs += 2
    z2 = k.region(6).rearrange("p (j g t) -> p j g t", j=2, g=NKV)
    n_col = NKV * NCMP
    pos = k.small[:, SM_POS:SM_POS + 32].rearrange("p (j i) -> p j i", j=2)
    b1 = k.small[:, SM_B1:SM_B1 + 4]
    bias = k.small[:, SM_MISC:SM_MISC + 4]
    w2k = k.small[:, SM_PHI2:SM_PHI2 + 256].rearrange("p (h c) -> p h c", h=2)
    w2v = k.small[:, SM_PHI2V:SM_PHI2V + 128].rearrange("p (h c) -> p h c", h=2)
    buf = lambda i: k.region(4, i * 512, 4 * n_col).rearrange("p (i c) -> p i c", i=4)
    u, v = buf(0), buf(1)
    g = buf(2)
    kc = k.region(8, R8_KC, 64).rearrange("p (a n) -> p a n", a=2)
    vc = k.region(8, R8_VC, 256)[0:CMPW, :]

    with nc.Block() as block:
        @block.sync
        def _(sp):
            for n, src in enumerate(nxt):
                sp.wait_ge(s["hidden"], 2 * n + 2)
                load_slab(k, sp, n, src)

        @block.tensor
        def _(pe):
            for j in range(2):
                slab_wait(k, pe, base + j)
                w = k.slab(j, 16, HID)
                for h in range(2):
                    for i in range(16):
                        pe.matmul(k.bank[4][:, 2 * j + h:2 * j + h + 1], w[:, i, h * P:(h + 1) * P],
                                  pos[:, j, i:i + 1], start=i == 0, stop=i == 15).then_inc(s["pos"], 1)
                    for i in range(16):
                        span = z2[:, j, :, 2 * i:2 * i + CMP_STRIDE * (NCMP - 1) + 1:CMP_STRIDE]
                        last = pe.matmul(k.bank[2 * j + h][:, 0:n_col].rearrange("p (g n) -> p g n", g=NKV),
                                         w[:, i, h * P:(h + 1) * P], span, start=i == 0, stop=i == 15)
                    last.then_inc(s["hidden"], 1)
            pe.wait_ge(s["act"], 1)
            for h in range(2):
                last = pe.matmul(k.bank[5][:, 0:n_col], w2k[:, h, :], g[:, h, :], start=h == 0, stop=h == 1)
            last.then_inc(s["keys"], 1)
            for q in range(NKV):
                for h in range(2):
                    last = pe.matmul(k.bank[6][0:NCMP, q * DH:(q + 1) * DH], g[:, 2 + h, q * NCMP:(q + 1) * NCMP],
                                     w2v[:, h, :], start=h == 0, stop=h == 1)
            last.then_inc(s["values"], 1)

        @block.vector
        def _(dve):
            dve.memset(kc, 0.0).then_inc(s["zero"], 1)
            dve.memset(vc, 0.0).then_inc(s["zero"], 1)
            dve.wait_ge(s["pos"], 64)
            dve.tensor_tensor(bias, k.bank[4][:, 0:4], b1, ALU.add).then_inc(s["bias"], 1)
            dve.wait_ge(s["bias"], 1)
            for i in range(4):
                dve.wait_ge(s["hidden"], i + 1)
                dve.tensor_scalar(u[:, i, :], k.bank[i][:, 0:n_col], bias[:, i:i + 1], None, ALU.add).then_inc(s["u"], 1)
            dve.wait_ge(s["u"], 4)
            dve.tensor_tensor(v, u, u, ALU.mult).then_inc(s["sq"], 1)
            dve.wait_ge(s["sq"], 1)
            dve.tensor_scalar(v, v, 0.044715, 1.0, ALU.mult, ALU.add).then_inc(s["sq"], 1)
            dve.wait_ge(s["sq"], 2)
            dve.tensor_tensor(v, v, u, ALU.mult).then_inc(s["cube"], 1)
            dve.wait_ge(s["tanh"], 1)
            dve.tensor_scalar(v, v, 0.5, 0.5, ALU.mult, ALU.add).then_inc(s["half"], 1)
            dve.wait_ge(s["half"], 1)
            dve.tensor_tensor(g, v, u, ALU.mult).then_inc(s["act"], 1)
            dve.wait_ge(s["keys"], 1)
            dve.wait_ge(s["zero"], 2)
            keys = k.bank[5][:, 0:n_col].rearrange("p (a e n) -> p a e n", a=2, e=2)
            for e in range(2):
                dve.tensor_copy(kc[64 * e:64 * e + 64, :, 0:NCMP], keys[64 * e:64 * e + 64, :, e, :]).then_inc(s["out"], 1)
            dve.wait_ge(s["values"], 1)
            dve.tensor_copy(vc[0:NCMP, :], k.bank[6][0:NCMP, 0:256]).then_inc(s["out"], 1)

        @block.scalar
        def _(act):
            act.wait_ge(s["cube"], 1)
            act.activation(v, v, ACT.Tanh, scale=math.sqrt(2.0 / math.pi)).then_inc(s["tanh"], 1)


def phase_attend(k):
    assert T // 64 <= 8 and T <= 512
    nc = k.nc
    s = {n: k.sem("att_" + n) for n in (
        "staged", "cs", "chalf", "cmask", "cmax", "csub", "cexp", "czero", "csum", "cguard", "crec", "ccoef", "cnorm",
        "cturn", "cevac", "cout", "cdone", "scores", "masked", "max", "neg", "exp", "turn", "evac", "out",
        "rec", "coef", "scaled", "added")}
    qn, qr = k.act(2), k.act(3)
    four = lambda r, a, n: k.region(r, a, n * T).rearrange("p (k t) -> p k t", t=T)
    keys = [four(4, 4 * T, 2), four(4, 6 * T, 2)]
    vals = [k.region(8, R8_VS, 1024).rearrange("p (m c) -> p m c", m=MT),
            k.region(8, R8_VW, 1024).rearrange("p (m c) -> p m c", m=MT)]
    cm = k.region(8, R8_CMPM, 256).rearrange("p (i m n) -> p i m n", i=2, m=MT)
    kc = k.region(8, R8_KC, 64).rearrange("p (a n) -> p a n", a=2)
    vc = k.region(8, R8_VC, 256)[0:CMPW, :]
    att = k.tok(5)
    gates = k.small[:, SM_GATES:SM_GATES + 192].rearrange("p (m c) -> p m c", m=MT)
    Qn, Qr, K2 = k.region(6, 0, T), k.region(6, T, T), [k.region(6, 2 * T, T), k.region(6, 3 * T, T)]
    Kc = k.region(6, 3328, CMPW)
    Pc = k.region(6, 3392, 256).rearrange("p (e m n) -> p e m n", e=2, m=MT)
    Pc8 = k.region(6, 3392, 256).rearrange("p (i n) -> p i n", i=8)
    Ot = k.region(6, 3648, 256).rearrange("p (m c) -> p m c", m=MT)
    prob = [k.region(6, 2048, 1280), k.slots[1][:, 4096:5376]]
    pcT = k.slots[0][0:CMPW, 4096:5120].rearrange("p (i t) -> p i t", i=8)
    PT = k.region(4, 0, 1280)
    stat = k.region(6, 3904, 64)
    c8 = [stat[:, 8 * i:8 * i + 8] for i in range(3)]
    mx, sm, cf = ([stat[:, 24 + 8 * i + 4 * b:28 + 8 * i + 4 * b] for b in range(2)] for i in range(3))
    width = [P * (m + 1) for m in range(MT)]
    at_s = [(0, 0), (0, P), (1, 0), (2, 0)]
    at_p = [0, P, 3 * P, 6 * P]
    at_t = [(3, 0), (4, 0), (5, 0), (5, 2 * P)]
    at_pt = [0, 512, 896, 1152]
    units = [(e, b) for e in range(2) for b in range(2)]

    def pairs(eng):
        return eng.Fori(0, 2), eng.Fori(0, NQ)

    with nc.Block() as block:
        @block.sync
        def _(sp):
            for each in s.values():
                sp.sem_inc(each, 1)

        @block.gpsimd
        def _(pool):
            with pool.Fori(0, 2) as a:
                with pool.Fori(0, NQ) as r:
                    f = 4 * a + r
                    flat = lambda x, i: x[:, ds(i, 1), :].rearrange("p a t -> p (a t)")
                    pool.wait_ge(s["scores"], 4 * f + 1)
                    pool.wait_ge(s["cs"], f + 1)
                    pool.nop(nofuse=True)
                    for i, (dst, src) in enumerate(((Qn, flat(qn, f)), (Kc, flat(kc, a)), (Qr, flat(qr, f)),
                                                    (K2[0], flat(keys[0], a)), (K2[1], flat(keys[1], a)))):
                        pool.tensor_copy(dst, src).then_inc(s["staged"], 1)

        @block.tensor
        def _(pe):
            with pe.Fori(0, 2) as a:
                with pe.Fori(0, NQ) as r:
                    f = 4 * a + r

                    def scores(u):
                        e, b = units[u]
                        rows = slice(64 * e, 64 * e + 64)
                        pe.wait_ge(s["exp"], 16 * f + 4 * u + 1)
                        for m in range(MT):
                            bank, col = at_s[m]
                            last = pe.matmul(k.bank[bank][:, col:col + width[m]], Qr[rows, m * P:(m + 1) * P],
                                             K2[b][rows, 0:width[m]], start=True, stop=True)
                        last.then_inc(s["scores"], 1)

                    def values(u):
                        e, b = units[u]
                        n = 4 * f + u
                        pe.wait_ge(s["exp"], 16 * f + 4 * u + 4 + 1)
                        pe.wait_ge(s["evac"], 3 * n + 1)
                        for kb in range(MT):
                            bank, col = at_t[kb]
                            for m in range(kb, MT):
                                src = prob[u % 2][:, at_p[m] + kb * P:at_p[m] + (kb + 1) * P]
                                last = pe.transpose(k.bank[bank][:, col + (m - kb) * P:col + (m - kb + 1) * P], src,
                                                    k.c("ident"))
                            if kb != 2:
                                last.then_inc(s["turn"], 1)
                        pe.wait_ge(s["evac"], 3 * n + 3 + 1)
                        pe.wait_ge(s["cdone"], f + 1 + 1)
                        pe.wait_ge(s["scaled"], n + 1)
                        for m in range(MT):
                            for kb in range(m + 1):
                                lhs = PT[:, at_pt[kb] + (m - kb) * P:at_pt[kb] + (m - kb + 1) * P]
                                last = pe.matmul(k.bank[6][:, m * DH:(m + 1) * DH], lhs,
                                                 vals[b][:, kb, ds((2 * a + e) * DH, DH)], start=kb == 0, stop=kb == m)
                        last.then_inc(s["out"], 1)

                    pe.wait_ge(s["staged"], 5 * f + 2 + 1)
                    pe.wait_ge(s["cmask"], f + 1)
                    for e in range(2):
                        for m in range(MT):
                            last = pe.matmul(k.bank[7][:, (4 * e + m) * CMPW:(4 * e + m + 1) * CMPW],
                                             Qn[64 * e:64 * e + 64, m * P:(m + 1) * P], Kc[64 * e:64 * e + 64, :],
                                             start=True, stop=True)
                        if e == 0:
                            last.then_inc(s["chalf"], 1)
                            pe.wait_ge(s["chalf"], f + 1 + 1)
                    last.then_inc(s["cs"], 1)
                    pe.wait_ge(s["staged"], 5 * f + 5 + 1)
                    scores(0)
                    pe.wait_ge(s["cnorm"], f + 1 + 1)
                    pe.wait_ge(s["evac"], 12 * f + 1)
                    for i in range(8):
                        last = pe.transpose(k.bank[3 + i // 4][0:CMPW, (i % 4) * P:(i % 4 + 1) * P], Pc8[:, i, :],
                                            k.c("ident"))
                    last.then_inc(s["cturn"], 1)
                    pe.wait_ge(s["cevac"], 2 * f + 2 + 1)
                    pe.wait_ge(s["scaled"], 4 * f + 1)
                    for e in range(2):
                        for m in range(MT):
                            last = pe.matmul(k.bank[6][:, (4 * e + m) * DH:(4 * e + m + 1) * DH], pcT[:, 4 * e + m, :],
                                             vc[:, ds((2 * a + e) * DH, DH)], start=True, stop=True)
                    last.then_inc(s["cout"], 1)
                    for u in range(1, 4):
                        scores(u)
                        values(u - 1)
                    values(3)

        @block.scalar
        def _(act):
            with act.Fori(0, 2) as a:
                with act.Fori(0, NQ) as r:
                    f = 4 * a + r

                    def exps(u):
                        n = 4 * f + u
                        act.wait_ge(s["neg"], n + 1 + 1)
                        if u < 2:
                            act.wait_ge(s["turn"], 12 * f + 1)
                        else:
                            act.wait_ge(s["turn"], 12 * f + 3 * (u - 1) + 1)
                        for m in range(MT):
                            bank, col = at_s[m]
                            act.activation(prob[u % 2][:, at_p[m]:at_p[m] + width[m]],
                                           k.bank[bank][:, col:col + width[m]], ACT.Exp, bias=mx[u % 2][:, m:m + 1],
                                           scale=SCALE, accum_out=sm[u % 2][:, m:m + 1]).then_inc(s["exp"], 1)

                    def evacs(u):
                        n = 4 * f + u
                        act.wait_ge(s["out"], n + 1)
                        for i, (w, c0) in enumerate(((512, 0), (384, 512), (384, 896))):
                            act.wait_ge(s["turn"], 3 * n + i + 1 + 1)
                            act.activation(PT[:, c0:c0 + w], k.bank[3 + i][:, 0:w], ACT.Copy).then_inc(s["evac"], 1)

                    act.wait_ge(s["csub"], f + 1 + 1)
                    act.activation(Pc8, Pc8, ACT.Exp, scale=SCALE).then_inc(s["cexp"], 1)
                    exps(0)
                    act.wait_ge(s["cturn"], f + 1 + 1)
                    for i in range(2):
                        act.activation(pcT[:, 4 * i:4 * i + 4, :],
                                       k.bank[3 + i][0:CMPW, :].rearrange("p (i t) -> p i t", i=4),
                                       ACT.Copy).then_inc(s["cevac"], 1)
                    for u in range(1, 4):
                        exps(u)
                        evacs(u - 1)
                    evacs(3)

        @block.vector
        def _(dve):
            with dve.Fori(0, 2) as a:
                with dve.Fori(0, NQ) as r:
                    f = 4 * a + r
                    head = lambda e: 8 * a + 4 * e + r
                    spread8 = lambda x: x.rearrange("p (i n) -> p i n", n=1).to_broadcast([P, 8, CMPW])
                    n1 = f + 1

                    dve.wait_ge(s["cs"], n1 + 1)
                    dve.wait_ge(s["cturn"], f + 1)
                    for e in range(2):
                        dve.tensor_tensor(Pc[:, e], k.bank[7][:, e * P:(e + 1) * P].rearrange("p (m n) -> p m n", m=MT),
                                          cm[:, 0], ALU.add).then_inc(s["csum"], 1)
                    dve.wait_ge(s["csum"], 3 * f + 2 + 1)
                    dve.tensor_reduce(c8[0], Pc8, AX.X, ALU.max).then_inc(s["cmask"], 1)
                    dve.wait_ge(s["cmask"], n1 + 1)
                    dve.tensor_tensor(Pc8, Pc8, spread8(c8[0]), ALU.subtract).then_inc(s["csub"], 1)

                    def maxima(u):
                        n = 4 * f + u
                        dve.wait_ge(s["scores"], n + 1 + 1)
                        for m in range(MT):
                            bank, col = at_s[m]
                            diag = k.bank[bank][:, col + m * P:col + (m + 1) * P]
                            dve.tensor_tensor(diag, diag, k.c("causal"), ALU.add).then_inc(s["masked"], 1)
                        for m in range(MT):
                            bank, col = at_s[m]
                            dve.wait_ge(s["masked"], 16 * f + 4 * u + m + 1 + 1)
                            dve.tensor_reduce(mx[u % 2][:, m:m + 1], k.bank[bank][:, col:col + width[m]], AX.X,
                                              ALU.max).then_inc(s["max"], 1)
                        dve.wait_ge(s["max"], 16 * f + 4 * u + 4 + 1)
                        dve.tensor_scalar(mx[u % 2], mx[u % 2], -SCALE, None, ALU.mult).then_inc(s["neg"], 1)

                    def combine(u):
                        e, b = units[u]
                        n = 4 * f + u
                        dve.wait_ge(s["exp"], 16 * f + 4 * u + 4 + 1)
                        dve.reciprocal(cf[u % 2], sm[u % 2]).then_inc(s["rec"], 1)
                        dve.wait_ge(s["rec"], n + 1 + 1)
                        dve.tensor_tensor(cf[u % 2], cf[u % 2], gates[:, :, ds(head(e) * 3 + 1 + b, 1)].rearrange(
                            "p m o -> p (m o)"), ALU.mult).then_inc(s["coef"], 1)
                        dve.wait_ge(s["coef"], n + 1 + 1)
                        dve.wait_ge(s["out"], n + 1 + 1)
                        dve.tensor_tensor(Ot, k.bank[6][:, 0:256].rearrange("p (m c) -> p m c", m=MT),
                                          cf[u % 2].rearrange("p (m c) -> p m c", c=1).to_broadcast([P, MT, DH]),
                                          ALU.mult).then_inc(s["scaled"], 1)
                        dve.wait_ge(s["scaled"], n + 1 + 1)
                        dst = att[:, :, ds(head(e) * DH, DH)]
                        dve.tensor_tensor(dst, dst, Ot, ALU.add).then_inc(s["added"], 1)

                    maxima(0)
                    dve.wait_ge(s["cexp"], n1 + 1)
                    for e in range(2):
                        dve.tensor_tensor(Pc[:, e], Pc[:, e], cm[:, 1], ALU.mult).then_inc(s["czero"], 1)
                    dve.wait_ge(s["czero"], 2 * f + 2 + 1)
                    dve.tensor_reduce(c8[1], Pc8, AX.X, ALU.add).then_inc(s["csum"], 1)
                    dve.wait_ge(s["csum"], 3 * f + 3 + 1)
                    dve.tensor_scalar(c8[1], c8[1], 1e-30, None, ALU.max).then_inc(s["cguard"], 1)
                    dve.wait_ge(s["cguard"], n1 + 1)
                    dve.reciprocal(c8[2], c8[1]).then_inc(s["crec"], 1)
                    dve.wait_ge(s["crec"], n1 + 1)
                    for e in range(2):
                        dve.tensor_tensor(c8[2][:, 4 * e:4 * e + 4], c8[2][:, 4 * e:4 * e + 4],
                                          gates[:, :, ds(head(e) * 3, 1)].rearrange("p m o -> p (m o)"),
                                          ALU.mult).then_inc(s["ccoef"], 1)
                    dve.wait_ge(s["ccoef"], 2 * f + 2 + 1)
                    dve.tensor_tensor(Pc8, Pc8, spread8(c8[2]), ALU.mult).then_inc(s["cnorm"], 1)
                    maxima(1)
                    dve.wait_ge(s["cout"], n1 + 1)
                    for e in range(2):
                        op = dve.tensor_copy(att[:, :, ds(head(e) * DH, DH)],
                                             k.bank[6][:, e * 256:(e + 1) * 256].rearrange("p (m c) -> p m c", m=MT))
                    op.then_inc(s["cdone"], 1)
                    dve.wait_ge(s["cdone"], n1 + 1)
                    combine(0)
                    maxima(2)
                    combine(1)
                    maxima(3)
                    combine(2)
                    combine(3)


def phase_turn(k, src, dst):
    nc = k.nc
    turned, copied = k.sem("turn_turned"), k.sem("turn_copied")
    with nc.Block() as block:
        @block.tensor
        def _(pe):
            for i in range(2 * MT):
                m, b = i // 2, i % 2
                for q in range(4):
                    last = pe.transpose(k.bank[i][:, q * P:(q + 1) * P], src[:, m, (4 * b + q) * P:(4 * b + q + 1) * P],
                                        k.c("ident"))
                last.then_inc(turned, 1)

        @block.scalar
        def _(act):
            for i in range(2 * MT):
                m, b = i // 2, i % 2
                act.wait_ge(turned, i + 1)
                act.activation(dst[:, 4 * b:4 * b + 4, m * P:(m + 1) * P],
                               k.bank[i][:, :].rearrange("p (q t) -> p q t", q=4), ACT.Copy).then_inc(copied, 1)


def phase_route(k, XT):
    nc = k.nc
    s = {n: k.sem("route_" + n) for n in ("full", "chain", "exp")}
    wr = k.small[:, SM_ROUTER:SM_ROUTER + 64].rearrange("p (k e) -> p k e", k=KT)
    br = k.small[:, SM_BR:SM_BR + NE].rearrange("p (m e) -> p m e", m=1).to_broadcast([P, MT, NE])
    wt = k.small[:, SM_WEIGHTS:SM_WEIGHTS + 32].rearrange("p (m e) -> p m e", m=MT)
    lower = k.region(8, R8_RANK, 64).rearrange("p (e g) -> p e g", e=NE)
    at = lambda a, n: k.region(6, a, n)
    L = at(0, 32).rearrange("p (m e) -> p m e", m=MT)
    big = [at(512 * (i + 1), 256).rearrange("p (m e g) -> p m e g", m=MT, e=NE) for i in range(3)]
    rank, sel0, sel1, t = (at(64 + 64 * i, 32).rearrange("p (m e) -> p m e", m=MT) for i in range(4))
    l0, l1, den = (at(384 + 16 * i, 4) for i in range(3))
    wide = lambda x: x.rearrange("p (m e) -> p m e", e=1).to_broadcast([P, MT, NE])

    with nc.Block() as block:
        @block.tensor
        def _(pe):
            for m in range(MT):
                for kk in range(KT):
                    last = pe.matmul(k.bank[0][:, m * NE:(m + 1) * NE], XT[:, kk, m * P:(m + 1) * P], wr[:, kk, :],
                                     start=kk == 0, stop=kk == KT - 1)
            last.then_inc(s["full"], 1)

        @block.scalar
        def _(act):
            act.wait_ge(s["chain"], 11)
            act.activation(l1, l1, ACT.Exp).then_inc(s["exp"], 1)

        @block.vector
        def _(dve):
            n = [0]

            def link(op):
                n[0] += 1
                op.then_inc(s["chain"], 1)
                dve.wait_ge(s["chain"], n[0])

            dve.wait_ge(s["full"], 1)
            link(dve.tensor_tensor(L, k.bank[0][:, 0:32].rearrange("p (m e) -> p m e", m=MT), br, ALU.add))
            for m in range(MT):
                mine = L[:, m].rearrange("p (e g) -> p e g", g=1).to_broadcast([P, NE, NE])
                other = L[:, m].rearrange("p (e g) -> p e g", e=1).to_broadcast([P, NE, NE])
                dve.tensor_tensor(big[0][:, m], other, mine, ALU.is_gt)
                op = dve.tensor_tensor(big[1][:, m], other, mine, ALU.is_equal)
            link(op)
            low = lower.rearrange("p e (m g) -> p m e g", m=1).to_broadcast([P, MT, NE, NE])
            link(dve.tensor_tensor(big[1], big[1], low, ALU.mult))
            link(dve.tensor_tensor(big[2], big[1], big[0], ALU.add))
            link(dve.tensor_reduce(rank, big[2], AX.X, ALU.add))
            dve.tensor_scalar(sel0, rank, 0.0, None, ALU.is_equal)
            link(dve.tensor_scalar(sel1, rank, 1.0, None, ALU.is_equal))
            link(dve.tensor_tensor(t, L, sel0, ALU.mult))
            link(dve.tensor_reduce(l0, t, AX.X, ALU.add))
            link(dve.tensor_tensor(t, L, sel1, ALU.mult))
            link(dve.tensor_reduce(l1, t, AX.X, ALU.add))
            link(dve.tensor_tensor(l1, l1, l0, ALU.subtract))
            dve.wait_ge(s["exp"], 1)
            link(dve.tensor_scalar(den, l1, 1.0, None, ALU.add))
            link(dve.reciprocal(den, den))
            link(dve.tensor_tensor(l1, l1, den, ALU.mult))
            link(dve.tensor_tensor(sel0, sel0, wide(den), ALU.mult))
            link(dve.tensor_tensor(sel1, sel1, wide(l1), ALU.mult))
            link(dve.tensor_tensor(wt, sel0, sel1, ALU.add))


def phase_experts(k, XT, H, acc):
    nc, io = k.nc, k.io
    s = {n: k.sem("moe_" + n) for n in ("up", "sig", "part", "hid", "down", "acc", "zero")}
    base = k.slabs
    n_f = D_FFE // P
    per = n_f + 2
    k.slabs += NE * per
    tmp = k.region(8, 0, 1024).rearrange("p (j t) -> p j t", j=2)
    wt = k.small[:, SM_WEIGHTS:SM_WEIGHTS + 32].rearrange("p (m e) -> p m e", m=MT)

    with nc.Block() as block:
        @block.sync
        def _(sp):
            for each in s.values():
                sp.sem_inc(each, 1)
            with sp.Fori(0, NE // 2) as i:
                for n in range(2 * per):
                    u, x = divmod(n, per)
                    pu, px = divmod(n - 2, per)
                    if n < 2:
                        sp.wait_ge(s["down"], 16 * i + 1)
                    elif px < n_f:
                        sp.wait_ge(s["up"], 22 * i + 11 * pu + px + 1 + 1)
                    else:
                        sp.wait_ge(s["down"], 16 * i + 8 * pu + 4 * (px - n_f + 1) + 1)
                    if x < n_f:
                        src = io["m_up"][ds((2 * i + u) * n_f + x, 1)]
                    else:
                        src = io["m_down"][ds((2 * i + u) * 2 + x - n_f, 1)]
                    load_slab(k, sp, n % 2, src.rearrange("a p k c -> (a p) k c"))

        @block.tensor
        def _(pe):
            with pe.Fori(0, NE // 2) as i:
                for n in range(2 * per):
                    u, x = divmod(n, per)
                    pe.wait_ge(k.slab_ready[n % 2], 16 * per * i + 16 * (base // 2 + n // 2 + 1))
                    if x < n_f:
                        w = k.slab(n, KT, 256)
                        b = x % 2
                        if x >= 2:
                            pe.wait_ge(s["hid"], 22 * i + 11 * u + x - 1 + 1)
                        elif n < 2:
                            pe.wait_ge(s["hid"], 22 * i + 1)
                        else:
                            pe.wait_ge(s["hid"], 22 * i + 11 + 1)
                        for half in range(2):
                            for kk in range(KT):
                                last = pe.matmul(k.bank[2 * b + half][:, :], w[:, kk, half * P:(half + 1) * P],
                                                 XT[:, kk, :], start=kk == 0, stop=kk == KT - 1)
                        last.then_inc(s["up"], 1)
                    else:
                        h = x - n_f
                        w = k.slab(n, n_f, 512)
                        for m in range(MT):
                            if h == 0 and m == 0:
                                pe.wait_ge(s["hid"], 22 * i + 11 * u + 11 + 1)
                            if u == h == 0:
                                pe.wait_ge(s["acc"], 16 * i + 1)
                            else:
                                pe.wait_ge(s["acc"], 16 * i + 8 * u + 4 * h + m - 3 + 1)
                            for kk in range(n_f):
                                last = pe.matmul(k.bank[4 + m][:, :], H[:, kk, m * P:(m + 1) * P], w[:, kk, :],
                                                 start=kk == 0, stop=kk == n_f - 1)
                            last.then_inc(s["down"], 1)

        @block.scalar
        def _(act):
            with act.Fori(0, NE // 2) as i:
                for n in range(2 * n_f):
                    act.wait_ge(s["up"], 22 * i + n + 1 + 1)
                    if n >= 2:
                        act.wait_ge(s["hid"], 22 * i + n - 1 + 1)
                    else:
                        act.wait_ge(s["hid"], 22 * i + 1)
                    b = n % n_f % 2
                    act.activation(tmp[:, b, :], k.bank[2 * b][:, :], ACT.Sigmoid).then_inc(s["sig"], 1)

        @block.vector
        def _(dve):
            dve.memset(acc, 0.0).then_inc(s["zero"], 1)
            dve.wait_ge(s["zero"], 1 + 1)
            with dve.Fori(0, NE // 2) as i:
                for u in range(2):
                    for x in range(n_f):
                        n = n_f * u + x
                        b = x % 2
                        dve.wait_ge(s["sig"], 22 * i + n + 1 + 1)
                        dve.tensor_tensor(tmp[:, b, :], tmp[:, b, :], k.bank[2 * b][:, :], ALU.mult).then_inc(s["part"], 1)
                        dve.wait_ge(s["part"], 22 * i + n + 1 + 1)
                        if x == 0:
                            dve.wait_ge(s["down"], 16 * i + 8 * u + 1)
                        dve.tensor_tensor(H[:, x, :], tmp[:, b, :], k.bank[2 * b + 1][:, :], ALU.mult).then_inc(s["hid"], 1)
                    for h in range(2):
                        for m in range(MT):
                            n = 8 * u + 4 * h + m
                            dve.wait_ge(s["down"], 16 * i + n + 1 + 1)
                            dst = acc[:, m, h * 512:(h + 1) * 512]
                            if n >= 8:
                                dve.wait_ge(s["acc"], 16 * i + n - 7 + 1)
                            else:
                                dve.wait_ge(s["acc"], 16 * i + 1)
                            dve.scalar_tensor_tensor(out=dst, in0=k.bank[4 + m][:, :], scalar=wt[:, m, ds(2 * i + u, 1)],
                                                     in1=dst, op0=ALU.mult, op1=ALU.add).then_inc(s["acc"], 1)


def build(nc, io):
    with ExitStack() as ctx:
        k = Core(nc, ctx, io)
        phase_load(k)
        phase_project(k)
        phase_scale(k)
        phase_recurrence(k)
        phase_gate(k)
        X, XT = k.tok(1), k.act(0)
        row = lambda r, i: k.region(r, i * D, D)
        phase_out_norm(k, "mixa", k.act(3), io["w_o_a"], [KT], X, row(6, 0), row(6, 1), XT,
                       nxt=[io["w_up"][n] for n in range(2)])
        H = k.arena[:, 2 * TILE:2 * TILE + D_FF // P * T].rearrange("p (k t) -> p k t", t=T)
        phase_ffn_up(k, XT, H, nxt=[io["w_down"][n] for n in range(2)])
        ple = lambda l: lambda n: io["ple_w"][l, n // 2] if n % 2 == 0 else io["ple_g"][l, n // 2]
        phase_out_norm(k, "ffn", H, io["w_down"], [11, 11], X, row(6, 2), row(6, 3), XT, nxt=[ple(0)(n) for n in range(2)])
        pT = lambda r, a: k.region(r, a, 2 * T).rearrange("p (k t) -> p k t", k=2)
        phase_ple(k, "ple0", X, XT, pT(5, 2 * D), row(5, 1), k.region(8, 0, 2048).rearrange("p (m t) -> p m t", m=4),
                  ple(0), True, [io["w_kv"][n] for n in range(2)], 16 * 5)
        k.clear_sems()
        phase_kv_q(k, XT, nxt=[io["phi_w1"][n] for n in range(2)])
        phase_compress(k, nxt=[io["w_o_b"][n] for n in range(2)])
        phase_attend(k)
        attT = k.act(2)
        phase_turn(k, k.tok(5), attT)
        phase_out_norm(k, "mixb", attT, io["w_o_b"], [KT], X, row(7, 0), row(7, 1), XT)
        phase_route(k, XT)
        acc = k.tok(4)
        H = k.arena[:, 2 * TILE:2 * TILE + D_FFE // P * T].rearrange("p (k t) -> p k t", t=T)
        phase_experts(k, XT, H, acc)
        phase_rows(k)
        phase_out_norm(k, "moe", None, None, [], X, row(7, 2), row(7, 3), XT, acc=acc,
                       nxt=[ple(1)(n) for n in range(2)])
        phase_ple(k, "ple1", X, XT, pT(5, 2 * D), row(5, 1), k.region(8, 0, 2048).rearrange("p (m t) -> p m t", m=4),
                  ple(1), False, [], 16 * 7)


def phase_rows(k):
    nc, io = k.nc, k.io
    with nc.Block() as block:
        @block.sync
        def _(sp):
            rows = io["rows"].rearrange("(o r) d -> o (r d)", o=1)
            sp.dma_start(k.region(5, D, D), rows[:, 9 * D:10 * D].to_broadcast([P, D])).then_inc(k.rows, 16)
            sp.dma_start(k.region(5, 2 * D, 2 * T), io["pT"][1]).then_inc(k.rows, 16)


def constants():
    c = np.zeros((P, NCONST), np.float32)
    i, j = np.arange(P)[:, None], np.arange(P)[None, :]
    same = i // CH == j // CH
    put = lambda name, a: c.__setitem__((slice(None), slice(CONST[name][0], CONST[name][0] + CONST[name][1])), a)
    put("ident", i == j)
    put("bones", same)
    put("strict", same & (i < j))
    levels = []
    for m in (1, 2, 4, 8, 16, 32):
        levels.append((i // (2 * m) == j // (2 * m)) & (i // m % 2 == 0) & (j // m % 2 == 1))
    put("lev", np.concatenate(levels, 1))
    put("incl", i % CH <= np.arange(CH)[None, :])
    half = DH // 2
    rm = np.zeros((P, P), np.float32)
    for o in range(P):
        b, r = o // DH * DH, o % DH
        rm[b + (r + half) % DH, o] = -1.0 if r < half else 1.0
    put("rmat", rm)
    put("causal", np.where(j <= i, 0.0, NEG))
    put("mhalf", -0.5)
    put("reset", np.broadcast_to((np.arange(T) % CH != 0).astype(np.float32), (P, T)))
    return c


def tables():
    half = DH // 2
    inv = np.float32(10000.0) ** (-np.arange(half, dtype=np.float32) / np.float32(half))
    ang = np.arange(T, dtype=np.float32)[None, :] * inv[np.arange(P) % half][:, None]
    rot = np.stack([np.cos(ang), np.sin(ang)], 1).astype(np.float32)
    t = (np.arange(MT)[None, :, None] * P + np.arange(P)[:, None, None])
    ok = (np.arange(CMPW) * CMP_STRIDE + CMP_LEN - 1 <= t) & (np.arange(CMPW) < NCMP)
    cmp = np.stack([np.where(ok, 0.0, NEG), ok], 1).astype(np.float32)
    rank = np.broadcast_to((np.arange(NE)[None, :] < np.arange(NE)[:, None]).astype(np.float32).reshape(1, -1), (P, 64))
    return np.ascontiguousarray(np.concatenate([rot.reshape(P, -1), cmp.reshape(P, -1), rank], 1))


def slabs(w, kt, cols):
    w = np.asarray(w)
    return np.ascontiguousarray(w.reshape(kt, P, -1, cols).transpose(2, 1, 0, 3))


def layout(i):
    g = {n: np.asarray(a) for n, a in i.items()}
    feat = lambda v: v.reshape(KT, P).T
    o = {"const": constants(), "tables": tables()}
    mu = g["a_mu"][0]
    o["vec"] = np.ascontiguousarray(np.concatenate(
        [feat(mu[m]) for m in range(6)] + [feat(g[n][0]) for n in
         ("a_w0", "a_a0", "a_k_k", "a_k_a", "a_r_k", "a_gn_g", "a_gn_b")], 1))
    x = g["x"][0]
    o["x"] = x
    o["xT"] = np.ascontiguousarray(x.T.reshape(KT, P, T).transpose(1, 0, 2).reshape(P, -1))
    o["lora_in"] = slabs(np.concatenate([g["a_w1"][0], g["a_a1"][0], g["a_g1"][0]], 1), KT, 256).reshape(P, -1)
    o["lora_out"] = np.ascontiguousarray(np.concatenate([g["a_w2"][0], g["a_a2"][0]], 1))
    o["g2"] = g["a_g2"][0]
    o["w_rkv"] = np.concatenate([slabs(g["a_w_rkv"][0, m], KT, 512) for m in range(3)])
    o["w_o_a"] = slabs(g["a_w_o"][0], KT, 512)
    o["rows"] = np.ascontiguousarray(np.concatenate(
        [np.stack([g["ln_g"][l, j], g["ln_b"][l, j]]) for l in range(DEPTH) for j in range(2)] + [g["ple_gate_b"]]))
    o["pT"] = np.ascontiguousarray(g["p"][:, 0].transpose(0, 2, 1).reshape(DEPTH, 2, P, T).transpose(0, 2, 1, 3)
                                   .reshape(DEPTH, P, 2 * T))
    gu = lambda w, f: np.stack([w[:, :f].reshape(D, f // P, P), w[:, f:].reshape(D, f // P, P)], 2).reshape(D, -1)
    o["w_up"] = slabs(gu(g["f_w_gu"][0], D_FF), KT, 256)
    part = lambda w: np.ascontiguousarray(w.reshape(-1, 11, P, 2, 512).transpose(3, 0, 2, 1, 4).reshape(-1, P, 11, 512))
    o["w_down"] = part(g["f_w_down"][0])
    o["ple_w"] = np.stack([slabs(g["ple_w"][l], 2, 512) for l in range(DEPTH)])
    o["ple_g"] = np.stack([slabs(g["ple_gate_w"][l], KT, 512) for l in range(DEPTH)])
    o["w_kv"] = slabs(g["b_w_kv"], KT, 256)
    order = [(2 * a + e) * NQ + r for a in range(2) for r in range(NQ) for e in range(2)]
    wq = g["b_w_in"][0][:, :D].reshape(D, 2 * KT, DH)[:, order].reshape(D, D)
    o["w_q"] = slabs(wq, KT, 512)
    o["phi_w1"] = slabs(np.concatenate([g["b_phi_w1"][0], g["b_phi_w1"][1]], 1), 16, HID)
    tile = lambda w: w.reshape(-1, P, w.shape[-1]).transpose(1, 0, 2).reshape(P, -1)
    w2 = g["b_phi_w2"]
    o["nsa_small"] = np.ascontiguousarray(np.concatenate(
        [tile(g["b_w_in"][0][:, D:]), tile(np.concatenate([w2[0], w2[0]], 1)), tile(w2[1]),
         g["b_phi_b1"].reshape(4, P).T, g["b_cmp_pos"].reshape(32, P).T, tile(g["m_w_router"][0])], 1))
    o["router_b"] = g["m_b_router"]
    o["w_o_b"] = slabs(g["b_w_o"][0], KT, 512)
    o["m_up"] = np.concatenate([slabs(gu(g["m_w_gu"][0, e], D_FFE), KT, 256) for e in range(NE)])
    o["m_down"] = np.concatenate([part(g["m_w_down"][0, e]) for e in range(NE)])
    return o


def kernel(**inputs):
    import concourse.bacc as bacc
    from concourse.bass_utils import run_bass_kernel_spmd

    nc = bacc.Bacc("TRN2", target_bir_lowering=False, num_devices=1)
    arrays = layout(inputs)
    io = {n: nc.dram_tensor("in_" + n, a.shape, F32, kind="ExternalInput").ap() for n, a in arrays.items()}
    io["out"] = nc.dram_tensor("out", (1, T, D), F32, kind="ExternalOutput").ap()
    build(nc, io)
    r = run_bass_kernel_spmd(nc, [{"in_" + n: a for n, a in arrays.items()}], core_ids=[0])
    return np.asarray(r.results[0]["out"])
```

```python
import math
from contextlib import ExitStack

import numpy as np
import concourse.bass as bass
from concourse import mybir

F32 = mybir.dt.float32
F32R = mybir.dt.float32r
I32 = mybir.dt.int32
ALU = mybir.AluOpType
ACT = mybir.ActivationFunctionType
AX = mybir.AxisListType
ds = bass.ds

P = 128
T, D = 512, 1024
KT = D // P
MT = T // P
DH = 64
CH = 64
NCH = T // CH
GRP = 4
NG = KT // GRP
LEVELS = 5
D_FF, D_FFE, NE = 2816, 1408, 8
PLE = 256
NBLK = (2 * T + NE * (P - 1)) // P
UPW = KT * 2 * P
NKV = 4
NQ = 4
CMP_LEN, CMP_STRIDE = 32, 16
NCMP = (T - CMP_LEN) // CMP_STRIDE + 1
CMPW = 32
HID = 256
DEPTH = 2
ALPHA = (2.0 * DEPTH) ** 0.25
LN_EPS, GN_EPS = 1e-5, 64e-5
EM05 = math.exp(-0.5)
NEG = -1e30
SCALE = DH ** -0.5

SLOT = 11 * 512
TILE = KT * T

CONST = {}
_at = 0
for _n, _w in (("ident", P), ("bones", P), ("strict", P), ("lev", 6 * P), ("incl", CH), ("rmat", P),
               ("causal", P), ("reset", T), ("mhalf", 1), ("tri", P), ("ones", P), ("iota", P)):
    CONST[_n] = (_at, _w)
    _at += _w
NCONST = _at
VEC = ["mu0", "mu1", "mu2", "mu3", "mu4", "mu5", "w0", "a0", "k_k", "k_a", "r_k", "gn_g", "gn_b"]


class Core:

    def __init__(self, nc, ctx, io):
        self.nc, self.ctx, self.io = nc, ctx, io
        self.xtok = self.sb("xtok", [P, TILE])
        self.const = self.sb("const", [P, NCONST])
        self.vec = self.sb("vec", [P, len(VEC), KT])
        self.small = self.sb("small", [P, 1184])
        self.bank = [ctx.enter_context(nc.psum_tensor(f"bank{i}", [P, 512], F32)) for i in range(8)]
        self.row_index = ctx.enter_context(nc.sbuf_tensor("row_index", [P, 8], I32))
        self.block_expert = ctx.enter_context(nc.sbuf_tensor("block_expert", [P, 16], I32))
        self.phase_sems = []
        self.slab_ready = [self.kept_sem(f"slab_ready{i}") for i in range(2)]
        self.slabs = 0
        self.scope = None

    def open_arena(self, tag):
        self.scope = ExitStack()
        hold = lambda name, n: self.scope.enter_context(self.nc.sbuf_tensor(name, [P, n], F32))
        self.arena = hold(f"arena_{tag}", 8 * TILE)
        self.slots = [hold(f"slot{i}_{tag}", SLOT) for i in range(2)]

    def close_arena(self):
        self.scope.close()

    def sb(self, name, shape):
        return self.ctx.enter_context(self.nc.sbuf_tensor(name, shape, F32))

    def sem(self, name):
        h = self.nc.alloc_semaphore(name=name)
        self.phase_sems.append(h)
        return h

    def kept_sem(self, name):
        return self.ctx.enter_context(self.nc.semaphore(name))

    def clear_sems(self):
        self.nc.clear_and_free_semaphores(self.phase_sems)
        self.nc.all_engine_barrier()
        self.phase_sems = []

    def c(self, name):
        a, w = CONST[name]
        return self.const[:, a:a + w]

    def v(self, name, f):
        return self.vec[:, VEC.index(name), f:f + 1] if isinstance(f, int) else self.vec[:, VEC.index(name), ds(f, 1)]

    def region(self, i, a=0, n=TILE):
        if i == 1:
            return self.xtok[:, a:a + n]
        i -= i > 1
        return self.arena[:, i * TILE + a:i * TILE + a + n]

    def act(self, i):
        return self.region(i).rearrange("p (k t) -> p k t", k=KT)

    def tok(self, i):
        return self.region(i).rearrange("p (m d) -> p m d", m=MT)

    def slab(self, n, kt, cols):
        return self.slots[n % 2][:, 0:kt * cols].rearrange("p (k c) -> p k c", k=kt)


def load_slab(k, sp, slot, src):
    kt, cols = src.shape[1:]
    dst = k.slots[slot][:, 0:kt * cols].rearrange("p (k c) -> p k c", k=kt)
    sp.dma_start(dst, src).then_inc(k.slab_ready[slot], 16)


def slab_wait(k, pe, n):
    pe.wait_ge(k.slab_ready[n % 2], 16 * (n // 2 + 1))


def phase_load(k):
    nc, io = k.nc, k.io
    loaded = k.sem("loaded")
    k.loaded = loaded
    with nc.Block() as block:
        @block.sync
        def _(sp):
            sp.dma_start(k.const[:, :], io["const"]).then_inc(loaded, 16)
            sp.dma_start(k.vec[:, :, :], io["vec"].rearrange("p (n k) -> p n k", k=KT)).then_inc(loaded, 16)
            sp.dma_start(k.act(0), io["xT"].rearrange("p (k t) -> p k t", k=KT)).then_inc(loaded, 16)
            sp.dma_start(k.region(8, 0, 2048), io["lora_in"]).then_inc(loaded, 16)
            sp.dma_start(k.region(8, 2048, 2048)[0:64, :], io["lora_out"]).then_inc(loaded, 16)
            sp.wait_ge(loaded, 80)


R_XT, R_MIX, R_R, R_K, R_V, R_A, R_S, R_BON = 0, 1, 3, 4, 5, 6, 7, 8
MIX_ORDER = [3, 4, 5, 0, 1, 2]


def phase_project(k):
    nc, io = k.nc, k.io
    mixbase, mixed = k.sem("mixbase"), k.sem("mixed")
    one_minus = k.sem("one_minus_mu")
    tile_full, tile_free = k.sem("proj_full"), k.sem("proj_free")
    base = k.slabs
    k.slabs += 6
    xT = k.act(R_XT)
    mix = [k.act(R_MIX), k.act(R_MIX + 1)]
    lora_in = k.region(8, 0, 2048).rearrange("p (k c) -> p k c", k=KT)
    lora_out = k.region(8, 2048, 2048)[0:64, :].rearrange("p (i c) -> p i c", i=2)
    omu = k.small[:, 0:48].rearrange("p (m k) -> p m k", m=6)
    lhid = k.small[0:64, 48:560]
    sgate = k.small[:, 560:1072]
    k.sgate = sgate
    out = {3: R_R, 4: R_K, 5: R_V}
    first = [0, 9, 18, 19, 27, 35]

    with nc.Block() as block:
        @block.sync
        def _(sp):
            for n in range(6):
                if n >= 2:
                    sp.wait_ge(tile_full, 19 + 4 * (n - 1))
                load_slab(k, sp, n % 2, io["w_rkv"][n])

        @block.scalar
        def _(act):
            def mix_base(m):
                if m == 0:
                    act.wait_ge(one_minus, 1)
                if m >= 2:
                    act.wait_ge(tile_full, first[m - 1])
                for f in range(KT):
                    i = MIX_ORDER[m]
                    act.activation(mix[m % 2][:, f, :], xT[:, f, :], ACT.Copy,
                                   scale=omu[:, i, f:f + 1]).then_inc(mixbase, 1)

            def evacuate(n, dst, func, bias=0.0):
                act.wait_ge(tile_full, n + 1)
                act.activation(dst, k.bank[n % 8][0:dst.shape[0], :], func, bias=bias).then_inc(tile_free, 1)

            mix_base(0)
            mix_base(1)
            evacuate(0, lhid, ACT.Tanh)
            for f in range(KT):
                evacuate(1 + f, k.act(R_S)[:, f, :], ACT.Sigmoid, k.v("w0", f))
            mix_base(2)
            evacuate(9, lhid, ACT.Identity)
            for f in range(KT):
                evacuate(10 + f, k.act(R_A)[:, f, :], ACT.Sigmoid, k.v("a0", f))
            mix_base(3)
            evacuate(18, sgate, ACT.Sigmoid)
            for m in range(3, 6):
                if m < 5:
                    mix_base(m + 1)
                for f in range(KT):
                    evacuate(first[m] + f, k.act(out[m])[:, f, :], ACT.Identity)

        @block.vector
        def _(dve):
            dve.tensor_scalar(omu, k.vec[:, 0:6, :], -1.0, 1.0, ALU.mult, ALU.add).then_inc(one_minus, 1)
            for m in range(6):
                for f in range(KT):
                    i = MIX_ORDER[m]
                    dve.wait_ge(mixbase, m * KT + f + 1)
                    dst = mix[m % 2][:, f, 1:T]
                    dve.scalar_tensor_tensor(out=dst, in0=xT[:, f, 0:T - 1], scalar=k.v(f"mu{i}", f), in1=dst,
                                             op0=ALU.mult, op1=ALU.add).then_inc(mixed, 1)

        @block.tensor
        def _(pe):
            tile = [0]

            def group(lhs, rhs, ready=None):
                n = tile[0]
                tile[0] += 1
                if n >= 8:
                    pe.wait_ge(tile_free, n - 7)
                for i, (a, b) in enumerate(zip(lhs, rhs)):
                    if ready is not None:
                        pe.wait_ge(mixed, ready + i + 1)
                    last = pe.matmul(k.bank[n % 8][0:a.shape[1], :], a, b, start=i == 0, stop=i == len(lhs) - 1)
                return last

            for m in range(2):
                mx = mix[m]
                group([lora_in[:, kk, 64 * m:64 * m + 64] for kk in range(KT)], [mx[:, kk, :] for kk in range(KT)],
                      ready=m * KT).then_inc(tile_full, 1)
                pe.wait_ge(tile_free, first[m] + 1)
                for f in range(KT):
                    last = group([lora_out[:, m, f * P:(f + 1) * P]], [lhid])
                    last.then_inc(tile_full, 1)
            mx = mix[0]
            group([lora_in[:, kk, 128:256] for kk in range(KT)], [mx[:, kk, :] for kk in range(KT)],
                  ready=2 * KT).then_inc(tile_full, 1)
            for m in range(3, 6):
                for h in range(2):
                    n = 2 * (m - 3) + h
                    slab_wait(k, pe, base + n)
                    w = k.slab(n, KT, 512)
                    for o in range(4):
                        last = group([w[:, kk, o * P:(o + 1) * P] for kk in range(KT)],
                                     [mix[m % 2][:, kk, :] for kk in range(KT)],
                                     ready=m * KT if h == 0 and o == 0 else None)
                        last.then_inc(tile_full, 1)


def phase_scale(k):
    nc = k.nc
    dots, dots_full = k.sem("dots"), k.sem("dots_full")
    head_key, dec_sum, dec, dec_inv, dec_prev = (k.sem(n) for n in ("head_key", "dec_sum", "dec", "dec_inv", "dec_prev"))
    chain, ptmp, pool_done, kept = k.sem("scale_chain"), k.sem("scale_ptmp"), k.sem("scale_pool"), k.sem("decay_kept")
    newkey, tile_done = k.sem("newkey"), k.sem("scale_tile")
    Rr, Kk, Vv, Aa, Ss, Bon = (k.act(i) for i in (R_R, R_K, R_V, R_A, R_S, R_BON))
    tmp = [k.slots[j][:, 0:8 * T].rearrange("p (k t) -> p k t", k=8) for j in range(2)]
    norm = k.act(R_MIX)
    squared, summed, clamped, rooted, normed = (k.sem("norm_" + n) for n in ("squared", "summed", "clamped", "rooted", "done"))
    k.chunk_decay = k.small[:, 0:64].rearrange("p (k c) -> p k c", k=KT)
    omka = k.small[:, 1072:1080]

    with nc.Block() as block:
        @block.scalar
        def _(act):
            for f in range(KT):
                act.activation(norm[:, f, :], Kk[:, f, :], ACT.Square, scale=k.v("k_k", f)).then_inc(squared, 1)
            for f in range(KT):
                act.wait_ge(clamped, f + 1)
                act.activation(norm[:, f, :], norm[:, f, :], ACT.Sqrt).then_inc(rooted, 1)
            with act.Fori(0, KT // 2) as half:
                for j in range(2):
                    f, t = 2 * half + j, tmp[j]
                    n = f + 1
                    col = lambda name: k.v(name, f)
                    row = lambda x: x[:, ds(f, 1), :].rearrange("p a t -> p (a t)")
                    act.wait_ge(tile_done, f + 1)
                    act.wait_ge(pool_done, f + 1)
                    act.activation(t[:, 0, :], row(Kk), ACT.Copy, scale=col("k_k")).then_inc(head_key, 1)
                    act.wait_ge(dec_sum, n)
                    act.activation(t[:, 6, :], t[:, 5, :], ACT.Exp, scale=-EM05).then_inc(dec, 1)
                    act.activation(t[:, 7, :], t[:, 5, :], ACT.Exp, scale=EM05).then_inc(dec_inv, 1)
                    act.wait_ge(dec, n)
                    act.activation(k.chunk_decay[:, ds(f, 1), :].rearrange("p a c -> p (a c)"),
                                   t[:, 6, CH - 1:T:CH], ACT.Copy).then_inc(kept, 1)
                    act.wait_ge(ptmp, 3 * f + 1)
                    act.activation(t[:, 2, :], t[:, 2, :], ACT.Exp, scale=-EM05).then_inc(dec_prev, 1)

        @block.tensor
        def _(pe):
            for f in range(KT):
                pe.wait_ge(squared, f + 1)
                pe.matmul(k.bank[f][:, :], k.c("bones"), norm[:, f, :], start=True, stop=True).then_inc(summed, 1)
            pe.wait_ge(clamped, KT)
            with pe.Fori(0, KT // 2) as half:
                for j in range(2):
                    f, t = 2 * half + j, tmp[j]
                    pe.wait_ge(dots, f + 1)
                    pe.wait_ge(tile_done, f + 1)
                    pe.matmul(k.bank[2 * j + 1][:, :], k.c("bones"), t[:, 4, :], start=True,
                              stop=True).then_inc(dots_full, 1)

        @block.vector
        def _(dve):
            dve.tensor_scalar(omka, k.vec[:, VEC.index("k_a"), :], -1.0, 1.0, ALU.mult, ALU.add).then_inc(chain, 1)
            dve.wait_ge(chain, 1)
            for f in range(KT):
                dve.wait_ge(summed, f + 1)
                dve.tensor_scalar(norm[:, f, :], k.bank[f][:, :], 1e-24, None, ALU.max).then_inc(clamped, 1)
            for f in range(KT):
                dve.wait_ge(rooted, f + 1)
                dve.reciprocal(norm[:, f, :], norm[:, f, :]).then_inc(normed, 1)
            dve.wait_ge(normed, KT)
            dve.sem_inc(tile_done, 2)
            with dve.Fori(0, KT // 2) as half:
                for j in range(2):
                    f, t = 2 * half + j, tmp[j]
                    n = f + 1
                    col = lambda name: k.v(name, f)
                    row = lambda x: x[:, ds(f, 1), :].rearrange("p a t -> p (a t)")
                    dve.wait_ge(pool_done, f + 1)
                    dve.tensor_tensor_scan(t[:, 5, :], k.c("reset"), row(Ss), 0.0, ALU.mult,
                                           ALU.add).then_inc(dec_sum, 1)
                    dve.tensor_scalar(t[:, 3, :], row(Aa), col("k_a"), omka[:, ds(f, 1)], ALU.mult,
                                      ALU.add).then_inc(chain, 1)
                    dve.wait_ge(chain, 2 * f + 2)
                    dve.tensor_tensor(t[:, 3, :], t[:, 3, :], row(Kk), ALU.mult).then_inc(newkey, 1)
                    dve.wait_ge(newkey, n)
                    dve.scalar_tensor_tensor(out=t[:, 4, :], in0=row(Rr), scalar=col("r_k"), in1=t[:, 3, :],
                                             op0=ALU.mult, op1=ALU.mult).then_inc(dots, 1)
                    dve.wait_ge(head_key, n)
                    dve.tensor_tensor(t[:, 0, :], t[:, 0, :], row(norm), ALU.mult).then_inc(chain, 1)
                    dve.wait_ge(dots_full, n)
                    dve.tensor_tensor(row(Bon), k.bank[2 * j + 1][:, :], row(Vv), ALU.mult)
                    dve.wait_ge(dec, n)
                    dve.tensor_tensor(row(Rr), row(Rr), t[:, 6, :], ALU.mult)
                    dve.wait_ge(dec_prev, n)
                    dve.wait_ge(kept, n)
                    dve.wait_ge(chain, 2 * f + 3)
                    dve.tensor_tensor(row(Ss), t[:, 0, :], t[:, 2, :], ALU.mult).then_inc(tile_done, 1)

        @block.gpsimd
        def _(pool):
            pool.sem_inc(pool_done, 2)
            with pool.Fori(0, KT // 2) as half:
                for j in range(2):
                    f, t = 2 * half + j, tmp[j]
                    n = f + 1
                    row = lambda x: x[:, ds(f, 1), :].rearrange("p a t -> p (a t)")
                    pool.wait_ge(dec_sum, n)
                    pool.wait_ge(tile_done, f + 1)
                    pool.nop(nofuse=True)
                    pool.tensor_tensor(t[:, 2, :], t[:, 5, :], row(Ss), ALU.subtract).then_inc(ptmp, 1)
                    pool.wait_ge(dec_inv, n)
                    pool.wait_ge(newkey, n)
                    pool.wait_ge(dots, n)
                    pool.nop(nofuse=True)
                    pool.tensor_tensor(row(Kk), t[:, 3, :], t[:, 7, :], ALU.mult).then_inc(ptmp, 1)
                    pool.wait_ge(chain, 2 * f + 3)
                    pool.nop(nofuse=True)
                    pool.tensor_tensor(t[:, 1, :], t[:, 0, :], row(Aa), ALU.mult).then_inc(ptmp, 1)
                    pool.wait_ge(ptmp, 3 * f + 3)
                    pool.nop(nofuse=True)
                    pool.tensor_tensor(row(Aa), t[:, 1, :], t[:, 7, :], ALU.mult).then_inc(pool_done, 1)


def phase_recurrence(k):
    nc = k.nc
    S = {n: k.sem("rec_" + n) for n in (
        "ab", "ak", "rm", "tb", "tk", "tv", "ty", "p", "xp", "py", "w", "u", "o", "ds",
        "built_dve", "built_pool", "nmask", "kmask", "rmask", "btok", "ktok", "vtok", "levels", "first", "y1", "x1",
        "p_sb", "x", "y", "w_sb", "u_sb", "out", "sum", "state", "zero", "zero_state")}
    rho, kap, vv, bet, alp, out = (k.act(i) for i in (R_R, R_K, R_V, R_A, R_S, R_XT))
    W = GRP * P

    def take(pool=[k.region(1), 0, k.region(2), 0, k.slots[0][:, :], 0, k.slots[1][:, :], 0]):
        for i in range(0, len(pool), 2):
            if pool[i + 1] + W <= pool[i].shape[1]:
                a = pool[i + 1]
                pool[i + 1] += W
                return pool[i][:, a:a + W].rearrange("p (q c) -> p q c", q=GRP)
        raise MemoryError("recurrence")

    names = ["bdA", "bdB", "bdK", "bdV", "N", "AK", "RM", "btok", "ktok", "vtok", "X", "Y", "Pm", "ST"]
    B = [{n: take() for n in names + [f"lev{i + 1}" for i in range(LEVELS)]} for g in range(NG)]
    for s in B:
        s["Wm"], s["U"] = s["Pm"], s["X"]
    bk = [[k.bank[4 * g + i][:, :].rearrange("p (q c) -> p q c", q=GRP) for i in range(4)] for g in range(NG)]
    ident = k.c("ident")
    over = lambda m: m.rearrange("p (q c) -> p q c", q=1).to_broadcast([P, GRP, m.shape[1]])
    strict = over(k.c("strict"))
    levm = k.c("lev").rearrange("p (l c) -> p l c", l=6)
    lev = [over(levm[:, l, :]) for l in range(6)]
    incl = k.c("incl").rearrange("p (q c) -> p q c", q=1).to_broadcast([P, 2 * GRP, CH])
    idn = over(ident)
    both = (0, 1)

    with nc.Block() as block:
        @block.sync
        def _(sp):
            for each in S.values():
                sp.sem_inc(each, 1)

        @block.tensor
        def _(pe):
            def four(bank, lhs, rhs, sem, width=P, add=None):
                for q in range(GRP):
                    terms = [(lhs, rhs)] + (add or [])
                    for i, (a, b) in enumerate(terms):
                        last = pe.matmul(bank[:, q, 0:width] if width == P else bank[:, q, :], a(q), b(q),
                                         start=i == 0, stop=i == len(terms) - 1)
                last.then_inc(sem, 1)

            def turn(bank, src, sem):
                for q in range(GRP):
                    last = pe.transpose(bank[:, q, :], src[:, q, :], ident)
                last.then_inc(sem, 1)

            with pe.Fori(0, NCH) as c:
                for g in both:
                    n, s = 2 * c + g + 1, B[g]
                    rc = lambda q, g=g: rho[:, GRP * g + q, ds(c * CH, CH)]
                    pe.wait_ge(S["built_dve"], 8 * c + 4 * g + 4 + 1)
                    pe.wait_ge(S["out"], 2 * c + 1)
                    four(bk[g][0], lambda q: s["bdB"][:, q, :], lambda q: s["bdA"][:, q, :], S["ab"])
                    pe.wait_ge(S["built_pool"], 8 * c + 4 * g + 4 + 1)
                    pe.wait_ge(S["sum"], 2 * c + 1)
                    four(bk[g][1], lambda q: s["bdK"][:, q, :], lambda q: s["bdA"][:, q, :], S["ak"])
                    pe.wait_ge(S["w_sb"], 2 * c + 1)
                    rm = k.bank[4 * g + 2][:, :].rearrange("p (q c) -> p q c", c=CH)
                    for i, b in enumerate(("bdB", "bdK")):
                        for q in range(GRP):
                            last = pe.matmul(rm[:, GRP * i + q, :], s[b][:, q, :], rc(q), start=True, stop=True)
                    last.then_inc(S["rm"], 1)
                for g in both:
                    n, s = 2 * c + g + 1, B[g]
                    pe.wait_ge(S["u_sb"], 2 * c + 1)
                    turn(bk[g][3], s["bdB"], S["tb"])
                    pe.wait_ge(S["nmask"], n + 1)
                    turn(bk[g][0], s["bdK"], S["tk"])
                    pe.wait_ge(S["kmask"], n + 1)
                    turn(bk[g][1], s["bdV"], S["tv"])
                for g in both:
                    n, s = 2 * c + g + 1, B[g]
                    pe.wait_ge(S["y1"], n + 1)
                    pe.wait_ge(S["rmask"], n + 1)
                    turn(bk[g][2], s["Y"], S["ty"])
                for l in range(LEVELS):
                    for g in both:
                        s = B[g]
                        m = 2 * c + g + 1
                        if l == 0:
                            pe.wait_ge(S["x1"], m + 1)
                            pe.wait_ge(S["btok"], m + 1)
                        else:
                            pe.wait_ge(S["x"], 8 * c + 2 * (l - 1) + g + 1 + 1)
                        pe.wait_ge(S["levels"], 10 * c + 5 * g + l + 1 + 1)
                        four(bk[g][3], lambda q: s[f"lev{l + 1}"][:, q, :], lambda q: s["X"][:, q, :], S["p"])
                    for g in both:
                        s = B[g]
                        m = 2 * c + g + 1
                        pe.wait_ge(S["p_sb"], 10 * c + 2 * l + g + 1 + 1)
                        if l == 0:
                            pe.wait_ge(S["ktok"], m + 1)
                            pe.wait_ge(S["vtok"], m + 1)
                        else:
                            pe.wait_ge(S["y"], 10 * c + 2 * (l - 1) + g + 1 + 1)
                        if l < LEVELS - 1:
                            four(bk[g][0], lambda q: s["Y"][:, q, :], lambda q: s["Pm"][:, q, :], S["xp"])
                        four(bk[g][1], lambda q: s["Pm"][:, q, :], lambda q: s["Y"][:, q, :], S["py"])
                for g in both:
                    n, s = 2 * c + g + 1, B[g]
                    pe.wait_ge(S["zero_state"], 2 + 1)
                    pe.wait_ge(S["state"], 2 * c + 1)
                    four(bk[g][2], lambda q: s["bdA"][:, q, :], lambda q: s["ST"][:, q, :], S["w"],
                         add=[(lambda q: s["AK"][:, q, :], lambda q: s["vtok"][:, q, :])])
                for g in both:
                    n, s = 2 * c + g + 1, B[g]
                    pe.wait_ge(S["w_sb"], n + 1)
                    pe.wait_ge(S["y"], 10 * c + 2 * (LEVELS - 1) + g + 1 + 1)
                    four(bk[g][3], lambda q: s["Y"][:, q, :], lambda q: s["Wm"][:, q, :], S["u"])
                for g in both:
                    n, s = 2 * c + g + 1, B[g]
                    rc = lambda q, g=g: rho[:, GRP * g + q, ds(c * CH, CH)]
                    rmv = s["RM"].rearrange("p q c -> p (q c)").rearrange("p (r c) -> p r c", c=CH)
                    ob = k.bank[4 * g][:, 0:GRP * CH].rearrange("p (q c) -> p q c", c=CH)
                    pe.wait_ge(S["u_sb"], n + 1)
                    four(ob, lambda q: s["ST"][:, q, :], rc, S["o"], width=CH,
                         add=[(lambda q: s["U"][:, q, :], lambda q: rmv[:, q, :]),
                              (lambda q: s["vtok"][:, q, :], lambda q: rmv[:, GRP + q, :])])
                    four(bk[g][1], lambda q: s["btok"][:, q, :], lambda q: s["U"][:, q, :], S["ds"],
                         add=[(lambda q: s["ktok"][:, q, :], lambda q: s["vtok"][:, q, :])])

        def spread(eng, dst, src, g, c, sem):
            for h in range(2):
                op = eng.tensor_copy(dst[64 * h:64 * h + 64, :, 64 * h:64 * h + 64],
                                     src[64 * h:64 * h + 64, GRP * g:GRP * g + GRP, ds(c * CH, CH)]).then_inc(sem, 1)

        @block.vector
        def _(dve):
            for g in both:
                for b in ("bdA", "bdB"):
                    op = dve.memset(B[g][b], 0.0)
                op.then_inc(S["zero"], 1)
            for g in both:
                dve.memset(B[g]["ST"], 0.0).then_inc(S["zero_state"], 1)
            dve.wait_ge(S["zero"], 4 + 1)
            dve.wait_ge(S["zero_state"], 2 + 1)
            with dve.Fori(0, NCH) as c:
                for g in both:
                    dve.wait_ge(S["w"], 2 * c + 1)
                    spread(dve, B[g]["bdB"], bet, g, c, S["built_dve"])
                    spread(dve, B[g]["bdA"], alp, g, c, S["built_dve"])
                for g in both:
                    n, s = 2 * c + g + 1, B[g]
                    dve.wait_ge(S["ab"], n + 1)
                    dve.wait_ge(S["levels"], 10 * c + 1)
                    dve.tensor_tensor(s["N"], bk[g][0], strict, ALU.mult).then_inc(S["nmask"], 1)
                    dve.wait_ge(S["nmask"], n + 1)
                    dve.wait_ge(S["u"], 2 * c + 1)
                    dve.tensor_tensor(s["Y"], s["N"], lev[0], ALU.mult).then_inc(S["first"], 1)
                    dve.wait_ge(S["first"], n + 1)
                    dve.tensor_tensor(s["Y"], idn, s["Y"], ALU.subtract).then_inc(S["y1"], 1)
                    dve.wait_ge(S["ak"], n + 1)
                    dve.tensor_tensor(s["AK"], bk[g][1], strict, ALU.mult).then_inc(S["kmask"], 1)
                    dve.wait_ge(S["rm"], n + 1)
                    dve.wait_ge(S["o"], 2 * c + 1)
                    flat = lambda x: x.rearrange("p q c -> p (q c)").rearrange("p (r c) -> p r c", c=CH)
                    dve.tensor_tensor(flat(s["RM"]), flat(bk[g][2]), incl, ALU.mult).then_inc(S["rmask"], 1)
                for l in range(LEVELS):
                    for g in both:
                        s = B[g]
                        if l < LEVELS - 1:
                            dve.wait_ge(S["xp"], 8 * c + 2 * l + g + 1 + 1)
                            if l == 0:
                                dve.wait_ge(S["x1"], 2 * c + g + 1 + 1)
                            else:
                                dve.wait_ge(S["x"], 8 * c + 2 * (l - 1) + g + 1 + 1)
                            dve.tensor_tensor(s["X"], s["X"], bk[g][0], ALU.subtract).then_inc(S["x"], 1)
                        dve.wait_ge(S["py"], 10 * c + 2 * l + g + 1 + 1)
                        if l == 0:
                            dve.wait_ge(S["y1"], 2 * c + g + 1 + 1)
                        else:
                            dve.wait_ge(S["y"], 10 * c + 2 * (l - 1) + g + 1 + 1)
                        dve.tensor_tensor(s["Y"], s["Y"], bk[g][1], ALU.subtract).then_inc(S["y"], 1)
                for g in both:
                    n, s = 2 * c + g + 1, B[g]
                    dve.wait_ge(S["ds"], n + 1)
                    dve.wait_ge(S["state"], 2 * c + 1)
                    dve.tensor_tensor(s["ST"], s["ST"], bk[g][1], ALU.add).then_inc(S["sum"], 1)
                    dve.wait_ge(S["sum"], n + 1)
                    dk = k.chunk_decay[:, GRP * g:GRP * g + GRP, ds(c, 1)].to_broadcast([P, GRP, P])
                    dve.tensor_tensor(s["ST"], s["ST"], dk, ALU.mult).then_inc(S["state"], 1)

        @block.gpsimd
        def _(pool):
            for g in both:
                for b in ("bdK", "bdV"):
                    op = pool.memset(B[g][b], 0.0)
                op.then_inc(S["zero"], 1)
            pool.wait_ge(S["zero"], 4 + 1)
            with pool.Fori(0, NCH) as c:
                for g in both:
                    pool.wait_ge(S["w"], 2 * c + 1)
                    pool.nop(nofuse=True)
                    spread(pool, B[g]["bdV"], vv, g, c, S["built_pool"])
                    spread(pool, B[g]["bdK"], kap, g, c, S["built_pool"])
                    pool.wait_ge(S["built_pool"], 8 * c + 4 * g + 4 + 1)
                for g in both:
                    pool.wait_ge(S["nmask"], 2 * c + g + 1 + 1)
                    for l in range(LEVELS):
                        if l == 0:
                            pool.wait_ge(S["p"], 10 * c + 1)
                        else:
                            pool.wait_ge(S["levels"], 10 * c + 5 * g + l + 1)
                        pool.tensor_tensor(B[g][f"lev{l + 1}"], B[g]["N"], lev[l + 1], ALU.mult).then_inc(S["levels"], 1)

        @block.scalar
        def _(act):
            def take_out(dst, src, sem, scale=1.0):
                act.activation(dst, src, ACT.Copy, scale=scale).then_inc(sem, 1)

            with act.Fori(0, NCH) as c:
                for g in both:
                    n, s = 2 * c + g + 1, B[g]
                    act.wait_ge(S["tb"], n + 1)
                    act.wait_ge(S["ds"], 2 * c + 1)
                    take_out(s["btok"], bk[g][3], S["btok"])
                    act.wait_ge(S["tk"], n + 1)
                    take_out(s["ktok"], bk[g][0], S["ktok"])
                    act.wait_ge(S["tv"], n + 1)
                    take_out(s["vtok"], bk[g][1], S["vtok"])
                for g in both:
                    act.wait_ge(S["ty"], 2 * c + g + 1 + 1)
                    take_out(B[g]["X"], bk[g][2], S["x1"])
                for l in range(LEVELS):
                    for g in both:
                        act.wait_ge(S["p"], 10 * c + 2 * l + g + 1 + 1)
                        take_out(B[g]["Pm"], bk[g][3], S["p_sb"])
                for g in both:
                    act.wait_ge(S["w"], 2 * c + g + 1 + 1)
                    take_out(B[g]["Wm"], bk[g][2], S["w_sb"])
                for g in both:
                    act.wait_ge(S["u"], 2 * c + g + 1 + 1)
                    take_out(B[g]["U"], bk[g][3], S["u_sb"], scale=-1.0)
                for g in both:
                    act.wait_ge(S["o"], 2 * c + g + 1 + 1)
                    ob = k.bank[4 * g][:, 0:GRP * CH].rearrange("p (q c) -> p q c", c=CH)
                    take_out(out[:, GRP * g:GRP * g + GRP, ds(c * CH, CH)], ob, S["out"])


def phase_gate(k):
    nc, io = k.nc, k.io
    s = {n: k.sem("gn_" + n) for n in ("mean", "var", "gate", "centred", "squared", "root", "chain", "done")}
    g2_ready, eps_set = k.sem("g2_ready"), k.sem("eps_set")
    o, y, bon = k.act(R_XT), k.act(3), k.act(R_BON)
    tmp = [k.region(2, j * 2048, 2048).rearrange("p (k t) -> p k t", k=4) for j in range(2)]
    g2 = k.region(5, 0, D)
    eps = k.small[:, 1080:1081]
    k.rows = k.kept_sem("rows_ready")
    with nc.Block() as block:
        @block.sync
        def _(sp):
            sp.dma_start(g2, io["g2"]).then_inc(g2_ready, 16)
            for n in range(2):
                load_slab(k, sp, n, io["w_o_a"][n])
            sp.dma_start(k.tok(1), io["x"].rearrange("(m p) d -> p m d", p=P)).then_inc(k.rows, 16)
            rows = io["rows"].rearrange("(o r) d -> o (r d)", o=1)
            sp.dma_start(k.region(6, 0, 2 * D), rows[:, 0:2 * D].to_broadcast([P, 2 * D])).then_inc(k.rows, 16)

        @block.tensor
        def _(pe):
            pe.wait_ge(g2_ready, 16)
            for f in range(KT):
                t, j = tmp[f % 2], f % 2
                if f >= 2:
                    pe.wait_ge(s["done"], f - 1)
                pe.matmul(k.bank[3 * j][:, :], k.c("bones"), o[:, f, :], start=True, stop=True).then_inc(s["mean"], 1)
                pe.matmul(k.bank[3 * j + 2][:, :], g2[:, f * P:(f + 1) * P], k.sgate, start=True,
                          stop=True).then_inc(s["gate"], 1)
                pe.wait_ge(s["squared"], f + 1)
                pe.matmul(k.bank[3 * j + 1][:, :], k.c("bones"), t[:, 1, :], start=True,
                          stop=True).then_inc(s["var"], 1)

        @block.scalar
        def _(act):
            act.wait_ge(eps_set, 1)
            for f in range(KT):
                t, j = tmp[f % 2], f % 2
                act.wait_ge(s["centred"], f + 1)
                act.activation(t[:, 1, :], t[:, 0, :], ACT.Square).then_inc(s["squared"], 1)
                act.wait_ge(s["var"], f + 1)
                act.activation(t[:, 2, :], k.bank[3 * j + 1][:, :], ACT.Sqrt, bias=eps,
                               scale=1.0 / DH).then_inc(s["root"], 1)

        @block.vector
        def _(dve):
            dve.memset(eps, GN_EPS).then_inc(eps_set, 1)

            def centre(f):
                t, j = tmp[f % 2], f % 2
                dve.wait_ge(s["mean"], f + 1)
                dve.scalar_tensor_tensor(out=t[:, 0, :], in0=k.bank[3 * j][:, :], scalar=-1.0 / DH, in1=o[:, f, :],
                                         op0=ALU.mult, op1=ALU.add).then_inc(s["centred"], 1)

            centre(0)
            for f in range(KT):
                t, j = tmp[f % 2], f % 2
                if f + 1 < KT:
                    centre(f + 1)
                dve.wait_ge(s["root"], f + 1)
                dve.reciprocal(t[:, 2, :], t[:, 2, :]).then_inc(s["chain"], 1)
                dve.wait_ge(s["chain"], 4 * f + 1)
                dve.tensor_tensor(t[:, 0, :], t[:, 0, :], t[:, 2, :], ALU.mult).then_inc(s["chain"], 1)
                dve.wait_ge(s["chain"], 4 * f + 2)
                dve.tensor_scalar(t[:, 0, :], t[:, 0, :], k.v("gn_g", f), k.v("gn_b", f), ALU.mult,
                                  ALU.add).then_inc(s["chain"], 1)
                dve.wait_ge(s["chain"], 4 * f + 3)
                dve.tensor_tensor(t[:, 0, :], t[:, 0, :], bon[:, f, :], ALU.add).then_inc(s["chain"], 1)
                dve.wait_ge(s["chain"], 4 * f + 4)
                dve.wait_ge(s["gate"], f + 1)
                dve.tensor_tensor(y[:, f, :], t[:, 0, :], k.bank[3 * j + 2][:, :], ALU.mult).then_inc(s["done"], 1)


def phase_out_norm(k, tag, lhs, weights, kts, X, gain, shift, XT=None, acc=None, nxt=(), rows=0, load=None):
    nc = k.nc
    s = {n: k.sem(f"{tag}_{n}") for n in ("full", "added", "stats", "mv", "rstd", "normed", "scaled", "shifted",
                                          "turned", "copied", "eps")}
    base = k.slabs
    parts = len(kts)
    if weights is not None:
        k.slabs += 2 * parts
    stat = k.small[:, 1082:1082 + 12]
    mv = k.small[:, 1094:1094 + 8].rearrange("p (m c) -> p m c", m=MT)
    rstd = k.small[:, 1102:1106]
    srcs = list(nxt)

    with nc.Block() as block:
        @block.sync
        def _(sp):
            if weights is not None:
                for n in range(2, 2 * parts):
                    sp.wait_ge(s["full"], MT * (n - 1))
                    load_slab(k, sp, n % 2, weights[n])
            for n, src in enumerate(srcs):
                if weights is not None:
                    sp.wait_ge(s["full"], MT * (2 * parts - 1 + n))
                load_slab(k, sp, n, src)
            if load is not None:
                load(sp)

        @block.tensor
        def _(pe):
            n = 0
            if weights is not None:
                for h in range(2):
                    k0 = 0
                    for part, kt in enumerate(kts):
                        slab_wait(k, pe, base + n)
                        w = k.slab(n, kt, 512)
                        for m in range(MT):
                            for kk in range(kt):
                                last = pe.matmul(k.bank[4 * h + m][:, :], lhs[:, k0 + kk, m * P:(m + 1) * P],
                                                 w[:, kk, :], start=k0 + kk == 0,
                                                 stop=part == parts - 1 and kk == kt - 1)
                            last.then_inc(s["full"], 1)
                        k0 += kt
                        n += 1
            if XT is not None:
                for m in range(MT):
                    pe.wait_ge(s["shifted"], m + 1)
                    if m >= 2:
                        pe.wait_ge(s["copied"], 2 * (m - 1))
                    for b in range(2):
                        bank = k.bank[2 * (m % 2) + b]
                        for q in range(4):
                            last = pe.transpose(bank[:, q * P:(q + 1) * P], X[:, m, (4 * b + q) * P:(4 * b + q + 1) * P],
                                                k.c("ident"))
                        last.then_inc(s["turned"], 1)

        @block.vector
        def _(dve):
            if gain is None:
                return
            dve.memset(k.small[:, 1106:1107], LN_EPS).then_inc(s["eps"], 1)
            if rows:
                dve.wait_ge(k.rows, 16 * rows)
            for h in range(2):
                for m in range(MT):
                    row = X[:, m, h * 512:(h + 1) * 512]
                    if weights is not None:
                        dve.wait_ge(s["full"], MT * (parts * (h + 1) - 1) + m + 1)
                        src = k.bank[4 * h + m][:, :]
                    elif acc is not None:
                        src = acc[:, m, h * 512:(h + 1) * 512]
                    if weights is not None or acc is not None:
                        dve.scalar_tensor_tensor(out=row, in0=row, scalar=ALPHA, in1=src, op0=ALU.mult,
                                                 op1=ALU.add).then_inc(s["added"], 1)
                    if h == 0:
                        continue
                    if weights is not None or acc is not None:
                        dve.wait_ge(s["added"], 5 + m)
                    if m:
                        dve.wait_ge(s["mv"], m)
                    for q in range(2):
                        dve.bn_stats(stat[:, 6 * q:6 * q + 6], X[:, m, q * 512:(q + 1) * 512]).then_inc(s["stats"], 1)
                    dve.wait_ge(s["stats"], 2 * m + 2)
                    dve.bn_aggr(mv[:, m, :], stat).then_inc(s["mv"], 1)
                    dve.wait_ge(s["rstd"], 2 * m + 2)
                    dve.tensor_scalar(X[:, m, :], X[:, m, :], mv[:, m, 0:1], rstd[:, m:m + 1], ALU.subtract,
                                      ALU.mult).then_inc(s["normed"], 1)
                    dve.wait_ge(s["normed"], m + 1)
                    dve.tensor_tensor(X[:, m, :], X[:, m, :], gain, ALU.mult).then_inc(s["scaled"], 1)
                    dve.wait_ge(s["scaled"], m + 1)
                    dve.tensor_tensor(X[:, m, :], X[:, m, :], shift, ALU.add).then_inc(s["shifted"], 1)

        @block.gpsimd
        def _(pool):
            if gain is None:
                return
            for m in range(MT):
                pool.wait_ge(s["mv"], m + 1)
                pool.tensor_scalar(rstd[:, m:m + 1], mv[:, m, 1:2], LN_EPS, None, ALU.add).then_inc(s["rstd"], 1)
                pool.wait_ge(s["rstd"], 2 * m + 1)
                pool.tensor_tensor(rstd[:, m:m + 1], rstd[:, m:m + 1], k.c("mhalf"), ALU.pow).then_inc(s["rstd"], 1)

        @block.scalar
        def _(act):
            if XT is not None:
                for m in range(MT):
                    for b in range(2):
                        act.wait_ge(s["turned"], 2 * m + b + 1)
                        act.activation(XT[:, 4 * b:4 * b + 4, m * P:(m + 1) * P],
                                       k.bank[2 * (m % 2) + b][:, :].rearrange("p (q t) -> p q t", q=4),
                                       ACT.Copy).then_inc(s["copied"], 1)


def phase_ffn(k, X):
    nc, io = k.nc, k.io
    n_f = D_FF // P
    n_up = 2 * n_f
    A = 3
    s = {n: k.sem("ffn_" + n) for n in ("hi", "lo", "used", "sig", "part", "h", "hh", "hl")}
    turned, x_hi, x_lo, full, added = (k.sem("ffn_" + n) for n in ("turned", "x_hi", "x_lo", "full", "added"))
    raw_in = [k.sem(f"ffn_raw{i}") for i in range(2)]
    scope = ExitStack()
    hold = lambda name, n, dt=F32: scope.enter_context(nc.sbuf_tensor("ffn_" + name, [P, n], dt))
    f32 = lambda ap: ap.bitcast(F32)
    xh, xl = (hold(n, KT * T, F32R)[:, :].rearrange("p (k t) -> p k t", k=KT) for n in ("xh", "xl"))
    hh, hl = (hold(n, n_f * T, F32R)[:, :].rearrange("p (f t) -> p f t", f=n_f) for n in ("hh", "hl"))
    raw = [hold(f"raw{i}", D) for i in range(2)]
    hi, lo = ([hold(f"{p}{i}", D, F32R) for i in range(2)] for p in ("hi", "lo"))
    sg, ht = ([hold(f"{n}{i}", T) for i in range(2)] for n in ("sg", "ht"))
    flat = lambda x, f: x[:, ds(f, 1), :].rearrange("p a t -> p (a t)")

    with nc.Block() as block:
        @block.sync
        def _(sp):
            for each in s.values():
                sp.sem_inc(each, A)

            def load(n, j, src):
                sp.wait_ge(s["lo"], n - 1 + A)
                sp.dma_start(raw[j][:, :], src).then_inc(raw_in[j], 16)

            up = lambda f, half: io["w_up"][ds(f, 1), :, half * D:(half + 1) * D].rearrange("a p c -> (a p) c")
            with sp.Fori(0, n_f) as f:
                for j in range(2):
                    load(2 * f + j, j, up(f, j))
            with sp.Fori(0, n_f // 2) as i:
                for j in range(2):
                    load(n_up + 2 * i + j, j, io["w_down"][ds(2 * i + j, 1)].rearrange("a p c -> (a p) c"))

        @block.tensor
        def _(pe):
            for m in range(MT):
                for b in range(2):
                    bank = k.bank[2 * (m % 4) + b]
                    for q in range(4):
                        last = pe.transpose(bank[:, q * P:(q + 1) * P], X[:, m, (4 * b + q) * P:(4 * b + q + 1) * P],
                                            k.c("ident"))
                    last.then_inc(turned, 1)
            pe.wait_ge(x_lo, 2 * MT)
            with pe.Fori(0, n_f // 2) as i:
                for j in range(2):
                    f = 2 * i + j
                    pe.wait_ge(s["h"], f - 1 + A)
                    for half in range(2):
                        pe.wait_ge(s["lo"], 2 * f + half + 1 + A)
                        for u in range(2):
                            bank = k.bank[2 * j + u][:, :]
                            for q in range(KT // 2):
                                kk = half * KT // 2 + q
                                w = slice(q * 2 * P + u * P, q * 2 * P + (u + 1) * P)
                                pe.matmul(bank, hi[half][:, w], xh[:, kk, :], start=kk == 0, stop=False)
                                pe.matmul(bank, lo[half][:, w], xh[:, kk, :], start=False, stop=False)
                                last = pe.matmul(bank, hi[half][:, w], xl[:, kk, :], start=False, stop=kk == KT - 1)
                        last.then_inc(s["used"], 1)
            for f in range(n_f):
                j = f % 2
                pe.wait_ge(s["lo"], n_up + f + 1 + A)
                pe.wait_ge(s["hl"], f + 1 + A)
                for half in (1, 0):
                    if f == 0 and half == 0:
                        pe.wait_ge(s["h"], n_f + A)
                    for m in range(MT):
                        bank = k.bank[4 * half + m][:, :]
                        rows, cols = slice(m * P, (m + 1) * P), slice(half * 512, half * 512 + 512)
                        pe.matmul(bank, hh[:, f, rows], hi[j][:, cols], start=f == 0, stop=False)
                        pe.matmul(bank, hh[:, f, rows], lo[j][:, cols], start=False, stop=False)
                        last = pe.matmul(bank, hl[:, f, rows], hi[j][:, cols], start=False, stop=f == n_f - 1)
                        if f == n_f - 1 and (half, m) != (0, MT - 1):
                            last.then_inc(full, 1)
                last.then_inc(s["used"], 1)

        @block.scalar
        def _(act):
            def split(turn, j, n):
                act.wait_ge(raw_in[j], 16 * turn + 16)
                act.wait_ge(s["used"], n - 1 + A)
                act.activation(hi[j][:, :], raw[j][:, :], ACT.Copy).then_inc(s["hi"], 1)

            def hidden_hi(f, j):
                act.wait_ge(s["h"], f + 1 + A)
                act.activation(flat(hh, f), ht[j][:, :], ACT.Copy).then_inc(s["hh"], 1)

            for n in range(2 * MT):
                m, b = n // 2, n % 2
                act.wait_ge(turned, n + 1)
                act.activation(xh[:, 4 * b:4 * b + 4, m * P:(m + 1) * P],
                               k.bank[n][:, :].rearrange("p (q t) -> p q t", q=4), ACT.Copy).then_inc(x_hi, 1)
                if n < 2:
                    split(0, n, n)
            with act.Fori(0, n_f // 2) as i:
                for j in range(2):
                    f = 2 * i + j
                    for half in range(2):
                        split(f + 1, half, 2 * f + half + 2)
                    act.wait_ge(s["used"], 2 * f + 2 + A)
                    act.activation(sg[j][:, :], k.bank[2 * j][:, :], ACT.Sigmoid).then_inc(s["sig"], 1)
                    hidden_hi(f, j)
            with act.Fori(0, n_f // 2 - 1) as i:
                for j in range(2):
                    split(n_f + 1 + i, j, n_up + 2 * i + j + 2)

        @block.vector
        def _(dve):
            def split(j, n):
                dve.wait_ge(s["hi"], n + 1 + A)
                dve.tensor_tensor(lo[j][:, :], raw[j][:, :], f32(hi[j][:, :]), ALU.subtract).then_inc(s["lo"], 1)

            for n in range(2 * MT):
                m, b = n // 2, n % 2
                dst = (slice(None), slice(4 * b, 4 * b + 4), slice(m * P, (m + 1) * P))
                dve.wait_ge(x_hi, n + 1)
                dve.tensor_tensor(xl[dst], k.bank[n][:, :].rearrange("p (q t) -> p q t", q=4), f32(xh[dst]),
                                  ALU.subtract).then_inc(x_lo, 1)
                if n < 2:
                    split(n, n)
            with dve.Fori(0, n_f // 2) as i:
                for j in range(2):
                    f = 2 * i + j
                    for half in range(2):
                        split(half, 2 * f + half + 2)
                    dve.wait_ge(s["sig"], f + 1 + A)
                    dve.wait_ge(s["hh"], f - 1 + A)
                    dve.tensor_tensor(sg[j][:, :], sg[j][:, :], k.bank[2 * j][:, :], ALU.mult).then_inc(s["part"], 1)
                    dve.wait_ge(s["part"], f + 1 + A)
                    dve.wait_ge(s["hl"], f - 1 + A)
                    dve.tensor_tensor(ht[j][:, :], sg[j][:, :], k.bank[2 * j + 1][:, :], ALU.mult).then_inc(s["h"], 1)
                    dve.wait_ge(s["hh"], f + 1 + A)
                    dve.tensor_tensor(flat(hl, f), ht[j][:, :], f32(flat(hh, f)), ALU.subtract).then_inc(s["hl"], 1)
            with dve.Fori(0, n_f // 2 - 1) as i:
                for j in range(2):
                    split(j, n_up + 2 * i + j + 2)
            for n in range(2 * MT):
                m, half = n % MT, 1 - n // MT
                if n < 2 * MT - 1:
                    dve.wait_ge(full, n + 1)
                else:
                    dve.wait_ge(s["used"], n_up + n_f + A)
                row = X[:, m, half * 512:half * 512 + 512]
                dve.scalar_tensor_tensor(out=row, in0=row, scalar=ALPHA, in1=k.bank[4 * half + m][:, :],
                                         op0=ALU.mult, op1=ALU.add).then_inc(added, 1)
    scope.close()


def phase_ple(k, tag, X, XT, pT, bias, tmp, weights, turn, nxt, rows):
    nc, io = k.nc, k.io
    s = {n: k.sem(f"{tag}_{n}") for n in ("ple", "gate", "biased", "sig", "mul", "added", "turned", "copied", "stored")}
    base = k.slabs
    k.slabs += 4
    with nc.Block() as block:
        @block.sync
        def _(sp):
            for n in (2, 3):
                sp.wait_ge(s["ple" if n == 2 else "gate"], MT)
                load_slab(k, sp, n % 2, weights(n))
            for n, src in enumerate(nxt):
                sp.wait_ge(s["ple" if n == 0 else "gate"], 2 * MT)
                load_slab(k, sp, n, src)
            if not turn:
                for m in range(MT):
                    sp.wait_ge(s["added"], MT + m + 1)
                    sp.dma_start(io["out"][0, m * P:(m + 1) * P, :], X[:, m, :]).then_inc(s["stored"], 16)
                sp.wait_ge(s["stored"], 16 * MT)

        @block.tensor
        def _(pe):
            pe.wait_ge(k.rows, rows)
            for h in range(2):
                slab_wait(k, pe, base + 2 * h)
                w = k.slab(0, 2, 512)
                for m in range(MT):
                    if h:
                        pe.wait_ge(s["mul"], m + 1)
                    for kk in range(2):
                        last = pe.matmul(k.bank[4 + m][:, :], pT[:, kk, m * P:(m + 1) * P], w[:, kk, :],
                                         start=kk == 0, stop=kk == 1)
                    last.then_inc(s["ple"], 1)
                slab_wait(k, pe, base + 2 * h + 1)
                w = k.slab(1, KT, 512)
                for m in range(MT):
                    for kk in range(KT):
                        last = pe.matmul(k.bank[m][:, :], XT[:, kk, m * P:(m + 1) * P], w[:, kk, :],
                                         start=kk == 0, stop=kk == KT - 1)
                    last.then_inc(s["gate"], 1)
            if turn:
                for m in range(MT):
                    pe.wait_ge(s["added"], MT + m + 1)
                    if m >= 2:
                        pe.wait_ge(s["copied"], 2 * (m - 1))
                    else:
                        pe.wait_ge(s["mul"], 2 * MT)
                    pe.wait_ge(s["biased"], 2 * MT)
                    for b in range(2):
                        bank = k.bank[4 + 2 * (m % 2) + b]
                        for q in range(4):
                            last = pe.transpose(bank[:, q * P:(q + 1) * P], X[:, m, (4 * b + q) * P:(4 * b + q + 1) * P],
                                                k.c("ident"))
                        last.then_inc(s["turned"], 1)

        @block.scalar
        def _(act):
            for n in range(2 * MT):
                act.wait_ge(s["biased"], n + 1)
                act.activation(tmp[:, n % 4, :], tmp[:, n % 4, :], ACT.Sigmoid).then_inc(s["sig"], 1)
            if turn:
                for m in range(MT):
                    for b in range(2):
                        act.wait_ge(s["turned"], 2 * m + b + 1)
                        act.activation(XT[:, 4 * b:4 * b + 4, m * P:(m + 1) * P],
                                       k.bank[4 + 2 * (m % 2) + b][:, :].rearrange("p (q t) -> p q t", q=4),
                                       ACT.Copy).then_inc(s["copied"], 1)

        @block.vector
        def _(dve):
            dve.wait_ge(k.rows, rows)
            for n in range(2 * MT):
                h, m = n // MT, n % MT
                cols = slice(h * 512, (h + 1) * 512)
                dve.wait_ge(s["gate"], n + 1)
                if h:
                    dve.wait_ge(s["added"], m + 1)
                dve.tensor_tensor(tmp[:, m, :], k.bank[m][:, :], bias[:, cols], ALU.add).then_inc(s["biased"], 1)
                dve.wait_ge(s["sig"], n + 1)
                dve.wait_ge(s["ple"], n + 1)
                dve.tensor_tensor(tmp[:, m, :], tmp[:, m, :], k.bank[4 + m][:, :], ALU.mult).then_inc(s["mul"], 1)
                dve.wait_ge(s["mul"], n + 1)
                dve.tensor_tensor(X[:, m, cols], X[:, m, cols], tmp[:, m, :], ALU.add).then_inc(s["added"], 1)


SM_GATEW, SM_PHI2, SM_PHI2V, SM_B1, SM_POS, SM_ROUTER, SM_BR = 0, 384, 640, 768, 772, 804, 868
SM_GATES, SM_WEIGHTS, SM_MISC = 876, 1108, 1140
R8_VS, R8_VW, R8_ROT, R8_CMPM, R8_RANK, R8_KC, R8_VC = 0, 1024, 2048, 3072, 3328, 3392, 3456


def phase_kv_q(k, XT, nxt):
    nc, io = k.nc, k.io
    s = {n: k.sem("kvq_" + n) for n in ("tables", "full", "free", "rot", "cos", "sin", "done", "twins")}
    base = k.slabs
    k.slabs += 8
    qn, qr = k.act(2), k.act(3)
    four = lambda r, a, n: k.region(r, a, n * T).rearrange("p (k t) -> p k t", t=T)
    z = [four(4, 0, 2), four(4, 2 * T, 2)]
    ks, kw = four(4, 4 * T, 2), four(4, 6 * T, 2)
    vs = k.region(8, R8_VS, 1024).rearrange("p (m c) -> p m c", m=MT)
    vw = k.region(8, R8_VW, 1024).rearrange("p (m c) -> p m c", m=MT)
    rot = k.region(8, R8_ROT, 1024).rearrange("p (i t) -> p i t", i=2)
    z2 = k.region(6).rearrange("p (j a e t) -> p j a e t", j=2, a=2, e=2)
    gw = k.small[:, SM_GATEW:SM_GATEW + 384].rearrange("p (k c) -> p k c", k=KT)
    gates = k.small[:, SM_GATES:SM_GATES + 192]
    tmp = four(5, 0, 2)
    dst = [z[0][:, a, :] for a in range(2)] + [z[1][:, a, :] for a in range(2)] + [ks[:, a, :] for a in range(2)]
    dst += [vs[:, m, :] for m in range(MT)] + [kw[:, a, :] for a in range(2)] + [vw[:, m, :] for m in range(MT)]
    dst += [qn[:, f, :] for f in range(KT)]
    first = [0, 2, 4, 6, 10, 12, 16, 20, 24]
    turns = [(4 + a, ks[:, a, :], ks[:, a, :]) for a in range(2)] + [(10 + a, kw[:, a, :], kw[:, a, :]) for a in range(2)]
    turns += [(16 + f, qn[:, f, :], qr[:, f, :]) for f in range(KT)]

    with nc.Block() as block:
        @block.sync
        def _(sp):
            sp.dma_start(k.region(8, R8_ROT, 1024 + 256 + 64), io["tables"]).then_inc(s["tables"], 16)
            sp.dma_start(k.small[:, 0:SM_BR], io["nsa_small"]).then_inc(s["tables"], 16)
            sp.dma_start(k.small[:, SM_BR:SM_BR + NE], io["router_b"].to_broadcast([P, NE])).then_inc(s["tables"], 16)
            for n in range(2, 8):
                sp.wait_ge(s["full"], first[n - 1])
                load_slab(k, sp, n % 2, io["w_kv"][n] if n < 6 else io["w_q"][n - 6])
            for n, src in enumerate(nxt):
                sp.wait_ge(s["full"], first[7 + n])
                load_slab(k, sp, n, src)
            for j in range(2):
                sp.wait_ge(s["free"], 2 * j + 2)
                for e in range(2):
                    part = z[j][64 * e:64 * e + 64, :, :]
                    sp.dma_start(z2[0:64, j, :, e, :], part).then_inc(s["twins"], 16)
                    sp.dma_start(z2[64:128, j, :, e, 0:T - 1], part[:, :, 1:T]).then_inc(s["twins"], 16)
            sp.wait_ge(s["twins"], 16 * 8)

        @block.tensor
        def _(pe):
            n = [0, 0]

            def room():
                if n[0] >= 4:
                    pe.wait_ge(s["free"], n[0] - 3)
                n[0] += 1
                return k.bank[(n[0] - 1) % 4]

            def rotate(count):
                for _ in range(count):
                    t = n[1]
                    n[1] += 1
                    pe.wait_ge(s["free"], turns[t][0] + 1)
                    if t >= 4:
                        pe.wait_ge(s["sin"], t - 3)
                    pe.matmul(k.bank[4 + t % 4][:, :], k.c("rmat"), turns[t][1], start=True,
                              stop=True).then_inc(s["rot"], 1)

            for i in range(8):
                slab_wait(k, pe, base + i)
                if i in (3, 5):
                    w = k.slab(i, KT, 256)
                    for m in range(MT):
                        bank = room()
                        for kk in range(KT):
                            last = pe.matmul(bank[:, 0:256], XT[:, kk, m * P:(m + 1) * P], w[:, kk, :],
                                             start=kk == 0, stop=kk == KT - 1)
                        last.then_inc(s["full"], 1)
                    rotate(2)
                    continue
                cols = 256 if i < 6 else 512
                w = k.slab(i, KT, cols)
                for o in range(cols // P):
                    bank = room()
                    for kk in range(KT):
                        last = pe.matmul(bank[:, :], w[:, kk, o * P:(o + 1) * P], XT[:, kk, :],
                                         start=kk == 0, stop=kk == KT - 1)
                    last.then_inc(s["full"], 1)
                if i == 7:
                    rotate(4)
            bank = room()
            pe.wait_ge(s["tables"], 48)
            for m in range(MT):
                for kk in range(KT):
                    last = pe.matmul(bank[:, m * 48:(m + 1) * 48], XT[:, kk, m * P:(m + 1) * P], gw[:, kk, :],
                                     start=kk == 0, stop=kk == KT - 1)
            last.then_inc(s["full"], 1)
            rotate(4)

        @block.scalar
        def _(act):
            for t, d in enumerate(dst):
                act.wait_ge(s["full"], t + 1)
                act.activation(d, k.bank[t % 4][:, 0:d.shape[1]], ACT.Copy).then_inc(s["free"], 1)
            act.wait_ge(s["full"], len(dst) + 1)
            act.wait_ge(s["tables"], 48)
            act.activation(gates, k.bank[len(dst) % 4][:, 0:192], ACT.Sigmoid).then_inc(s["free"], 1)

        @block.vector
        def _(dve):
            dve.wait_ge(s["tables"], 48)
            for t, (tile, src, out) in enumerate(turns):
                dve.wait_ge(s["rot"], t + 1)
                if t >= 2:
                    dve.wait_ge(s["done"], t - 1)
                dve.tensor_tensor(tmp[:, t % 2, :], k.bank[4 + t % 4][:, :], rot[:, 1, :], ALU.mult).then_inc(s["sin"], 1)
                dve.wait_ge(s["free"], tile + 1)
                dve.tensor_tensor(out, src, rot[:, 0, :], ALU.mult).then_inc(s["cos"], 1)
                dve.wait_ge(s["sin"], t + 1)
                dve.wait_ge(s["cos"], t + 1)
                dve.tensor_tensor(out, out, tmp[:, t % 2, :], ALU.add).then_inc(s["done"], 1)


def phase_compress(k, nxt):
    nc = k.nc
    s = {n: k.sem("cmp_" + n) for n in ("hidden", "pos", "bias", "u", "sq", "cube", "tanh", "half", "act", "keys",
                                        "values", "zero", "out")}
    base = k.slabs
    k.slabs += 2
    z2 = k.region(6).rearrange("p (j g t) -> p j g t", j=2, g=NKV)
    n_col = NKV * NCMP
    pos = k.small[:, SM_POS:SM_POS + 32].rearrange("p (j i) -> p j i", j=2)
    b1 = k.small[:, SM_B1:SM_B1 + 4]
    bias = k.small[:, SM_MISC:SM_MISC + 4]
    w2k = k.small[:, SM_PHI2:SM_PHI2 + 256].rearrange("p (h c) -> p h c", h=2)
    w2v = k.small[:, SM_PHI2V:SM_PHI2V + 128].rearrange("p (h c) -> p h c", h=2)
    buf = lambda i: k.region(4, i * 512, 4 * n_col).rearrange("p (i c) -> p i c", i=4)
    u, v = buf(0), buf(1)
    g = buf(2)
    kc = k.region(8, R8_KC, 64).rearrange("p (a n) -> p a n", a=2)
    vc = k.region(8, R8_VC, 256)[0:CMPW, :]

    with nc.Block() as block:
        @block.sync
        def _(sp):
            for n, src in enumerate(nxt):
                sp.wait_ge(s["hidden"], 2 * n + 2)
                load_slab(k, sp, n, src)

        @block.tensor
        def _(pe):
            for j in range(2):
                slab_wait(k, pe, base + j)
                w = k.slab(j, 16, HID)
                for h in range(2):
                    for i in range(16):
                        pe.matmul(k.bank[4][:, 2 * j + h:2 * j + h + 1], w[:, i, h * P:(h + 1) * P],
                                  pos[:, j, i:i + 1], start=i == 0, stop=i == 15).then_inc(s["pos"], 1)
                    for i in range(16):
                        span = z2[:, j, :, 2 * i:2 * i + CMP_STRIDE * (NCMP - 1) + 1:CMP_STRIDE]
                        last = pe.matmul(k.bank[2 * j + h][:, 0:n_col].rearrange("p (g n) -> p g n", g=NKV),
                                         w[:, i, h * P:(h + 1) * P], span, start=i == 0, stop=i == 15)
                    last.then_inc(s["hidden"], 1)
            pe.wait_ge(s["act"], 1)
            for h in range(2):
                last = pe.matmul(k.bank[5][:, 0:n_col], w2k[:, h, :], g[:, h, :], start=h == 0, stop=h == 1)
            last.then_inc(s["keys"], 1)
            for q in range(NKV):
                for h in range(2):
                    last = pe.matmul(k.bank[6][0:NCMP, q * DH:(q + 1) * DH], g[:, 2 + h, q * NCMP:(q + 1) * NCMP],
                                     w2v[:, h, :], start=h == 0, stop=h == 1)
            last.then_inc(s["values"], 1)

        @block.vector
        def _(dve):
            dve.memset(kc, 0.0).then_inc(s["zero"], 1)
            dve.memset(vc, 0.0).then_inc(s["zero"], 1)
            dve.wait_ge(s["pos"], 64)
            dve.tensor_tensor(bias, k.bank[4][:, 0:4], b1, ALU.add).then_inc(s["bias"], 1)
            dve.wait_ge(s["bias"], 1)
            for i in range(4):
                dve.wait_ge(s["hidden"], i + 1)
                dve.tensor_scalar(u[:, i, :], k.bank[i][:, 0:n_col], bias[:, i:i + 1], None, ALU.add).then_inc(s["u"], 1)
            dve.wait_ge(s["u"], 4)
            dve.tensor_tensor(v, u, u, ALU.mult).then_inc(s["sq"], 1)
            dve.wait_ge(s["sq"], 1)
            dve.tensor_scalar(v, v, 0.044715, 1.0, ALU.mult, ALU.add).then_inc(s["sq"], 1)
            dve.wait_ge(s["sq"], 2)
            dve.tensor_tensor(v, v, u, ALU.mult).then_inc(s["cube"], 1)
            dve.wait_ge(s["tanh"], 1)
            dve.tensor_scalar(v, v, 0.5, 0.5, ALU.mult, ALU.add).then_inc(s["half"], 1)
            dve.wait_ge(s["half"], 1)
            dve.tensor_tensor(g, v, u, ALU.mult).then_inc(s["act"], 1)
            dve.wait_ge(s["keys"], 1)
            dve.wait_ge(s["zero"], 2)
            keys = k.bank[5][:, 0:n_col].rearrange("p (a e n) -> p a e n", a=2, e=2)
            for e in range(2):
                dve.tensor_copy(kc[64 * e:64 * e + 64, :, 0:NCMP], keys[64 * e:64 * e + 64, :, e, :]).then_inc(s["out"], 1)
            dve.wait_ge(s["values"], 1)
            dve.tensor_copy(vc[0:NCMP, :], k.bank[6][0:NCMP, 0:256]).then_inc(s["out"], 1)

        @block.scalar
        def _(act):
            act.wait_ge(s["cube"], 1)
            act.activation(v, v, ACT.Tanh, scale=math.sqrt(2.0 / math.pi)).then_inc(s["tanh"], 1)


def phase_attend(k):
    assert T // 64 <= 8 and T <= 512
    nc = k.nc
    A = 17
    s = {n: k.sem("att_" + n) for n in (
        "keys_in", "values_in", "q_in", "cs", "cadd", "cmax", "csub", "cexp", "czero", "ctotal", "cguard", "crec", "ccoef", "cnorm",
        "cturn", "cevac", "cout", "scores", "masked", "max", "neg", "exp", "turn", "evac", "out",
        "rec", "coef", "norm", "stored")}
    qn, qr = k.act(2), k.act(3)
    four = lambda r, a, n: k.region(r, a, n * T).rearrange("p (k t) -> p k t", t=T)
    keys = [four(4, 4 * T, 2), four(4, 6 * T, 2)]
    vals = [k.region(8, R8_VS, 1024).rearrange("p (m c) -> p m c", m=MT),
            k.region(8, R8_VW, 1024).rearrange("p (m c) -> p m c", m=MT)]
    cm = k.region(8, R8_CMPM, 256).rearrange("p (i m n) -> p i m n", i=2, m=MT)
    kc = k.region(8, R8_KC, 64).rearrange("p (a n) -> p a n", a=2)
    vc = k.region(8, R8_VC, 256)[0:CMPW, :]
    attT = k.act(5)
    gates = k.small[:, SM_GATES:SM_GATES + 192].rearrange("p (m c) -> p m c", m=MT)
    Qn, Qr, K2 = k.region(6, 0, T), k.region(6, T, T), [k.region(6, 3328 - T, T), k.region(4, 1536, T)]
    Kc = k.region(6, 3328, CMPW)
    Pc = k.region(6, 3392, 256).rearrange("p (e m n) -> p e m n", e=2, m=MT)
    Pc8 = k.region(6, 3392, 256).rearrange("p (i n) -> p i n", i=8)
    V2 = k.region(4, 0, 1024).rearrange("p (b e m c) -> p b e m c", b=2, e=2, m=MT)
    Vc = k.region(4, 1024, 2 * DH)[0:CMPW, :]
    prob = [k.region(6, 1024, 1280), k.slots[1][:, 4096:5376]]
    pcT = k.slots[0][0:CMPW, 4096:5120].rearrange("p (i t) -> p i t", i=8)
    PT = [k.region(0, 2048 * i, 2048).rearrange("p (m t) -> p m t", m=MT) for i in range(2)]
    stat = k.region(6, 3904, 64)
    c8 = [stat[:, 8 * i:8 * i + 8] for i in range(3)]
    mx, sm, cf = ([stat[:, 24 + 8 * i + 4 * b:28 + 8 * i + 4 * b] for b in range(2)] for i in range(3))
    width = [P * (m + 1) for m in range(MT)]
    at_p = [0, P, 3 * P, 6 * P]
    items = [(0, 1), (2,), (3,)]
    tiles_up_to = [2, 3, 4]
    units = [(e, b) for e in range(2) for b in range(2)]
    score_bank = lambda u, i: (3 * u + i) % 4
    score_col = lambda m: P if m == 1 else 0

    with nc.Block() as block:
        @block.sync
        def _(sp):
            for each in s.values():
                sp.sem_inc(each, A)
            flat = lambda x, i: x[:, ds(i, 1), :].rearrange("p a t -> p (a t)")
            with sp.Fori(0, 2) as a:
                sp.wait_ge(s["scores"], 48 * a + A)
                sp.wait_ge(s["cs"], 8 * a + A)
                for dst, src in ((Kc, flat(kc, a)), (K2[0], flat(keys[0], a)), (K2[1], flat(keys[1], a))):
                    sp.dma_start(dst, src).then_inc(s["keys_in"], 16)
                sp.wait_ge(s["out"], 16 * a + A)
                sp.wait_ge(s["cout"], 8 * a + A)
                for b in range(2):
                    for e in range(2):
                        sp.dma_start(V2[:, b, e], vals[b][:, :, ds((2 * a + e) * DH, DH)]).then_inc(s["values_in"], 16)
                sp.dma_start(Vc, vc[:, ds(2 * a * DH, 2 * DH)]).then_inc(s["values_in"], 16)

        @block.gpsimd
        def _(pool):
            flat = lambda x, i: x[:, ds(i, 1), :].rearrange("p a t -> p (a t)")
            with pool.Fori(0, 2) as a:
                with pool.Fori(0, NQ) as r:
                    f = 4 * a + r
                    pool.wait_ge(s["cs"], 2 * f + A)
                    pool.wait_ge(s["scores"], 12 * f + A)
                    pool.nop(nofuse=True)
                    for dst, src in ((Qn, flat(qn, f)), (Qr, flat(qr, f))):
                        pool.tensor_copy(dst, src).then_inc(s["q_in"], 1)

        @block.tensor
        def _(pe):
            with pe.Fori(0, 2) as a:
                with pe.Fori(0, NQ) as r:
                    f = 4 * a + r

                    def scores(u):
                        e, b = units[u]
                        rows = slice(64 * e, 64 * e + 64)
                        for i, tiles in enumerate(items):
                            j = 3 * u + i - 4
                            before = 4 * (j // 3) + tiles_up_to[j % 3]
                            pe.wait_ge(s["exp"], 16 * f + before + A)
                            for m in tiles:
                                col = score_col(m)
                                last = pe.matmul(k.bank[score_bank(u, i)][:, col:col + width[m]],
                                                 Qr[rows, m * P:(m + 1) * P], K2[b][rows, 0:width[m]],
                                                 start=True, stop=True)
                            last.then_inc(s["scores"], 1)

                    def turn(u):
                        for i, tiles in enumerate(items):
                            pe.wait_ge(s["norm"], 16 * f + 4 * u + tiles_up_to[i] + A)
                            pe.wait_ge(s["evac"], 16 * f + 4 * u - 4 + tiles_up_to[i] + A)
                            if u == 0 and i > 0:
                                pe.wait_ge(s["cadd"], 2 * f + 2 + A)
                            if u == 1 and i < 2:
                                pe.wait_ge(s["cevac"], 2 * f + i + 1 + A)
                            for kb in range(tiles[-1] + 1):
                                for m in tiles:
                                    if m >= kb:
                                        at = kb + m - tiles[0]
                                        c = at_p[m] + kb * P
                                        last = pe.transpose(k.bank[4 + i][:, at * P:(at + 1) * P],
                                                            prob[u % 2][:, c:c + P], k.c("ident"))
                            last.then_inc(s["turn"], 1)

                    def values(u):
                        e, b = units[u]
                        if u == 0:
                            pe.wait_ge(s["values_in"], 80 * a + 80 + A)
                            pe.wait_ge(s["stored"], 2 * f - 1 + A)
                        pe.wait_ge(s["evac"], 16 * f + 4 * u + 4 + A)
                        for kb in range(MT):
                            last = pe.matmul(k.bank[7][64 * e:64 * e + 64, kb * P:T], V2[:, b, e, kb, :],
                                             PT[u % 2][:, kb, kb * P:T], start=u == 0 and kb == 0,
                                             stop=b == 1 and kb == MT - 1)
                        last.then_inc(s["out"], 1)

                    def compressed_values(e):
                        pe.wait_ge(s["cevac"], 2 * f + e + 1 + A)
                        if e == 1:
                            pe.wait_ge(s["stored"], 2 * f + A)
                        pe.matmul(k.bank[7][64 * e:64 * e + 64, :], Vc[:, e * DH:(e + 1) * DH],
                                  pcT[:, 4 * e:4 * e + 4, :].rearrange("p m t -> p (m t)"),
                                  start=e == 1, stop=False).then_inc(s["cout"], 1)

                    pe.wait_ge(s["keys_in"], 48 * a + 48 + A)
                    pe.wait_ge(s["q_in"], 2 * f + 1 + A)
                    pe.wait_ge(s["evac"], 16 * f + A)
                    for e in range(2):
                        for m in range(MT):
                            last = pe.matmul(k.bank[6 - e][:, m * CMPW:(m + 1) * CMPW],
                                             Qn[64 * e:64 * e + 64, m * P:(m + 1) * P], Kc[64 * e:64 * e + 64, :],
                                             start=True, stop=True)
                        last.then_inc(s["cs"], 1)
                    pe.wait_ge(s["q_in"], 2 * f + 2 + A)
                    scores(0)
                    scores(1)
                    turn(0)
                    scores(2)
                    values(0)
                    pe.wait_ge(s["cnorm"], f + 1 + A)
                    for i in range(8):
                        last = pe.transpose(k.bank[4 + i // 4][0:CMPW, (i % 4) * P:(i % 4 + 1) * P], Pc8[:, i, :],
                                            k.c("ident"))
                        if i % 4 == 3:
                            last.then_inc(s["cturn"], 1)
                    scores(3)
                    turn(1)
                    compressed_values(0)
                    values(1)
                    turn(2)
                    compressed_values(1)
                    values(2)
                    turn(3)
                    values(3)

        @block.scalar
        def _(act):
            with act.Fori(0, 2) as a:
                with act.Fori(0, NQ) as r:
                    f = 4 * a + r

                    def exps(u):
                        act.wait_ge(s["turn"], 12 * f + 3 * u - 3 + A)
                        act.wait_ge(s["rec"], 4 * f + u - 1 + A)
                        for i, tiles in enumerate(items):
                            act.wait_ge(s["neg"], 12 * f + 3 * u + i + 1 + A)
                            for m in tiles:
                                col = score_col(m)
                                act.activation(prob[u % 2][:, at_p[m]:at_p[m] + width[m]],
                                               k.bank[score_bank(u, i)][:, col:col + width[m]], ACT.Exp,
                                               bias=mx[u % 2][:, m:m + 1], scale=SCALE,
                                               accum_out=sm[u % 2][:, m:m + 1]).then_inc(s["exp"], 1)

                    def evacs(u):
                        act.wait_ge(s["out"], 4 * f + u - 1 + A)
                        for i, tiles in enumerate(items):
                            bank = k.bank[4 + i]
                            act.wait_ge(s["turn"], 12 * f + 3 * u + i + 1 + A)
                            if i == 0:
                                parts = [(PT[u % 2][:, 0, 0:2 * P], bank[:, 0:2 * P]),
                                         (PT[u % 2][:, 1, P:2 * P], bank[:, 2 * P:3 * P])]
                            else:
                                m = tiles[0]
                                parts = [(PT[u % 2][:, 0:m + 1, m * P:(m + 1) * P],
                                          bank[:, 0:width[m]].rearrange("p (k t) -> p k t", t=P))]
                            for dst, src in parts:
                                act.activation(dst, src, ACT.Copy).then_inc(s["evac"], 1)

                    def store(e):
                        act.wait_ge(s["out"], 4 * f + 2 * e + 2 + A)
                        rows = slice(64 * e, 64 * e + 64)
                        act.activation(attT[rows, ds(f, 1), :].rearrange("p a t -> p (a t)"), k.bank[7][rows, :],
                                       ACT.Copy).then_inc(s["stored"], 1)

                    act.wait_ge(s["csub"], f + 1 + A)
                    act.activation(Pc8, Pc8, ACT.Exp, scale=SCALE).then_inc(s["cexp"], 1)
                    exps(0)
                    evacs(0)
                    exps(1)
                    exps(2)
                    act.wait_ge(s["cout"], 2 * f + A)
                    for i in range(2):
                        act.wait_ge(s["cturn"], 2 * f + i + 1 + A)
                        act.activation(pcT[:, 4 * i:4 * i + 4, :],
                                       k.bank[4 + i][0:CMPW, :].rearrange("p (i t) -> p i t", i=4),
                                       ACT.Copy).then_inc(s["cevac"], 1)
                    evacs(1)
                    exps(3)
                    evacs(2)
                    store(0)
                    evacs(3)
                    store(1)

        @block.vector
        def _(dve):
            with dve.Fori(0, 2) as a:
                with dve.Fori(0, NQ) as r:
                    f = 4 * a + r
                    head = lambda e: 8 * a + 4 * e + r
                    spread8 = lambda x: x.rearrange("p (i n) -> p i n", n=1).to_broadcast([P, 8, CMPW])
                    n1 = f + 1

                    def maxima(u):
                        for i, tiles in enumerate(items):
                            n = 12 * f + 3 * u + i + 1 + A
                            bank = k.bank[score_bank(u, i)]
                            dve.wait_ge(s["scores"], n)
                            if i == 0:
                                diag = bank[:, :].rearrange("p (i c) -> p i c", c=2 * P)[:, :, 0:P]
                                causal = k.c("causal").rearrange("p (i c) -> p i c", i=1).to_broadcast([P, 2, P])
                            else:
                                diag, causal = bank[:, width[tiles[0]] - P:width[tiles[0]]], k.c("causal")
                            dve.tensor_tensor(diag, diag, causal, ALU.add).then_inc(s["masked"], 1)
                            dve.wait_ge(s["masked"], n)
                            for m in tiles:
                                col = score_col(m)
                                dve.tensor_reduce(mx[u % 2][:, m:m + 1], bank[:, col:col + width[m]], AX.X,
                                                  ALU.max).then_inc(s["max"], 1)
                            dve.wait_ge(s["max"], 16 * f + 4 * u + tiles_up_to[i] + A)
                            both = mx[u % 2][:, tiles[0]:tiles[-1] + 1]
                            dve.tensor_scalar(both, both, -SCALE, None, ALU.mult).then_inc(s["neg"], 1)

                    def normalise(u):
                        e, b = units[u]
                        n = 4 * f + u
                        dve.wait_ge(s["exp"], 16 * f + 4 * u + 4 + A)
                        dve.reciprocal(cf[u % 2], sm[u % 2]).then_inc(s["rec"], 1)
                        dve.wait_ge(s["rec"], n + 1 + A)
                        dve.tensor_tensor(cf[u % 2], cf[u % 2], gates[:, :, ds(head(e) * 3 + 1 + b, 1)].rearrange(
                            "p m o -> p (m o)"), ALU.mult).then_inc(s["coef"], 1)
                        dve.wait_ge(s["coef"], n + 1 + A)
                        for m in range(MT):
                            mine = prob[u % 2][:, at_p[m]:at_p[m] + width[m]]
                            dve.tensor_scalar(mine, mine, cf[u % 2][:, m:m + 1], None, ALU.mult).then_inc(s["norm"], 1)

                    dve.wait_ge(s["cturn"], 2 * f + A)
                    for e in range(2):
                        dve.wait_ge(s["cs"], 2 * f + e + 1 + A)
                        dve.tensor_tensor(Pc[:, e], k.bank[6 - e][:, 0:P].rearrange("p (m n) -> p m n", m=MT),
                                          cm[:, 0], ALU.add).then_inc(s["cadd"], 1)
                    dve.wait_ge(s["cadd"], 2 * f + 2 + A)
                    dve.tensor_reduce(c8[0], Pc8, AX.X, ALU.max).then_inc(s["cmax"], 1)
                    dve.wait_ge(s["cmax"], n1 + A)
                    dve.tensor_tensor(Pc8, Pc8, spread8(c8[0]), ALU.subtract).then_inc(s["csub"], 1)
                    maxima(0)
                    normalise(0)
                    maxima(1)
                    dve.wait_ge(s["cexp"], n1 + A)
                    for e in range(2):
                        dve.tensor_tensor(Pc[:, e], Pc[:, e], cm[:, 1], ALU.mult).then_inc(s["czero"], 1)
                    dve.wait_ge(s["czero"], 2 * f + 2 + A)
                    dve.tensor_reduce(c8[1], Pc8, AX.X, ALU.add).then_inc(s["ctotal"], 1)
                    dve.wait_ge(s["ctotal"], n1 + A)
                    dve.tensor_scalar(c8[1], c8[1], 1e-30, None, ALU.max).then_inc(s["cguard"], 1)
                    dve.wait_ge(s["cguard"], n1 + A)
                    dve.reciprocal(c8[2], c8[1]).then_inc(s["crec"], 1)
                    dve.wait_ge(s["crec"], n1 + A)
                    for e in range(2):
                        dve.tensor_tensor(c8[2][:, 4 * e:4 * e + 4], c8[2][:, 4 * e:4 * e + 4],
                                          gates[:, :, ds(head(e) * 3, 1)].rearrange("p m o -> p (m o)"),
                                          ALU.mult).then_inc(s["ccoef"], 1)
                    dve.wait_ge(s["ccoef"], 2 * f + 2 + A)
                    dve.tensor_tensor(Pc8, Pc8, spread8(c8[2]), ALU.mult).then_inc(s["cnorm"], 1)
                    maxima(2)
                    normalise(1)
                    normalise(2)
                    maxima(3)
                    normalise(3)


def phase_route(k, XT):
    nc = k.nc
    s = {n: k.sem("route_" + n) for n in ("full", "chain", "exp", "picks", "counted")}
    wr = k.small[:, SM_ROUTER:SM_ROUTER + 64].rearrange("p (k e) -> p k e", k=KT)
    br = k.small[:, SM_BR:SM_BR + NE].rearrange("p (m e) -> p m e", m=1).to_broadcast([P, MT, NE])
    lower = k.region(8, R8_RANK, 64).rearrange("p (e g) -> p e g", e=NE)
    at = lambda a, n: k.region(6, a, n)
    L = at(0, 32).rearrange("p (m e) -> p m e", m=MT)
    big = [at(512 * (i + 1), 256).rearrange("p (m e g) -> p m e g", m=MT, e=NE) for i in range(3)]
    rank, sel0, sel1, t = (at(64 + 64 * i, 32).rearrange("p (m e) -> p m e", m=MT) for i in range(4))
    l0, l1, den = (at(384 + 16 * i, 4) for i in range(3))
    picks, before, dest, zero = (at(2304 + 64 * i, 32).rearrange("p (m e) -> p m e", m=MT) for i in range(4))
    total, count, nblk, bend = (at(2560 + 16 * i, NE) for i in range(4))
    be = at(2624, 16)
    w0, w1 = k.small[:, SM_WEIGHTS:SM_WEIGHTS + 4], k.small[:, SM_WEIGHTS + 4:SM_WEIGHTS + 8]
    k.dest = k.small[:, SM_WEIGHTS + 8:SM_WEIGHTS + 16]
    wide = lambda x: x.rearrange("p (m e) -> p m e", e=1).to_broadcast([P, MT, NE])

    with nc.Block() as block:
        @block.tensor
        def _(pe):
            for m in range(MT):
                for kk in range(KT):
                    last = pe.matmul(k.bank[0][:, m * NE:(m + 1) * NE], XT[:, kk, m * P:(m + 1) * P], wr[:, kk, :],
                                     start=kk == 0, stop=kk == KT - 1)
            last.then_inc(s["full"], 1)
            pe.wait_ge(s["picks"], 1)
            for m in range(MT):
                pe.matmul(k.bank[1][:, m * NE:(m + 1) * NE], k.c("tri"), picks[:, m], start=True, stop=False)
                pe.matmul(k.bank[1][:, m * NE:(m + 1) * NE], k.c("ones"), before[:, m], start=False, stop=True)
            pe.matmul(k.bank[2][:, 0:NE], k.c("ones"), total, start=True, stop=True).then_inc(s["counted"], 1)

        @block.scalar
        def _(act):
            act.wait_ge(s["chain"], 11)
            act.activation(l1, l1, ACT.Exp).then_inc(s["exp"], 1)

        @block.vector
        def _(dve):
            n = [0]

            def link(op):
                n[0] += 1
                op.then_inc(s["chain"], 1)
                dve.wait_ge(s["chain"], n[0])

            dve.wait_ge(s["full"], 1)
            dve.memset(at(2304, 256), 0.0)
            link(dve.tensor_tensor(L, k.bank[0][:, 0:32].rearrange("p (m e) -> p m e", m=MT), br, ALU.add))
            for m in range(MT):
                mine = L[:, m].rearrange("p (e g) -> p e g", g=1).to_broadcast([P, NE, NE])
                other = L[:, m].rearrange("p (e g) -> p e g", e=1).to_broadcast([P, NE, NE])
                dve.tensor_tensor(big[0][:, m], other, mine, ALU.is_gt)
                op = dve.tensor_tensor(big[1][:, m], other, mine, ALU.is_equal)
            link(op)
            low = lower.rearrange("p e (m g) -> p m e g", m=1).to_broadcast([P, MT, NE, NE])
            link(dve.tensor_tensor(big[1], big[1], low, ALU.mult))
            link(dve.tensor_tensor(big[2], big[1], big[0], ALU.add))
            link(dve.tensor_reduce(rank, big[2], AX.X, ALU.add))
            dve.tensor_scalar(sel0, rank, 0.0, None, ALU.is_equal)
            link(dve.tensor_scalar(sel1, rank, 1.0, None, ALU.is_equal))
            link(dve.tensor_tensor(t, L, sel0, ALU.mult))
            link(dve.tensor_reduce(l0, t, AX.X, ALU.add))
            link(dve.tensor_tensor(t, L, sel1, ALU.mult))
            link(dve.tensor_reduce(l1, t, AX.X, ALU.add))
            link(dve.tensor_tensor(l1, l1, l0, ALU.subtract))
            dve.wait_ge(s["exp"], 1)
            link(dve.tensor_scalar(den, l1, 1.0, None, ALU.add))
            link(dve.reciprocal(den, den))
            link(dve.tensor_tensor(l1, l1, den, ALU.mult))
            dve.tensor_copy(w0, den)
            dve.tensor_copy(w1, l1)
            link(dve.tensor_tensor(picks, sel0, sel1, ALU.add))
            link(dve.tensor_tensor(before, zero, picks, ALU.mult))
            for m in range(1, MT):
                link(dve.tensor_tensor(before[:, m], before[:, m - 1], picks[:, m - 1], ALU.add))
            link(dve.tensor_tensor(total, before[:, MT - 1], picks[:, MT - 1], ALU.add))
            dve.engine_nop().then_inc(s["picks"], 1)
            dve.wait_ge(s["counted"], 1)
            link(dve.tensor_copy(count, k.bank[2][:, 0:NE]))
            link(dve.tensor_scalar(nblk, count, 0.0, None, ALU.is_gt))
            for j in range(1, MT):
                link(dve.scalar_tensor_tensor(out=nblk, in0=count, scalar=float(P * j), in1=nblk, op0=ALU.is_gt,
                                              op1=ALU.add))
            link(dve.tensor_tensor_scan(bend, k.c("ones")[:, 0:NE], nblk, 0.0, ALU.mult, ALU.add))
            link(dve.tensor_tensor(nblk, bend, nblk, ALU.subtract))
            link(dve.tensor_scalar(nblk, nblk, float(P), None, ALU.mult))
            start = nblk.rearrange("p (m e) -> p m e", m=1).to_broadcast([P, MT, NE])
            link(dve.tensor_tensor(dest, k.bank[1][:, 0:32].rearrange("p (m e) -> p m e", m=MT), start, ALU.add))
            for sel, row in ((sel0, k.dest[:, 0:4]), (sel1, k.dest[:, 4:8])):
                link(dve.tensor_tensor(t, dest, sel, ALU.mult))
                link(dve.tensor_reduce(row, t, AX.X, ALU.add))
            link(dve.tensor_copy(k.row_index[:, :], k.dest))
            blocks = k.c("iota")[:, 0:16].rearrange("p (b e) -> p b e", e=1).to_broadcast([P, 16, NE])
            ends = bend.rearrange("p (b e) -> p b e", b=1).to_broadcast([P, 16, NE])
            past = at(2048, 128).rearrange("p (b e) -> p b e", b=16)
            link(dve.tensor_tensor(past, ends, blocks, ALU.is_le))
            link(dve.tensor_reduce(be, past, AX.X, ALU.add))
            link(dve.tensor_scalar(be, be, float(NE - 1), None, ALU.min))
            link(dve.tensor_copy(k.block_expert[:, :], be))


def phase_experts(k, X):
    nc, io = k.nc, k.io
    n_f = D_FFE // P
    U = 3 * n_f
    RAW, SPLIT = n_f, 5
    A = RAW + 1
    s = {n: k.sem("moe_" + n) for n in (
        "xhi", "xlo", "sel0", "sel", "iota", "gh", "gl", "xgh", "xgl", "hi", "lo", "used",
        "sig", "part", "h", "turn", "th", "tl", "y", "y_out")}
    raw_in = [k.sem(f"moe_raw{i}") for i in range(RAW)]
    stored = k.sem("moe_stored")
    scope = ExitStack()
    hold = lambda name, n, dt=F32: scope.enter_context(nc.sbuf_tensor("moe_" + name, [P, n], dt))
    f32 = lambda ap: ap.bitcast(F32)
    raw = [hold(f"raw{i}", D) for i in range(RAW)]
    hi, lo = ([hold(f"{p}{i}", D, F32R) for i in range(SPLIT)] for p in ("hi", "lo"))
    xh, xl = hold("xh", TILE, F32R), hold("xl", TILE, F32R)
    sel = hold("sel", T, F32R)
    sel_tmp, iota = hold("sel_tmp", T), hold("iota", P)
    gh, gl = hold("gh", KT * P, F32R), hold("gl", KT * P, F32R)
    h, sg = hold("h", D_FFE), hold("sg", 2 * P)
    th, tl = hold("th", D_FFE, F32R), hold("tl", D_FFE, F32R)
    y = hold("y", D)
    before = lambda u: u - SPLIT if u >= SPLIT else max(v for v in range(U) if v % SPLIT == u % SPLIT) - U
    slab_done = lambda x: 2 * x + 2

    def each_block(eng):
        return eng.Fori(0, NBLK)

    with nc.Block() as block:
        @block.sync
        def _(sp):
            for each in s.values():
                sp.sem_inc(each, A)

            def load(b, u, e):
                sp.wait_ge(s["lo"], U * b + u - RAW + 1 + A)
                if u < 2 * n_f:
                    src = io["m_up"][ds(e * n_f + u // 2, 1), :, u % 2 * D:(u % 2 + 1) * D]
                else:
                    src = io["m_down"][ds(e * n_f + u - 2 * n_f, 1)]
                sp.dma_start(raw[u % RAW][:, :], src.rearrange("a p c -> (a p) c")).then_inc(raw_in[u % RAW], 16)

            e0 = sp.value_load(k.block_expert[0:1, 0:1], min_val=0, max_val=NE - 1)
            for u in range(RAW):
                load(0, u, e0)
            with each_block(sp) as b:
                e = sp.value_load(k.block_expert[0:1, ds(b, 1)], min_val=0, max_val=NE - 1)
                nxt = sp.value_load(k.block_expert[0:1, ds(b + 1, 1)], min_val=0, max_val=NE - 1)
                for u in range(RAW, U):
                    load(b, u, e)
                for u in range(RAW):
                    load(b + 1, u, nxt)
            for each in raw_in:
                sp.wait_ge(each, 16 * (U // RAW * NBLK + 1))

        @block.gpsimd
        def _(pool):
            with each_block(pool) as b:
                pool.wait_ge(s["y"], 2 * b + 2 + A)
                pool.nop(nofuse=True)
                pool.dma_start(io["rows_y"][ds(b * P, P), :], y[:, :]).then_inc(stored, 16)
                pool.wait_ge(stored, 16 * b + 16)
                pool.sem_inc(s["y_out"], 1)
            pool.wait_ge(stored, 16 * NBLK)

        @block.tensor
        def _(pe):
            def gather(b):
                pe.wait_ge(s["sel"], b + 1 + A)
                for part, banks, sem in ((xh, (6, 7), s["gh"]), (xl, (0, 1), s["gl"])):
                    if part is xl:
                        pe.wait_ge(s["h"], n_f * b + A)
                    for i in range(2):
                        for q in range(4):
                            for m in range(MT):
                                f = 4 * i + q
                                last = pe.matmul(k.bank[banks[i]][:, q * P:(q + 1) * P],
                                                 part[:, m * D + f * P:m * D + (f + 1) * P], sel[:, m * P:(m + 1) * P],
                                                 start=m == 0, stop=m == MT - 1)
                        last.then_inc(sem, 1)

            def turn(b, i):
                n = min(4, n_f - 4 * i)
                pe.wait_ge(s["h"], n_f * b + 4 * i + n + A)
                pe.wait_ge(s["tl"], 3 * b + (1 if i == 2 else 0) + A)
                for q in range(n):
                    last = pe.transpose(k.bank[4 + i % 2][:, q * P:(q + 1) * P],
                                        h[:, (4 * i + q) * P:(4 * i + q + 1) * P], k.c("ident"))
                last.then_inc(s["turn"], 1)

            pe.wait_ge(s["xlo"], MT + A)
            gather(0)
            with each_block(pe) as b:
                pe.wait_ge(s["xgh"], 2 * b + 2 + A)
                pe.wait_ge(s["xgl"], 2 * b + 2 + A)
                for u in range(2 * n_f):
                    x = u // 2
                    pe.wait_ge(s["lo"], U * b + u + 1 + A)
                    if x >= 2 and u % 2 == 0:
                        pe.wait_ge(s["h"], n_f * b + x - 1 + A)
                    out = k.bank[x % 2][:, 0:2 * P]
                    wh, wl = hi[u % SPLIT], lo[u % SPLIT]
                    for kk in range(KT // 2):
                        first, end = u % 2 == 0 and kk == 0, u % 2 == 1 and kk == KT // 2 - 1
                        cols = slice((u % 2 * 4 + kk) * P, (u % 2 * 4 + kk + 1) * P)
                        w = slice(kk * 2 * P, (kk + 1) * 2 * P)
                        pe.matmul(out, gh[:, cols], wh[:, w], start=first, stop=False)
                        pe.matmul(out, gh[:, cols], wl[:, w], start=False, stop=False)
                        last = pe.matmul(out, gl[:, cols], wh[:, w], start=False, stop=end)
                    last.then_inc(s["used"], 1)
                    if u == 13:
                        turn(b, 0)
                turn(b, 1)
                gather(b + 1)
                turn(b, 2)
                for x in range(n_f):
                    u = 2 * n_f + x
                    pe.wait_ge(s["lo"], U * b + u + 1 + A)
                    pe.wait_ge(s["tl"], 3 * b + x // 4 + 1 + A)
                    if x == 0:
                        pe.wait_ge(s["y"], 2 * b + A)
                    cols = slice(x * P, (x + 1) * P)
                    for a, w in ((th, hi), (th, lo), (tl, hi)):
                        for i in range(2):
                            last = pe.matmul(k.bank[2 + i][:, :], a[:, cols], w[u % SPLIT][:, i * 512:(i + 1) * 512],
                                             start=x == 0 and a is th and w is hi, stop=x == n_f - 1 and a is tl)
                    last.then_inc(s["used"], 1)

        @block.scalar
        def _(act):
            def split(b, u):
                act.wait_ge(raw_in[u % RAW], 16 * (U // RAW * b + u // RAW + 1))
                act.wait_ge(s["used"], U * b + before(u) + 1 + A)
                act.activation(hi[u % SPLIT][:, :], raw[u % RAW][:, :], ACT.Copy).then_inc(s["hi"], 1)

            def sigmoid(b, x):
                act.wait_ge(s["used"], U * b + slab_done(x) + A)
                act.wait_ge(s["h"], n_f * b + max(x - 1, 0) + A)
                act.activation(sg[:, x % 2 * P:(x % 2 + 1) * P], k.bank[x % 2][:, 0:P],
                               ACT.Sigmoid).then_inc(s["sig"], 1)

            def gathered(b, i):
                act.wait_ge(s["gh"], 2 * b + i + 1 + A)
                act.activation(gh[:, i * 512:(i + 1) * 512], k.bank[6 + i][:, :], ACT.Copy).then_inc(s["xgh"], 1)

            def turned(b, i):
                n = min(4, n_f - 4 * i) * P
                act.wait_ge(s["turn"], 3 * b + i + 1 + A)
                act.wait_ge(s["used"], U * b + A)
                act.activation(th[:, i * 512:i * 512 + n], k.bank[4 + i % 2][:, 0:n], ACT.Copy).then_inc(s["th"], 1)

            for m in range(MT):
                act.activation(xh[:, m * D:(m + 1) * D], X[:, m, :], ACT.Copy).then_inc(s["xhi"], 1)
            for u in range(SPLIT):
                split(0, u)
            for i in range(2):
                gathered(0, i)
            with each_block(act) as b:
                for u in range(SPLIT, 2 * n_f + SPLIT):
                    if (u - SPLIT) % 2 == 1:
                        sigmoid(b, (u - SPLIT) // 2)
                    split(b, u)
                    if u == 20:
                        turned(b, 0)
                turned(b, 1)
                for i in range(2):
                    gathered(b + 1, i)
                turned(b, 2)
                for u in range(2 * n_f + SPLIT, U):
                    split(b, u)
                for u in range(SPLIT):
                    split(b + 1, u)
                act.wait_ge(s["y_out"], b + A)
                for i in range(2):
                    act.wait_ge(s["used"], U * b + U + A)
                    act.activation(y[:, i * 512:(i + 1) * 512], k.bank[2 + i][:, :], ACT.Copy).then_inc(s["y"], 1)

        @block.vector
        def _(dve):
            def split(b, u):
                dve.wait_ge(s["hi"], U * b + u + 1 + A)
                dve.tensor_tensor(lo[u % SPLIT][:, :], raw[u % RAW][:, :], f32(hi[u % SPLIT][:, :]),
                                  ALU.subtract).then_inc(s["lo"], 1)

            def hidden(b, x):
                mine = sg[:, x % 2 * P:(x % 2 + 1) * P]
                dve.wait_ge(s["sig"], n_f * b + x + 1 + A)
                dve.tensor_tensor(mine, mine, k.bank[x % 2][:, 0:P], ALU.mult).then_inc(s["part"], 1)
                dve.wait_ge(s["part"], n_f * b + x + 1 + A)
                dve.wait_ge(s["turn"], 3 * b + A)
                dve.tensor_tensor(h[:, x * P:(x + 1) * P], mine, k.bank[x % 2][:, P:2 * P],
                                  ALU.mult).then_inc(s["h"], 1)

            def select(b, step):
                m = step % MT
                if step < MT:
                    if step == 0:
                        dve.wait_ge(s["gl"], 2 * b + A)
                        dve.wait_ge(s["iota"], b + 1 + A)
                    dve.tensor_scalar(sel_tmp[:, m * P:(m + 1) * P], iota[:, :], k.dest[:, m:m + 1], None,
                                      ALU.is_equal).then_inc(s["sel0"], 1)
                elif step < 2 * MT:
                    dve.wait_ge(s["sel0"], MT * b + m + 1 + A)
                    op = dve.scalar_tensor_tensor(out=sel[:, m * P:(m + 1) * P], in0=iota[:, :],
                                                  scalar=k.dest[:, 4 + m:5 + m], in1=sel_tmp[:, m * P:(m + 1) * P],
                                                  op0=ALU.is_equal, op1=ALU.add)
                    if m == MT - 1:
                        op.then_inc(s["sel"], 1)
                else:
                    dve.wait_ge(s["sel"], b + 1 + A)
                    dve.tensor_scalar(iota[:, :], iota[:, :], float(P), None, ALU.add).then_inc(s["iota"], 1)

            def gathered(b, i):
                dve.wait_ge(s["gl"], 2 * b + i + 1 + A)
                dve.tensor_copy(gl[:, i * 512:(i + 1) * 512], k.bank[i][:, :]).then_inc(s["xgl"], 1)

            def turned(b, i):
                n = min(4, n_f - 4 * i) * P
                dve.wait_ge(s["th"], 3 * b + i + 1 + A)
                dve.tensor_tensor(tl[:, i * 512:i * 512 + n], k.bank[4 + i % 2][:, 0:n],
                                  f32(th[:, i * 512:i * 512 + n]), ALU.subtract).then_inc(s["tl"], 1)

            dve.tensor_copy(iota[:, :], k.c("iota")).then_inc(s["iota"], 1)
            for step in range(2 * MT + 1):
                select(0, step)
            for m in range(MT):
                dve.wait_ge(s["xhi"], m + 1 + A)
                dve.tensor_tensor(xl[:, m * D:(m + 1) * D], X[:, m, :], f32(xh[:, m * D:(m + 1) * D]),
                                  ALU.subtract).then_inc(s["xlo"], 1)
            for u in range(SPLIT):
                split(0, u)
            for i in range(2):
                gathered(0, i)
            with each_block(dve) as b:
                for u in range(SPLIT, 2 * n_f + SPLIT):
                    if (u - SPLIT) % 2 == 1:
                        hidden(b, (u - SPLIT) // 2)
                    split(b, u)
                    if u < SPLIT + 2 * MT + 1:
                        select(b + 1, u - SPLIT)
                    if u == 20:
                        turned(b, 0)
                turned(b, 1)
                for i in range(2):
                    gathered(b + 1, i)
                turned(b, 2)
                for u in range(2 * n_f + SPLIT, U):
                    split(b, u)
                for u in range(SPLIT):
                    split(b + 1, u)
    scope.close()


def phase_collect(k, first, second, nxt):
    nc, io = k.nc, k.io
    rows, weighted, done = k.sem("collect_rows"), k.sem("collect_weighted"), k.sem("collect_done")
    w = k.small[:, SM_WEIGHTS:SM_WEIGHTS + 8]
    with nc.Block() as block:
        @block.gpsimd
        def _(pool):
            for m in range(MT):
                for j, dst in enumerate((first, second)):
                    at = bass.IndirectOffsetOnAxis(ap=k.row_index[:, 4 * j + m:4 * j + m + 1], axis=0)
                    pool.indirect_dma_start(dst[:, m, :], None, io["rows_y"], at).then_inc(rows, 16)

        @block.sync
        def _(sp):
            for n, src in enumerate(nxt):
                load_slab(k, sp, n, src)
            flat = io["rows"].rearrange("(o r) d -> o (r d)", o=1)
            sp.dma_start(k.region(7, 2 * D, 2 * D), flat[:, 6 * D:8 * D].to_broadcast([P, 2 * D])).then_inc(k.rows, 16)
            sp.dma_start(k.region(5, D, D), flat[:, 9 * D:10 * D].to_broadcast([P, D])).then_inc(k.rows, 16)
            sp.dma_start(k.region(5, 2 * D, 2 * T), io["pT"][1]).then_inc(k.rows, 16)
            sp.wait_ge(k.rows, 16 * 9)

        @block.vector
        def _(dve):
            dve.wait_ge(rows, 16 * 2 * MT)
            for m in range(MT):
                dve.tensor_scalar(second[:, m, :], second[:, m, :], w[:, 4 + m:5 + m], None,
                                  ALU.mult).then_inc(weighted, 1)
                dve.wait_ge(weighted, m + 1)
                dve.scalar_tensor_tensor(out=first[:, m, :], in0=first[:, m, :], scalar=w[:, m:m + 1],
                                         in1=second[:, m, :], op0=ALU.mult, op1=ALU.add).then_inc(done, 1)


def build(nc, io):
    with ExitStack() as ctx:
        k = Core(nc, ctx, io)
        k.open_arena("a")
        phase_load(k)
        phase_project(k)
        phase_scale(k)
        phase_recurrence(k)
        phase_gate(k)
        X, XT = k.tok(1), k.act(0)
        row = lambda r, i: k.region(r, i * D, D)
        phase_out_norm(k, "mixa", k.act(3), io["w_o_a"], [KT], X, row(6, 0), row(6, 1), rows=2)
        k.close_arena()
        phase_ffn(k, X)
        k.clear_sems()
        k.open_arena("b")
        XT = k.act(0)
        ple = lambda l: lambda n: io["ple_w"][l, n // 2] if n % 2 == 0 else io["ple_g"][l, n // 2]

        def second_rows(sp):
            flat = io["rows"].rearrange("(o r) d -> o (r d)", o=1)
            for dst, src in ((k.region(6, 2 * D, 2 * D), flat[:, 2 * D:4 * D].to_broadcast([P, 2 * D])),
                             (k.region(5, D, D), flat[:, 8 * D:9 * D].to_broadcast([P, D])),
                             (k.region(5, 2 * D, 2 * T), io["pT"][0]),
                             (k.region(7, 0, 2 * D), flat[:, 4 * D:6 * D].to_broadcast([P, 2 * D]))):
                sp.dma_start(dst, src).then_inc(k.rows, 16)

        phase_out_norm(k, "ffn_ln", None, None, [], X, row(6, 2), row(6, 3), XT, nxt=[ple(0)(n) for n in range(2)],
                       rows=6, load=second_rows)
        pT = lambda r, a: k.region(r, a, 2 * T).rearrange("p (k t) -> p k t", k=2)
        phase_ple(k, "ple0", X, XT, pT(5, 2 * D), row(5, 1), k.region(8, 0, 2048).rearrange("p (m t) -> p m t", m=4),
                  ple(0), True, [io["w_kv"][n] for n in range(2)], 16 * 6)
        k.clear_sems()
        phase_kv_q(k, XT, nxt=[io["phi_w1"][n] for n in range(2)])
        phase_compress(k, nxt=[io["w_o_b"][n] for n in range(2)])
        phase_attend(k)
        phase_out_norm(k, "mixb", k.act(5), io["w_o_b"], [KT], X, row(7, 0), row(7, 1), XT, rows=6)
        phase_route(k, XT)
        k.close_arena()
        phase_experts(k, X)
        k.clear_sems()
        k.open_arena("c")
        XT, acc = k.act(0), k.tok(4)
        phase_collect(k, acc, k.tok(3), nxt=[ple(1)(n) for n in range(2)])
        phase_out_norm(k, "moe", None, None, [], X, row(7, 2), row(7, 3), XT, acc=acc)
        phase_ple(k, "ple1", X, XT, pT(5, 2 * D), row(5, 1), k.region(8, 0, 2048).rearrange("p (m t) -> p m t", m=4),
                  ple(1), False, [], 16 * 9)
        k.close_arena()


def constants():
    c = np.zeros((P, NCONST), np.float32)
    i, j = np.arange(P)[:, None], np.arange(P)[None, :]
    same = i // CH == j // CH
    put = lambda name, a: c.__setitem__((slice(None), slice(CONST[name][0], CONST[name][0] + CONST[name][1])), a)
    put("ident", i == j)
    put("bones", same)
    put("strict", same & (i < j))
    levels = []
    for m in (1, 2, 4, 8, 16, 32):
        levels.append((i // (2 * m) == j // (2 * m)) & (i // m % 2 == 0) & (j // m % 2 == 1))
    put("lev", np.concatenate(levels, 1))
    put("incl", i % CH <= np.arange(CH)[None, :])
    half = DH // 2
    rm = np.zeros((P, P), np.float32)
    for o in range(P):
        b, r = o // DH * DH, o % DH
        rm[b + (r + half) % DH, o] = -1.0 if r < half else 1.0
    put("rmat", rm)
    put("causal", np.where(j <= i, 0.0, NEG))
    put("mhalf", -0.5)
    put("tri", i < j)
    put("ones", 1.0)
    put("iota", np.broadcast_to(np.arange(P, dtype=np.float32), (P, P)))
    put("reset", np.broadcast_to((np.arange(T) % CH != 0).astype(np.float32), (P, T)))
    return c


def tables():
    half = DH // 2
    inv = np.float32(10000.0) ** (-np.arange(half, dtype=np.float32) / np.float32(half))
    ang = np.arange(T, dtype=np.float32)[None, :] * inv[np.arange(P) % half][:, None]
    rot = np.stack([np.cos(ang), np.sin(ang)], 1).astype(np.float32)
    t = (np.arange(MT)[None, :, None] * P + np.arange(P)[:, None, None])
    ok = (np.arange(CMPW) * CMP_STRIDE + CMP_LEN - 1 <= t) & (np.arange(CMPW) < NCMP)
    cmp = np.stack([np.where(ok, 0.0, NEG), ok], 1).astype(np.float32)
    rank = np.broadcast_to((np.arange(NE)[None, :] < np.arange(NE)[:, None]).astype(np.float32).reshape(1, -1), (P, 64))
    return np.ascontiguousarray(np.concatenate([rot.reshape(P, -1), cmp.reshape(P, -1), rank], 1))


def slabs(w, kt, cols):
    w = np.asarray(w)
    return np.ascontiguousarray(w.reshape(kt, P, -1, cols).transpose(2, 1, 0, 3))


def layout(i):
    g = {n: np.asarray(a) for n, a in i.items()}
    feat = lambda v: v.reshape(KT, P).T
    o = {"const": constants(), "tables": tables()}
    mu = g["a_mu"][0]
    o["vec"] = np.ascontiguousarray(np.concatenate(
        [feat(mu[m]) for m in range(6)] + [feat(g[n][0]) for n in
         ("a_w0", "a_a0", "a_k_k", "a_k_a", "a_r_k", "a_gn_g", "a_gn_b")], 1))
    x = g["x"][0]
    o["x"] = x
    o["xT"] = np.ascontiguousarray(x.T.reshape(KT, P, T).transpose(1, 0, 2).reshape(P, -1))
    o["lora_in"] = slabs(np.concatenate([g["a_w1"][0], g["a_a1"][0], g["a_g1"][0]], 1), KT, 256).reshape(P, -1)
    o["lora_out"] = np.ascontiguousarray(np.concatenate([g["a_w2"][0], g["a_a2"][0]], 1))
    o["g2"] = g["a_g2"][0]
    o["w_rkv"] = np.concatenate([slabs(g["a_w_rkv"][0, m], KT, 512) for m in range(3)])
    o["w_o_a"] = slabs(g["a_w_o"][0], KT, 512)
    o["rows"] = np.ascontiguousarray(np.concatenate(
        [np.stack([g["ln_g"][l, j], g["ln_b"][l, j]]) for l in range(DEPTH) for j in range(2)] + [g["ple_gate_b"]]))
    o["pT"] = np.ascontiguousarray(g["p"][:, 0].transpose(0, 2, 1).reshape(DEPTH, 2, P, T).transpose(0, 2, 1, 3)
                                   .reshape(DEPTH, P, 2 * T))
    gu = lambda w, f: np.stack([w[:, :f].reshape(D, f // P, P), w[:, f:].reshape(D, f // P, P)], 2).reshape(D, -1)
    o["w_up"] = slabs(gu(g["f_w_gu"][0], D_FF), KT, 256).reshape(-1, P, UPW)
    o["w_down"] = g["f_w_down"][0].reshape(-1, P, D)
    o["ple_w"] = np.stack([slabs(g["ple_w"][l], 2, 512) for l in range(DEPTH)])
    o["ple_g"] = np.stack([slabs(g["ple_gate_w"][l], KT, 512) for l in range(DEPTH)])
    o["w_kv"] = slabs(g["b_w_kv"], KT, 256)
    order = [(2 * a + e) * NQ + r for a in range(2) for r in range(NQ) for e in range(2)]
    wq = g["b_w_in"][0][:, :D].reshape(D, 2 * KT, DH)[:, order].reshape(D, D)
    o["w_q"] = slabs(wq, KT, 512)
    o["phi_w1"] = slabs(np.concatenate([g["b_phi_w1"][0], g["b_phi_w1"][1]], 1), 16, HID)
    tile = lambda w: w.reshape(-1, P, w.shape[-1]).transpose(1, 0, 2).reshape(P, -1)
    w2 = g["b_phi_w2"]
    o["nsa_small"] = np.ascontiguousarray(np.concatenate(
        [tile(g["b_w_in"][0][:, D:]), tile(np.concatenate([w2[0], w2[0]], 1)), tile(w2[1]),
         g["b_phi_b1"].reshape(4, P).T, g["b_cmp_pos"].reshape(32, P).T, tile(g["m_w_router"][0])], 1))
    o["router_b"] = g["m_b_router"]
    pairs = g["b_w_o"][0].reshape(2, 2, NQ, DH, D).transpose(0, 2, 1, 3, 4).reshape(D, D)
    o["w_o_b"] = slabs(pairs, KT, 512)
    o["m_up"] = np.concatenate([slabs(gu(g["m_w_gu"][0, e], D_FFE), KT, 256) for e in range(NE)]).reshape(-1, P, UPW)
    o["m_down"] = g["m_w_down"][0].reshape(-1, P, D)
    return o


def kernel(**inputs):
    import concourse.bacc as bacc
    from concourse.bass_utils import run_bass_kernel_spmd

    nc = bacc.Bacc("TRN2", target_bir_lowering=False, num_devices=1)
    arrays = layout(inputs)
    io = {n: nc.dram_tensor("in_" + n, a.shape, F32, kind="ExternalInput").ap() for n, a in arrays.items()}
    io["out"] = nc.dram_tensor("out", (1, T, D), F32, kind="ExternalOutput").ap()
    io["rows_y"] = nc.dram_tensor("rows_y", (NBLK * P, D), F32).ap()
    build(nc, io)
    r = run_bass_kernel_spmd(nc, [{"in_" + n: a for n, a in arrays.items()}], core_ids=[0])
    return np.asarray(r.results[0]["out"])
```

```python
import math
from contextlib import ExitStack

import numpy as np
import concourse.bass as bass
from concourse import mybir

F32 = mybir.dt.float32
F32R = mybir.dt.float32r
I32 = mybir.dt.int32
ALU = mybir.AluOpType
ACT = mybir.ActivationFunctionType
AX = mybir.AxisListType
ds = bass.ds

P = 128
T, D = 512, 1024
KT = D // P
MT = T // P
DH = 64
CH = 64
NCH = T // CH
GRP = 4
NG = KT // GRP
LEVELS = 5
D_FF, D_FFE, NE = 2816, 1408, 8
PLE = 256
NBLK = (2 * T + NE * (P - 1)) // P
UPW = KT * 2 * P
NKV = 4
NQ = 4
NH = D // DH
CMP_LEN, CMP_STRIDE = 32, 16
NCMP = (T - CMP_LEN) // CMP_STRIDE + 1
CMPW = 32
HID = 256
DEPTH = 2
ALPHA = (2.0 * DEPTH) ** 0.25
LN_EPS, GN_EPS = 1e-5, 64e-5
EM05 = math.exp(-0.5)
NEG = -1e30
SCALE = DH ** -0.5

SLOT = 11 * 512
TILE = KT * T

CONST = {}
_at = 0
for _n, _w in (("ident", P), ("bones", P), ("strict", P), ("lev", 6 * P), ("incl", CH), ("rmat", P),
               ("causal", P), ("reset", T), ("mhalf", 1), ("tri", P), ("ones", P), ("iota", P), ("ids", MT),
               ("pick", KT * NH), ("spread", KT * P)):
    CONST[_n] = (_at, _w)
    _at += _w
NCONST = _at
VEC = ["mu0", "mu1", "mu2", "mu3", "mu4", "mu5", "w0", "a0", "k_k", "k_a", "r_k", "gn_g", "gn_b"]


class Core:

    def __init__(self, nc, ctx, io):
        self.nc, self.ctx, self.io = nc, ctx, io
        self.xtok = self.sb("xtok", [P, TILE])
        self.const = self.sb("const", [P, NCONST])
        self.vec = self.sb("vec", [P, len(VEC), KT])
        self.small = self.sb("small", [P, 1184])
        self.bank = [ctx.enter_context(nc.psum_tensor(f"bank{i}", [P, 512], F32)) for i in range(8)]
        self.row_index = ctx.enter_context(nc.sbuf_tensor("row_index", [P, 8], I32))
        self.token_ids = ctx.enter_context(nc.sbuf_tensor("token_ids", [P, MT], I32))
        self.slot_token = ctx.enter_context(nc.sbuf_tensor("slot_token", [P, 16], I32))
        self.block_expert = ctx.enter_context(nc.sbuf_tensor("block_expert", [P, 16], I32))
        self.phase_sems = []
        self.slab_ready = [self.kept_sem(f"slab_ready{i}") for i in range(2)]
        self.slabs = 0
        self.scope = None

    def open_arena(self, tag):
        self.scope = ExitStack()
        hold = lambda name, n: self.scope.enter_context(self.nc.sbuf_tensor(name, [P, n], F32))
        self.arena = hold(f"arena_{tag}", 8 * TILE)
        self.slots = [hold(f"slot{i}_{tag}", SLOT) for i in range(2)]

    def close_arena(self):
        self.scope.close()

    def sb(self, name, shape):
        return self.ctx.enter_context(self.nc.sbuf_tensor(name, shape, F32))

    def sem(self, name):
        h = self.nc.alloc_semaphore(name=name)
        self.phase_sems.append(h)
        return h

    def kept_sem(self, name):
        return self.ctx.enter_context(self.nc.semaphore(name))

    def clear_sems(self):
        self.nc.clear_and_free_semaphores(self.phase_sems)
        self.nc.all_engine_barrier()
        self.phase_sems = []

    def c(self, name):
        a, w = CONST[name]
        return self.const[:, a:a + w]

    def v(self, name, f):
        return self.vec[:, VEC.index(name), f:f + 1] if isinstance(f, int) else self.vec[:, VEC.index(name), ds(f, 1)]

    def region(self, i, a=0, n=TILE):
        if i == 1:
            return self.xtok[:, a:a + n]
        i -= i > 1
        return self.arena[:, i * TILE + a:i * TILE + a + n]

    def act(self, i):
        return self.region(i).rearrange("p (k t) -> p k t", k=KT)

    def tok(self, i):
        return self.region(i).rearrange("p (m d) -> p m d", m=MT)

    def slab(self, n, kt, cols):
        return self.slots[n % 2][:, 0:kt * cols].rearrange("p (k c) -> p k c", k=kt)


def load_slab(k, sp, slot, src):
    kt, cols = src.shape[1:]
    dst = k.slots[slot][:, 0:kt * cols].rearrange("p (k c) -> p k c", k=kt)
    sp.dma_start(dst, src).then_inc(k.slab_ready[slot], 16)


def slab_wait(k, pe, n):
    pe.wait_ge(k.slab_ready[n % 2], 16 * (n // 2 + 1))


R_XT, R_MIX, R_R, R_K, R_V, R_A, R_S, R_BON = 0, 1, 3, 4, 5, 6, 7, 8
MIX_ORDER = [3, 4, 5, 0, 1, 2]


def phase_project(k):
    nc, io = k.nc, k.io
    mixbase, mixed = k.sem("mixbase"), k.sem("mixed")
    one_minus = k.sem("one_minus_mu")
    vec_in, lora_in_in, lora_out_in, const_in = (k.sem(n) for n in ("vec_in", "lora_in_in", "lora_out_in", "const_in"))
    xt_in = [k.sem(f"xt_in{i}") for i in range(2)]
    tile_full, tile_free = k.sem("proj_full"), k.sem("proj_free")
    base = k.slabs
    k.slabs += 6
    xT = k.act(R_XT)
    mix = [k.act(R_MIX), k.act(R_MIX + 1)]
    lora_in = k.region(8, 0, 2048).rearrange("p (k c) -> p k c", k=KT)
    lora_out = k.region(8, 2048, 2048)[0:64, :].rearrange("p (i c) -> p i c", i=2)
    omu = k.small[:, 0:48].rearrange("p (m k) -> p m k", m=6)
    lhid = k.small[0:64, 48:560]
    sgate = k.small[:, 560:1072]
    k.sgate = sgate
    out = {3: R_R, 4: R_K, 5: R_V}
    first = [0, 9, 18, 19, 27, 35]

    with nc.Block() as block:
        @block.sync
        def _(sp):
            sp.dma_start(k.vec[:, :, :], io["vec"].rearrange("p (n k) -> p n k", k=KT)).then_inc(vec_in, 16)
            for i in range(2):
                half = slice(i * KT // 2, (i + 1) * KT // 2)
                sp.dma_start(xT[:, half, :], io["xT"].rearrange("p (k t) -> p k t", k=KT)[:, half, :]
                             ).then_inc(xt_in[i], 16)
            sp.dma_start(k.region(8, 0, 2048), io["lora_in"]).then_inc(lora_in_in, 16)
            sp.dma_start(k.region(8, 2048, 2048)[0:64, :], io["lora_out"]).then_inc(lora_out_in, 16)
            for n in range(6):
                if n == 2:
                    sp.dma_start(k.const[:, :], io["const"]).then_inc(const_in, 16)
                if n >= 2:
                    sp.wait_ge(tile_full, 19 + 4 * (n - 1))
                load_slab(k, sp, n % 2, io["w_rkv"][n])
            sp.wait_ge(const_in, 16)

        @block.scalar
        def _(act):
            def mix_base(m):
                if m == 0:
                    act.wait_ge(one_minus, 1)
                if m >= 2:
                    act.wait_ge(tile_full, first[m - 1])
                for f in range(KT):
                    i = MIX_ORDER[m]
                    if m == 0 and f % (KT // 2) == 0:
                        act.wait_ge(xt_in[f // (KT // 2)], 16)
                    act.activation(mix[m % 2][:, f, :], xT[:, f, :], ACT.Copy,
                                   scale=omu[:, i, f:f + 1]).then_inc(mixbase, 1)

            def evacuate(n, dst, func, bias=0.0):
                act.wait_ge(tile_full, n + 1)
                act.activation(dst, k.bank[n % 8][0:dst.shape[0], :], func, bias=bias).then_inc(tile_free, 1)

            mix_base(0)
            mix_base(1)
            evacuate(0, lhid, ACT.Tanh)
            for f in range(KT):
                evacuate(1 + f, k.act(R_S)[:, f, :], ACT.Sigmoid, k.v("w0", f))
            mix_base(2)
            evacuate(9, lhid, ACT.Identity)
            for f in range(KT):
                evacuate(10 + f, k.act(R_A)[:, f, :], ACT.Sigmoid, k.v("a0", f))
            mix_base(3)
            evacuate(18, sgate, ACT.Sigmoid)
            for m in range(3, 6):
                if m < 5:
                    mix_base(m + 1)
                for f in range(KT):
                    evacuate(first[m] + f, k.act(out[m])[:, f, :], ACT.Identity)

        @block.vector
        def _(dve):
            dve.wait_ge(vec_in, 16)
            dve.tensor_scalar(omu, k.vec[:, 0:6, :], -1.0, 1.0, ALU.mult, ALU.add).then_inc(one_minus, 1)
            for m in range(6):
                for f in range(KT):
                    i = MIX_ORDER[m]
                    dve.wait_ge(mixbase, m * KT + f + 1)
                    dst = mix[m % 2][:, f, 1:T]
                    dve.scalar_tensor_tensor(out=dst, in0=xT[:, f, 0:T - 1], scalar=k.v(f"mu{i}", f), in1=dst,
                                             op0=ALU.mult, op1=ALU.add).then_inc(mixed, 1)

        @block.tensor
        def _(pe):
            tile = [0]

            def group(lhs, rhs, ready=None):
                n = tile[0]
                tile[0] += 1
                if n >= 8:
                    pe.wait_ge(tile_free, n - 7)
                for i, (a, b) in enumerate(zip(lhs, rhs)):
                    if ready is not None:
                        pe.wait_ge(mixed, ready + i + 1)
                    last = pe.matmul(k.bank[n % 8][0:a.shape[1], :], a, b, start=i == 0, stop=i == len(lhs) - 1)
                return last

            pe.wait_ge(lora_in_in, 16)
            for m in range(2):
                mx = mix[m]
                group([lora_in[:, kk, 64 * m:64 * m + 64] for kk in range(KT)], [mx[:, kk, :] for kk in range(KT)],
                      ready=m * KT).then_inc(tile_full, 1)
                pe.wait_ge(tile_free, first[m] + 1)
                if m == 0:
                    pe.wait_ge(lora_out_in, 16)
                for f in range(KT):
                    last = group([lora_out[:, m, f * P:(f + 1) * P]], [lhid])
                    last.then_inc(tile_full, 1)
            mx = mix[0]
            group([lora_in[:, kk, 128:256] for kk in range(KT)], [mx[:, kk, :] for kk in range(KT)],
                  ready=2 * KT).then_inc(tile_full, 1)
            for m in range(3, 6):
                for h in range(2):
                    n = 2 * (m - 3) + h
                    slab_wait(k, pe, base + n)
                    w = k.slab(n, KT, 512)
                    for o in range(4):
                        last = group([w[:, kk, o * P:(o + 1) * P] for kk in range(KT)],
                                     [mix[m % 2][:, kk, :] for kk in range(KT)],
                                     ready=m * KT if h == 0 and o == 0 else None)
                        last.then_inc(tile_full, 1)


def phase_scale(k):
    nc = k.nc
    dots, dots_full = k.sem("dots"), k.sem("dots_full")
    head_key, dec_sum, dec, dec_inv, dec_prev = (
        k.sem(n) for n in ("head_key", "dec_sum", "dec", "dec_inv", "dec_prev"))
    chain, ptmp, pool_done, kept = k.sem("scale_chain"), k.sem("scale_ptmp"), k.sem("scale_pool"), k.sem("decay_kept")
    newkey, tile_done = k.sem("newkey"), k.sem("scale_tile")
    Rr, Kk, Vv, Aa, Ss, Bon = (k.act(i) for i in (R_R, R_K, R_V, R_A, R_S, R_BON))
    tmp = [k.slots[j][:, 0:8 * T].rearrange("p (k t) -> p k t", k=8) for j in range(2)]
    norm = k.act(R_MIX)
    squared, summed, clamped, rooted, normed = (
        k.sem("norm_" + n) for n in ("squared", "summed", "clamped", "rooted", "done"))
    inverted, spread = k.sem("norm_inverted"), k.sem("norm_spread")
    by_head = k.region(R_MIX + 1, 0, T)[0:NH, :]
    k.chunk_decay = k.small[:, 0:64].rearrange("p (k c) -> p k c", k=KT)
    omka = k.small[:, 1072:1080]

    with nc.Block() as block:
        @block.scalar
        def _(act):
            for f in range(KT):
                act.activation(norm[:, f, :], Kk[:, f, :], ACT.Square, scale=k.v("k_k", f)).then_inc(squared, 1)
            for f in range(KT):
                if f == 0:
                    act.wait_ge(clamped, 1)
                    act.activation(by_head, by_head, ACT.Sqrt).then_inc(rooted, 1)
                act.wait_ge(spread, f + 1)
                act.activation(norm[:, f, :], k.bank[f][:, :], ACT.Copy).then_inc(normed, 1)
            with act.Fori(0, KT // 2) as half:
                for j in range(2):
                    f, t = 2 * half + j, tmp[j]
                    n = f + 1
                    col = lambda name: k.v(name, f)
                    row = lambda x: x[:, ds(f, 1), :].rearrange("p a t -> p (a t)")
                    act.wait_ge(tile_done, f + 1)
                    act.wait_ge(pool_done, f + 1)
                    act.activation(t[:, 0, :], row(Kk), ACT.Copy, scale=col("k_k")).then_inc(head_key, 1)
                    act.wait_ge(dec_sum, n)
                    act.activation(t[:, 6, :], t[:, 5, :], ACT.Exp, scale=-EM05).then_inc(dec, 1)
                    act.activation(t[:, 7, :], t[:, 5, :], ACT.Exp, scale=EM05).then_inc(dec_inv, 1)
                    act.wait_ge(dec, n)
                    act.activation(k.chunk_decay[:, ds(f, 1), :].rearrange("p a c -> p (a c)"),
                                   t[:, 6, CH - 1:T:CH], ACT.Copy).then_inc(kept, 1)
                    act.wait_ge(ptmp, 3 * f + 1)
                    act.activation(t[:, 2, :], t[:, 2, :], ACT.Exp, scale=-EM05).then_inc(dec_prev, 1)

        @block.tensor
        def _(pe):
            for f in range(KT):
                pe.wait_ge(squared, f + 1)
                last = pe.matmul(k.bank[0][0:NH, :], k.c("pick")[:, f * NH:(f + 1) * NH], norm[:, f, :], start=f == 0,
                                 stop=f == KT - 1)
            last.then_inc(summed, 1)
            pe.wait_ge(inverted, 1)
            for f in range(KT):
                pe.matmul(k.bank[f][:, :], k.c("spread")[0:NH, f * P:(f + 1) * P], by_head, start=True,
                          stop=True).then_inc(spread, 1)
            pe.wait_ge(normed, KT)
            with pe.Fori(0, KT // 2) as half:
                for j in range(2):
                    f, t = 2 * half + j, tmp[j]
                    pe.wait_ge(dots, f + 1)
                    pe.wait_ge(tile_done, f + 1)
                    pe.matmul(k.bank[2 * j + 1][:, :], k.c("bones"), t[:, 4, :], start=True,
                              stop=True).then_inc(dots_full, 1)

        @block.vector
        def _(dve):
            dve.tensor_scalar(omka, k.vec[:, VEC.index("k_a"), :], -1.0, 1.0, ALU.mult, ALU.add).then_inc(chain, 1)
            dve.wait_ge(chain, 1)
            dve.wait_ge(summed, 1)
            dve.tensor_scalar(by_head, k.bank[0][0:NH, :], 1e-24, None, ALU.max).then_inc(clamped, 1)
            dve.wait_ge(rooted, 1)
            dve.reciprocal(by_head, by_head).then_inc(inverted, 1)
            dve.sem_inc(tile_done, 2)
            with dve.Fori(0, KT // 2) as half:
                for j in range(2):
                    f, t = 2 * half + j, tmp[j]
                    n = f + 1
                    col = lambda name: k.v(name, f)
                    row = lambda x: x[:, ds(f, 1), :].rearrange("p a t -> p (a t)")
                    dve.wait_ge(pool_done, f + 1)
                    dve.tensor_tensor_scan(t[:, 5, :], k.c("reset"), row(Ss), 0.0, ALU.mult,
                                           ALU.add).then_inc(dec_sum, 1)
                    dve.tensor_scalar(t[:, 3, :], row(Aa), col("k_a"), omka[:, ds(f, 1)], ALU.mult,
                                      ALU.add).then_inc(chain, 1)
                    dve.wait_ge(chain, 2 * f + 2)
                    dve.tensor_tensor(t[:, 3, :], t[:, 3, :], row(Kk), ALU.mult).then_inc(newkey, 1)
                    dve.wait_ge(newkey, n)
                    dve.scalar_tensor_tensor(out=t[:, 4, :], in0=row(Rr), scalar=col("r_k"), in1=t[:, 3, :],
                                             op0=ALU.mult, op1=ALU.mult).then_inc(dots, 1)
                    dve.wait_ge(head_key, n)
                    dve.wait_ge(normed, n)
                    dve.tensor_tensor(t[:, 0, :], t[:, 0, :], row(norm), ALU.mult).then_inc(chain, 1)
                    dve.wait_ge(dots_full, n)
                    dve.tensor_tensor(row(Bon), k.bank[2 * j + 1][:, :], row(Vv), ALU.mult)
                    dve.wait_ge(dec, n)
                    dve.tensor_tensor(row(Rr), row(Rr), t[:, 6, :], ALU.mult)
                    dve.wait_ge(dec_prev, n)
                    dve.wait_ge(kept, n)
                    dve.wait_ge(chain, 2 * f + 3)
                    dve.tensor_tensor(row(Ss), t[:, 0, :], t[:, 2, :], ALU.mult).then_inc(tile_done, 1)

        @block.gpsimd
        def _(pool):
            pool.sem_inc(pool_done, 2)
            with pool.Fori(0, KT // 2) as half:
                for j in range(2):
                    f, t = 2 * half + j, tmp[j]
                    n = f + 1
                    row = lambda x: x[:, ds(f, 1), :].rearrange("p a t -> p (a t)")
                    pool.wait_ge(dec_sum, n)
                    pool.wait_ge(tile_done, f + 1)
                    pool.nop(nofuse=True)
                    pool.tensor_tensor(t[:, 2, :], t[:, 5, :], row(Ss), ALU.subtract).then_inc(ptmp, 1)
                    pool.wait_ge(dec_inv, n)
                    pool.wait_ge(newkey, n)
                    pool.wait_ge(dots, n)
                    pool.nop(nofuse=True)
                    pool.tensor_tensor(row(Kk), t[:, 3, :], t[:, 7, :], ALU.mult).then_inc(ptmp, 1)
                    pool.wait_ge(chain, 2 * f + 3)
                    pool.nop(nofuse=True)
                    pool.tensor_tensor(t[:, 1, :], t[:, 0, :], row(Aa), ALU.mult).then_inc(ptmp, 1)
                    pool.wait_ge(ptmp, 3 * f + 3)
                    pool.nop(nofuse=True)
                    pool.tensor_tensor(row(Aa), t[:, 1, :], t[:, 7, :], ALU.mult).then_inc(pool_done, 1)


def phase_recurrence(k):
    nc = k.nc
    S = {n: k.sem("rec_" + n) for n in (
        "ab", "ak", "rm", "tb", "tk", "tv", "ty", "yt", "p", "xp", "py", "w", "u", "o", "ds",
        "built_dve", "built_pool", "nmask", "kmask", "rmask", "btok", "ktok", "vtok", "levels", "first", "y1", "x1",
        "p_sb", "x", "y", "w_sb", "u_sb", "out", "sum", "state", "zero", "zero_state")}
    rho, kap, vv, bet, alp, out = (k.act(i) for i in (R_R, R_K, R_V, R_A, R_S, R_XT))
    W = GRP * P

    def take(pool=[k.region(1), 0, k.region(2), 0, k.slots[0][:, :], 0, k.slots[1][:, :], 0]):
        for i in range(0, len(pool), 2):
            if pool[i + 1] + W <= pool[i].shape[1]:
                a = pool[i + 1]
                pool[i + 1] += W
                return pool[i][:, a:a + W].rearrange("p (q c) -> p q c", q=GRP)
        raise MemoryError("recurrence")

    names = ["bdA", "bdB", "bdK", "bdV", "N", "AK", "RM", "btok", "ktok", "vtok", "X", "Y", "Pm", "ST"]
    B = [{n: take() for n in names + [f"lev{i + 1}" for i in range(LEVELS)]} for g in range(NG)]
    for s in B:
        s["Wm"], s["U"] = s["Pm"], s["X"]
    bk = [[k.bank[4 * g + i][:, :].rearrange("p (q c) -> p q c", q=GRP) for i in range(4)] for g in range(NG)]
    ident = k.c("ident")
    over = lambda m: m.rearrange("p (q c) -> p q c", q=1).to_broadcast([P, GRP, m.shape[1]])
    strict = over(k.c("strict"))
    levm = k.c("lev").rearrange("p (l c) -> p l c", l=6)
    lev = [over(levm[:, l, :]) for l in range(6)]
    incl = k.c("incl").rearrange("p (q c) -> p q c", q=1).to_broadcast([P, 2 * GRP, CH])
    idn = over(ident)
    both = (0, 1)

    with nc.Block() as block:
        @block.sync
        def _(sp):
            for each in S.values():
                sp.sem_inc(each, 1)

        @block.tensor
        def _(pe):
            def four(bank, lhs, rhs, sem, width=P, add=None):
                for q in range(GRP):
                    terms = [(lhs, rhs)] + (add or [])
                    for i, (a, b) in enumerate(terms):
                        last = pe.matmul(bank[:, q, 0:width] if width == P else bank[:, q, :], a(q), b(q),
                                         start=i == 0, stop=i == len(terms) - 1)
                last.then_inc(sem, 1)

            def turn(bank, src, sem):
                for q in range(GRP):
                    last = pe.transpose(bank[:, q, :], src[:, q, :], ident)
                last.then_inc(sem, 1)

            with pe.Fori(0, NCH) as c:
                for g in both:
                    n, s = 2 * c + g + 1, B[g]
                    rc = lambda q, g=g: rho[:, GRP * g + q, ds(c * CH, CH)]
                    pe.wait_ge(S["built_dve"], 8 * c + 4 * g + 4 + 1)
                    pe.wait_ge(S["out"], 2 * c + 1)
                    four(bk[g][0], lambda q: s["bdB"][:, q, :], lambda q: s["bdA"][:, q, :], S["ab"])
                    pe.wait_ge(S["built_pool"], 8 * c + 4 * g + 4 + 1)
                    pe.wait_ge(S["sum"], 2 * c + 1)
                    four(bk[g][1], lambda q: s["bdK"][:, q, :], lambda q: s["bdA"][:, q, :], S["ak"])
                    pe.wait_ge(S["w_sb"], 2 * c + 1)
                    rm = k.bank[4 * g + 2][:, :].rearrange("p (q c) -> p q c", c=CH)
                    for i, b in enumerate(("bdB", "bdK")):
                        for q in range(GRP):
                            last = pe.matmul(rm[:, GRP * i + q, :], s[b][:, q, :], rc(q), start=True, stop=True)
                    last.then_inc(S["rm"], 1)
                for g in both:
                    n, s = 2 * c + g + 1, B[g]
                    pe.wait_ge(S["u_sb"], 2 * c + 1)
                    turn(bk[g][3], s["bdB"], S["tb"])
                    pe.wait_ge(S["nmask"], n + 1)
                    turn(bk[g][0], s["bdK"], S["tk"])
                    pe.wait_ge(S["kmask"], n + 1)
                    turn(bk[g][1], s["bdV"], S["tv"])
                for g in both:
                    n, s = 2 * c + g + 1, B[g]
                    pe.wait_ge(S["y1"], n + 1)
                    pe.wait_ge(S["rmask"], n + 1)
                    turn(bk[g][2], s["Y"], S["ty"])
                for l in range(LEVELS):
                    for g in both:
                        s = B[g]
                        m = 2 * c + g + 1
                        if l == 0:
                            pe.wait_ge(S["x1"], m + 1)
                            pe.wait_ge(S["btok"], m + 1)
                        else:
                            pe.wait_ge(S["x"], 8 * c + 2 * (l - 1) + g + 1 + 1)
                        pe.wait_ge(S["levels"], 10 * c + 5 * g + l + 1 + 1)
                        four(bk[g][3], lambda q: s[f"lev{l + 1}"][:, q, :], lambda q: s["X"][:, q, :], S["p"])
                        if l > 0:
                            turn(bk[g][1], B[g]["X"], S["yt"])
                    for g in both:
                        s = B[g]
                        m = 2 * c + g + 1
                        pe.wait_ge(S["p_sb"], 10 * c + 2 * l + g + 1 + 1)
                        if l == 0:
                            pe.wait_ge(S["ktok"], m + 1)
                            pe.wait_ge(S["vtok"], m + 1)
                        else:
                            pe.wait_ge(S["y"], 10 * c + 2 * (l - 1) + g + 1 + 1)
                        if l < LEVELS - 1:
                            four(bk[g][0], lambda q: s["Y"][:, q, :], lambda q: s["Pm"][:, q, :], S["xp"])
                        else:
                            four(bk[g][1], lambda q: s["Pm"][:, q, :], lambda q: s["Y"][:, q, :], S["py"])
                for g in both:
                    n, s = 2 * c + g + 1, B[g]
                    pe.wait_ge(S["zero_state"], 2 + 1)
                    pe.wait_ge(S["state"], 2 * c + 1)
                    four(bk[g][2], lambda q: s["bdA"][:, q, :], lambda q: s["ST"][:, q, :], S["w"],
                         add=[(lambda q: s["AK"][:, q, :], lambda q: s["vtok"][:, q, :])])
                for g in both:
                    n, s = 2 * c + g + 1, B[g]
                    pe.wait_ge(S["w_sb"], n + 1)
                    pe.wait_ge(S["y"], 10 * c + 2 * (LEVELS - 1) + g + 1 + 1)
                    four(bk[g][3], lambda q: s["Y"][:, q, :], lambda q: s["Wm"][:, q, :], S["u"])
                for g in both:
                    n, s = 2 * c + g + 1, B[g]
                    rc = lambda q, g=g: rho[:, GRP * g + q, ds(c * CH, CH)]
                    rmv = s["RM"].rearrange("p q c -> p (q c)").rearrange("p (r c) -> p r c", c=CH)
                    ob = k.bank[4 * g][:, 0:GRP * CH].rearrange("p (q c) -> p q c", c=CH)
                    pe.wait_ge(S["u_sb"], n + 1)
                    four(ob, lambda q: s["ST"][:, q, :], rc, S["o"], width=CH,
                         add=[(lambda q: s["U"][:, q, :], lambda q: rmv[:, q, :]),
                              (lambda q: s["vtok"][:, q, :], lambda q: rmv[:, GRP + q, :])])
                    four(bk[g][1], lambda q: s["btok"][:, q, :], lambda q: s["U"][:, q, :], S["ds"],
                         add=[(lambda q: s["ktok"][:, q, :], lambda q: s["vtok"][:, q, :])])

        def spread(eng, dst, src, g, c, sem):
            for h in range(2):
                op = eng.tensor_copy(dst[64 * h:64 * h + 64, :, 64 * h:64 * h + 64],
                                     src[64 * h:64 * h + 64, GRP * g:GRP * g + GRP, ds(c * CH, CH)]).then_inc(sem, 1)

        @block.vector
        def _(dve):
            for g in both:
                for b in ("bdA", "bdB"):
                    op = dve.memset(B[g][b], 0.0)
                op.then_inc(S["zero"], 1)
            for g in both:
                dve.memset(B[g]["ST"], 0.0).then_inc(S["zero_state"], 1)
            dve.wait_ge(S["zero"], 4 + 1)
            dve.wait_ge(S["zero_state"], 2 + 1)

            def build(c):
                for g in both:
                    dve.wait_ge(S["w"], 2 * c + 1)
                    spread(dve, B[g]["bdB"], bet, g, c, S["built_dve"])
                    spread(dve, B[g]["bdA"], alp, g, c, S["built_dve"])

            def chunk(c, more):
                for g in both:
                    n, s = 2 * c + g + 1, B[g]
                    dve.wait_ge(S["ab"], n + 1)
                    dve.wait_ge(S["levels"], 10 * c + 1)
                    dve.tensor_tensor(s["N"], bk[g][0], strict, ALU.mult).then_inc(S["nmask"], 1)
                    dve.wait_ge(S["nmask"], n + 1)
                    dve.wait_ge(S["u"], 2 * c + 1)
                    dve.tensor_tensor(s["Y"], s["N"], lev[0], ALU.mult).then_inc(S["first"], 1)
                    dve.wait_ge(S["first"], n + 1)
                    dve.tensor_tensor(s["Y"], idn, s["Y"], ALU.subtract).then_inc(S["y1"], 1)
                    dve.wait_ge(S["ak"], n + 1)
                    dve.tensor_tensor(s["AK"], bk[g][1], strict, ALU.mult).then_inc(S["kmask"], 1)
                    dve.wait_ge(S["rm"], n + 1)
                    dve.wait_ge(S["o"], 2 * c + 1)
                    flat = lambda x: x.rearrange("p q c -> p (q c)").rearrange("p (r c) -> p r c", c=CH)
                    dve.tensor_tensor(flat(s["RM"]), flat(bk[g][2]), incl, ALU.mult).then_inc(S["rmask"], 1)
                for l in range(LEVELS):
                    if l > 0:
                        for g in both:
                            dve.wait_ge(S["yt"], 8 * c + 2 * (l - 1) + g + 1 + 1)
                            dve.tensor_copy(B[g]["Y"], bk[g][1]).then_inc(S["y"], 1)
                    for g in both:
                        s = B[g]
                        if l < LEVELS - 1:
                            dve.wait_ge(S["xp"], 8 * c + 2 * l + g + 1 + 1)
                            if l == 0:
                                dve.wait_ge(S["x1"], 2 * c + g + 1 + 1)
                            else:
                                dve.wait_ge(S["x"], 8 * c + 2 * (l - 1) + g + 1 + 1)
                            dve.tensor_tensor(s["X"], s["X"], bk[g][0], ALU.subtract).then_inc(S["x"], 1)
                        else:
                            dve.wait_ge(S["py"], 2 * c + g + 1 + 1)
                            dve.wait_ge(S["y"], 10 * c + 2 * (l - 1) + g + 1 + 1)
                            dve.tensor_tensor(s["Y"], s["Y"], bk[g][1], ALU.subtract).then_inc(S["y"], 1)
                if more:
                    build(c + 1)
                for g in both:
                    n, s = 2 * c + g + 1, B[g]
                    dve.wait_ge(S["ds"], n + 1)
                    dve.wait_ge(S["state"], 2 * c + 1)
                    dve.tensor_tensor(s["ST"], s["ST"], bk[g][1], ALU.add).then_inc(S["sum"], 1)
                    dve.wait_ge(S["sum"], n + 1)
                    dk = k.chunk_decay[:, GRP * g:GRP * g + GRP, ds(c, 1)].to_broadcast([P, GRP, P])
                    dve.tensor_tensor(s["ST"], s["ST"], dk, ALU.mult).then_inc(S["state"], 1)

            build(0)
            with dve.Fori(0, NCH - 1) as c:
                chunk(c, True)
            chunk(NCH - 1, False)

        @block.gpsimd
        def _(pool):
            for g in both:
                for b in ("bdK", "bdV"):
                    op = pool.memset(B[g][b], 0.0)
                op.then_inc(S["zero"], 1)
            pool.wait_ge(S["zero"], 4 + 1)
            with pool.Fori(0, NCH) as c:
                for g in both:
                    pool.wait_ge(S["w"], 2 * c + 1)
                    pool.nop(nofuse=True)
                    spread(pool, B[g]["bdV"], vv, g, c, S["built_pool"])
                    spread(pool, B[g]["bdK"], kap, g, c, S["built_pool"])
                    pool.wait_ge(S["built_pool"], 8 * c + 4 * g + 4 + 1)
                for g in both:
                    pool.wait_ge(S["nmask"], 2 * c + g + 1 + 1)
                    for l in range(LEVELS):
                        if l == 0:
                            pool.wait_ge(S["p"], 10 * c + 1)
                        else:
                            pool.wait_ge(S["levels"], 10 * c + 5 * g + l + 1)
                        pool.tensor_tensor(B[g][f"lev{l + 1}"], B[g]["N"], lev[l + 1], ALU.mult).then_inc(S["levels"], 1)

        @block.scalar
        def _(act):
            def take_out(dst, src, sem, scale=1.0):
                act.activation(dst, src, ACT.Copy, scale=scale).then_inc(sem, 1)

            with act.Fori(0, NCH) as c:
                for g in both:
                    n, s = 2 * c + g + 1, B[g]
                    act.wait_ge(S["tb"], n + 1)
                    act.wait_ge(S["ds"], 2 * c + 1)
                    take_out(s["btok"], bk[g][3], S["btok"])
                    act.wait_ge(S["tk"], n + 1)
                    take_out(s["ktok"], bk[g][0], S["ktok"])
                    act.wait_ge(S["tv"], n + 1)
                    take_out(s["vtok"], bk[g][1], S["vtok"])
                for g in both:
                    act.wait_ge(S["ty"], 2 * c + g + 1 + 1)
                    take_out(B[g]["X"], bk[g][2], S["x1"])
                for l in range(LEVELS):
                    for g in both:
                        act.wait_ge(S["p"], 10 * c + 2 * l + g + 1 + 1)
                        take_out(B[g]["Pm"], bk[g][3], S["p_sb"])
                for g in both:
                    act.wait_ge(S["w"], 2 * c + g + 1 + 1)
                    take_out(B[g]["Wm"], bk[g][2], S["w_sb"])
                for g in both:
                    act.wait_ge(S["u"], 2 * c + g + 1 + 1)
                    take_out(B[g]["U"], bk[g][3], S["u_sb"], scale=-1.0)
                for g in both:
                    act.wait_ge(S["o"], 2 * c + g + 1 + 1)
                    ob = k.bank[4 * g][:, 0:GRP * CH].rearrange("p (q c) -> p q c", c=CH)
                    take_out(out[:, GRP * g:GRP * g + GRP, ds(c * CH, CH)], ob, S["out"])


def phase_gate(k):
    nc, io = k.nc, k.io
    s = {n: k.sem("gn_" + n) for n in ("mean", "var", "gate", "centred", "squared", "root", "inverted", "spread",
                                       "chain", "done")}
    g2_ready, eps_set = k.sem("g2_ready"), k.sem("eps_set")
    o, y, bon = k.act(R_XT), k.act(3), k.act(R_BON)
    tmp = [k.region(2, j * 2048, 2048).rearrange("p (k t) -> p k t", k=4) for j in range(2)]
    g2 = k.region(5, 0, D)
    by_head = tmp[0][0:NH, 2, :]
    eps = k.small[:, 1080:1081]
    k.rows = k.kept_sem("rows_ready")
    with nc.Block() as block:
        @block.sync
        def _(sp):
            sp.dma_start(g2, io["g2"]).then_inc(g2_ready, 16)
            for n in range(2):
                load_slab(k, sp, n, io["w_o_a"][n])
            sp.dma_start(k.tok(1), io["x"].rearrange("(m p) d -> p m d", p=P)).then_inc(k.rows, 16)
            rows = io["rows"].rearrange("(o r) d -> o (r d)", o=1)
            sp.dma_start(k.region(6, 0, 2 * D), rows[:, 0:2 * D].to_broadcast([P, 2 * D])).then_inc(k.rows, 16)

        @block.tensor
        def _(pe):
            def mean(f):
                if f >= 2:
                    pe.wait_ge(s["centred"], f - 1)
                pe.matmul(k.bank[f % 2][:, :], k.c("bones"), o[:, f, :], start=True, stop=True).then_inc(s["mean"], 1)

            def gate(f):
                if f >= 2:
                    pe.wait_ge(s["done"], f - 1)
                pe.matmul(k.bank[3 + f % 2][:, :], g2[:, f * P:(f + 1) * P], k.sgate, start=True,
                          stop=True).then_inc(s["gate"], 1)

            mean(0)
            for f in range(KT):
                if f + 1 < KT:
                    mean(f + 1)
                pe.wait_ge(s["squared"], f + 1)
                pe.matmul(k.bank[2][0:NH, :], k.c("pick")[:, f * NH:(f + 1) * NH], tmp[f % 2][:, 1, :], start=f == 0,
                          stop=f == KT - 1).then_inc(s["var"], 1)
            pe.wait_ge(g2_ready, 16)
            gate(0)
            gate(1)
            pe.wait_ge(s["inverted"], 1)
            for f in range(KT):
                if f >= 2:
                    gate(f)
                pe.matmul(k.bank[5 + f % 2][:, :], k.c("spread")[0:NH, f * P:(f + 1) * P], by_head, start=True,
                          stop=True).then_inc(s["spread"], 1)

        @block.scalar
        def _(act):
            act.wait_ge(eps_set, 1)
            for f in range(KT):
                act.wait_ge(s["centred"], f + 1)
                if f >= 2:
                    act.wait_ge(s["var"], f - 1)
                act.activation(tmp[f % 2][:, 1, :], y[:, f, :], ACT.Square).then_inc(s["squared"], 1)
            act.wait_ge(s["var"], KT)
            act.activation(by_head, k.bank[2][0:NH, :], ACT.Sqrt, bias=eps[0:NH, :],
                           scale=1.0 / DH).then_inc(s["root"], 1)

        @block.vector
        def _(dve):
            dve.memset(eps, GN_EPS).then_inc(eps_set, 1)
            for f in range(KT):
                dve.wait_ge(s["mean"], f + 1)
                dve.scalar_tensor_tensor(out=y[:, f, :], in0=k.bank[f % 2][:, :], scalar=-1.0 / DH, in1=o[:, f, :],
                                         op0=ALU.mult, op1=ALU.add).then_inc(s["centred"], 1)
            dve.wait_ge(s["root"], 1)
            dve.reciprocal(by_head, by_head).then_inc(s["inverted"], 1)
            for f in range(KT):
                t = tmp[f % 2][:, 0, :]
                dve.wait_ge(s["spread"], f + 1)
                dve.tensor_tensor(t, y[:, f, :], k.bank[5 + f % 2][:, :], ALU.mult).then_inc(s["chain"], 1)
                dve.wait_ge(s["chain"], 3 * f + 1)
                dve.tensor_scalar(t, t, k.v("gn_g", f), k.v("gn_b", f), ALU.mult, ALU.add).then_inc(s["chain"], 1)
                dve.wait_ge(s["chain"], 3 * f + 2)
                dve.tensor_tensor(t, t, bon[:, f, :], ALU.add).then_inc(s["chain"], 1)
                dve.wait_ge(s["chain"], 3 * f + 3)
                dve.wait_ge(s["gate"], f + 1)
                dve.tensor_tensor(y[:, f, :], t, k.bank[3 + f % 2][:, :], ALU.mult).then_inc(s["done"], 1)


def phase_out_norm(k, tag, lhs, weights, kts, X, gain, shift, XT=None, nxt=(), rows=0, load=None, before=None):
    nc = k.nc
    s = {n: k.sem(f"{tag}_{n}") for n in ("full", "added", "stats", "mv", "rstd", "normed", "shifted",
                                          "turned", "copied", "eps")}
    base = k.slabs
    parts = len(kts)
    if weights is not None:
        k.slabs += 2 * parts
    stat = k.small[:, 1082:1082 + 12]
    mv = k.small[:, 1094:1094 + 8].rearrange("p (m c) -> p m c", m=MT)
    rstd = k.small[:, 1102:1106]
    srcs = list(nxt)

    with nc.Block() as block:
        @block.sync
        def _(sp):
            if weights is not None:
                for n in range(2, 2 * parts):
                    sp.wait_ge(s["full"], MT * (n - 1))
                    load_slab(k, sp, n % 2, weights[n])
            if load is not None:
                load(sp)
            for n, src in enumerate(srcs):
                if weights is not None:
                    sp.wait_ge(s["full"], MT * (2 * parts - 1 + n))
                load_slab(k, sp, n, src)

        @block.tensor
        def _(pe):
            n = 0
            if weights is not None:
                for h in range(2):
                    k0 = 0
                    for part, kt in enumerate(kts):
                        slab_wait(k, pe, base + n)
                        w = k.slab(n, kt, 512)
                        for m in range(MT):
                            for kk in range(kt):
                                last = pe.matmul(k.bank[4 * h + m][:, :], lhs[:, k0 + kk, m * P:(m + 1) * P],
                                                 w[:, kk, :], start=k0 + kk == 0,
                                                 stop=part == parts - 1 and kk == kt - 1)
                            last.then_inc(s["full"], 1)
                        k0 += kt
                        n += 1
            if before is not None:
                before(pe)
            if XT is not None:
                for m in range(MT):
                    pe.wait_ge(s["shifted"], m + 1)
                    if m >= 2:
                        pe.wait_ge(s["copied"], 2 * (m - 1))
                    for b in range(2):
                        bank = k.bank[2 * (m % 2) + b]
                        for q in range(4):
                            last = pe.transpose(bank[:, q * P:(q + 1) * P], X[:, m, (4 * b + q) * P:(4 * b + q + 1) * P],
                                                k.c("ident"))
                        last.then_inc(s["turned"], 1)

        @block.vector
        def _(dve):
            if gain is None:
                return
            dve.memset(k.small[:, 1106:1107], LN_EPS).then_inc(s["eps"], 1)
            if rows:
                dve.wait_ge(k.rows, 16 * rows)
            for h in range(2):
                for m in range(MT):
                    row = X[:, m, h * 512:(h + 1) * 512]
                    if weights is not None:
                        dve.wait_ge(s["full"], MT * (parts * (h + 1) - 1) + m + 1)
                        src = k.bank[4 * h + m][:, :]
                        dve.scalar_tensor_tensor(out=row, in0=row, scalar=ALPHA, in1=src, op0=ALU.mult,
                                                 op1=ALU.add).then_inc(s["added"], 1)
                    if h == 0:
                        continue
                    if weights is not None:
                        dve.wait_ge(s["added"], 5 + m)
                    if m:
                        dve.wait_ge(s["mv"], m)
                    for q in range(2):
                        dve.bn_stats(stat[:, 6 * q:6 * q + 6], X[:, m, q * 512:(q + 1) * 512]).then_inc(s["stats"], 1)
                    dve.wait_ge(s["stats"], 2 * m + 2)
                    dve.bn_aggr(mv[:, m, :], stat).then_inc(s["mv"], 1)
                    dve.wait_ge(s["mv"], m + 1)
                    dve.scalar_tensor_tensor(out=X[:, m, :], in0=X[:, m, :], scalar=mv[:, m, 0:1], in1=gain,
                                             op0=ALU.subtract, op1=ALU.mult).then_inc(s["normed"], 1)
                    dve.wait_ge(s["normed"], m + 1)
                    dve.wait_ge(s["rstd"], 2 * m + 2)
                    dve.scalar_tensor_tensor(out=X[:, m, :], in0=X[:, m, :], scalar=rstd[:, m:m + 1], in1=shift,
                                             op0=ALU.mult, op1=ALU.add).then_inc(s["shifted"], 1)

        @block.gpsimd
        def _(pool):
            if gain is None:
                return
            for m in range(MT):
                pool.wait_ge(s["mv"], m + 1)
                pool.tensor_scalar(rstd[:, m:m + 1], mv[:, m, 1:2], LN_EPS, None, ALU.add).then_inc(s["rstd"], 1)
                pool.wait_ge(s["rstd"], 2 * m + 1)
                pool.tensor_tensor(rstd[:, m:m + 1], rstd[:, m:m + 1], k.c("mhalf"), ALU.pow).then_inc(s["rstd"], 1)

        @block.scalar
        def _(act):
            if XT is not None:
                for m in range(MT):
                    for b in range(2):
                        act.wait_ge(s["turned"], 2 * m + b + 1)
                        act.activation(XT[:, 4 * b:4 * b + 4, m * P:(m + 1) * P],
                                       k.bank[2 * (m % 2) + b][:, :].rearrange("p (q t) -> p q t", q=4),
                                       ACT.Copy).then_inc(s["copied"], 1)


def phase_ffn(k, X):
    nc, io = k.nc, k.io
    n_f = D_FF // P
    n_up = 2 * n_f
    A = 3
    s = {n: k.sem("ffn_" + n) for n in ("hi", "lo", "used", "sig", "part", "h", "hh", "hl")}
    turned, x_hi, x_lo, full, added = (k.sem("ffn_" + n) for n in ("turned", "x_hi", "x_lo", "full", "added"))
    raw_in = [k.sem(f"ffn_raw{i}") for i in range(2)]
    scope = ExitStack()
    hold = lambda name, n, dt=F32: scope.enter_context(nc.sbuf_tensor("ffn_" + name, [P, n], dt))
    f32 = lambda ap: ap.bitcast(F32)
    xh, xl = (hold(n, KT * T, F32R)[:, :].rearrange("p (k t) -> p k t", k=KT) for n in ("xh", "xl"))
    hh, hl = (hold(n, n_f * T, F32R)[:, :].rearrange("p (f t) -> p f t", f=n_f) for n in ("hh", "hl"))
    raw = [hold(f"raw{i}", D) for i in range(2)]
    hi, lo = ([hold(f"{p}{i}", D, F32R) for i in range(2)] for p in ("hi", "lo"))
    sg, ht = ([hold(f"{n}{i}", T) for i in range(2)] for n in ("sg", "ht"))
    flat = lambda x, f: x[:, ds(f, 1), :].rearrange("p a t -> p (a t)")

    with nc.Block() as block:
        @block.sync
        def _(sp):
            for each in s.values():
                sp.sem_inc(each, A)

            def load(n, j, src):
                sp.wait_ge(s["lo"], n - 1 + A)
                sp.dma_start(raw[j][:, :], src).then_inc(raw_in[j], 16)

            up = lambda f, half: io["w_up"][ds(f, 1), :, half * D:(half + 1) * D].rearrange("a p c -> (a p) c")
            with sp.Fori(0, n_f) as f:
                for j in range(2):
                    load(2 * f + j, j, up(f, j))
            with sp.Fori(0, n_f // 2) as i:
                for j in range(2):
                    load(n_up + 2 * i + j, j, io["w_down"][ds(2 * i + j, 1)].rearrange("a p c -> (a p) c"))

        @block.tensor
        def _(pe):
            for m in range(MT):
                for b in range(2):
                    bank = k.bank[2 * (m % 4) + b]
                    for q in range(4):
                        last = pe.transpose(bank[:, q * P:(q + 1) * P], X[:, m, (4 * b + q) * P:(4 * b + q + 1) * P],
                                            k.c("ident"))
                    last.then_inc(turned, 1)
            pe.wait_ge(x_lo, 2 * MT)
            with pe.Fori(0, n_f // 2) as i:
                for j in range(2):
                    f = 2 * i + j
                    pe.wait_ge(s["h"], f - 1 + A)
                    for half in range(2):
                        pe.wait_ge(s["lo"], 2 * f + half + 1 + A)
                        for u in range(2):
                            bank = k.bank[2 * j + u][:, :]
                            for q in range(KT // 2):
                                kk = half * KT // 2 + q
                                w = slice(q * 2 * P + u * P, q * 2 * P + (u + 1) * P)
                                pe.matmul(bank, hi[half][:, w], xh[:, kk, :], start=kk == 0, stop=False)
                                pe.matmul(bank, lo[half][:, w], xh[:, kk, :], start=False, stop=False)
                                last = pe.matmul(bank, hi[half][:, w], xl[:, kk, :], start=False, stop=kk == KT - 1)
                        last.then_inc(s["used"], 1)
            for f in range(n_f):
                j = f % 2
                pe.wait_ge(s["lo"], n_up + f + 1 + A)
                pe.wait_ge(s["hl"], f + 1 + A)
                for half in (1, 0):
                    if f == 0 and half == 0:
                        pe.wait_ge(s["h"], n_f + A)
                    for m in range(MT):
                        bank = k.bank[4 * half + m][:, :]
                        rows, cols = slice(m * P, (m + 1) * P), slice(half * 512, half * 512 + 512)
                        pe.matmul(bank, hh[:, f, rows], hi[j][:, cols], start=f == 0, stop=False)
                        pe.matmul(bank, hh[:, f, rows], lo[j][:, cols], start=False, stop=False)
                        last = pe.matmul(bank, hl[:, f, rows], hi[j][:, cols], start=False, stop=f == n_f - 1)
                        if f == n_f - 1 and (half, m) != (0, MT - 1):
                            last.then_inc(full, 1)
                last.then_inc(s["used"], 1)

        @block.scalar
        def _(act):
            def split(turn, j, n):
                act.wait_ge(raw_in[j], 16 * turn + 16)
                act.wait_ge(s["used"], n - 1 + A)
                act.activation(hi[j][:, :], raw[j][:, :], ACT.Copy).then_inc(s["hi"], 1)

            def hidden_hi(f, j):
                act.wait_ge(s["h"], f + 1 + A)
                act.activation(flat(hh, f), ht[j][:, :], ACT.Copy).then_inc(s["hh"], 1)

            for n in range(2 * MT):
                m, b = n // 2, n % 2
                act.wait_ge(turned, n + 1)
                act.activation(xh[:, 4 * b:4 * b + 4, m * P:(m + 1) * P],
                               k.bank[n][:, :].rearrange("p (q t) -> p q t", q=4), ACT.Copy).then_inc(x_hi, 1)
                if n < 2:
                    split(0, n, n)
            with act.Fori(0, n_f // 2) as i:
                for j in range(2):
                    f = 2 * i + j
                    for half in range(2):
                        split(f + 1, half, 2 * f + half + 2)
                    act.wait_ge(s["used"], 2 * f + 2 + A)
                    act.activation(sg[j][:, :], k.bank[2 * j][:, :], ACT.Sigmoid).then_inc(s["sig"], 1)
                    hidden_hi(f, j)
            with act.Fori(0, n_f // 2 - 1) as i:
                for j in range(2):
                    split(n_f + 1 + i, j, n_up + 2 * i + j + 2)

        @block.vector
        def _(dve):
            def split(j, n):
                dve.wait_ge(s["hi"], n + 1 + A)
                dve.tensor_tensor(lo[j][:, :], raw[j][:, :], f32(hi[j][:, :]), ALU.subtract).then_inc(s["lo"], 1)

            for n in range(2 * MT):
                m, b = n // 2, n % 2
                dst = (slice(None), slice(4 * b, 4 * b + 4), slice(m * P, (m + 1) * P))
                dve.wait_ge(x_hi, n + 1)
                dve.tensor_tensor(xl[dst], k.bank[n][:, :].rearrange("p (q t) -> p q t", q=4), f32(xh[dst]),
                                  ALU.subtract).then_inc(x_lo, 1)
                if n < 2:
                    split(n, n)
            with dve.Fori(0, n_f // 2) as i:
                for j in range(2):
                    f = 2 * i + j
                    for half in range(2):
                        split(half, 2 * f + half + 2)
                    dve.wait_ge(s["sig"], f + 1 + A)
                    dve.wait_ge(s["hh"], f - 1 + A)
                    dve.tensor_tensor(sg[j][:, :], sg[j][:, :], k.bank[2 * j][:, :], ALU.mult).then_inc(s["part"], 1)
                    dve.wait_ge(s["part"], f + 1 + A)
                    dve.wait_ge(s["hl"], f - 1 + A)
                    dve.tensor_tensor(ht[j][:, :], sg[j][:, :], k.bank[2 * j + 1][:, :], ALU.mult).then_inc(s["h"], 1)
                    dve.wait_ge(s["hh"], f + 1 + A)
                    dve.tensor_tensor(flat(hl, f), ht[j][:, :], f32(flat(hh, f)), ALU.subtract).then_inc(s["hl"], 1)
            with dve.Fori(0, n_f // 2 - 1) as i:
                for j in range(2):
                    split(j, n_up + 2 * i + j + 2)
            for n in range(2 * MT):
                m, half = n % MT, 1 - n // MT
                if n < 2 * MT - 1:
                    dve.wait_ge(full, n + 1)
                else:
                    dve.wait_ge(s["used"], n_up + n_f + A)
                row = X[:, m, half * 512:half * 512 + 512]
                dve.scalar_tensor_tensor(out=row, in0=row, scalar=ALPHA, in1=k.bank[4 * half + m][:, :],
                                         op0=ALU.mult, op1=ALU.add).then_inc(added, 1)
    scope.close()


def embed(k, pe, pT, slab, full, read=None):
    slab_wait(k, pe, slab)
    w = k.slab(0, 2, 512)
    for m in range(MT):
        if read is not None:
            pe.wait_ge(read, m + 1)
        for kk in range(2):
            last = pe.matmul(k.bank[4 + m][:, :], pT[:, kk, m * P:(m + 1) * P], w[:, kk, :],
                             start=kk == 0, stop=kk == 1)
        last.then_inc(full, 1)


def embed_first_half(k, pT, full, rows):
    slab = k.slabs

    def work(pe):
        pe.wait_ge(k.rows, rows)
        embed(k, pe, pT, slab, full)
    return work


def phase_ple(k, tag, X, XT, pT, bias, tmp, weights, turn, nxt, rows, embedded):
    nc, io = k.nc, k.io
    s = {n: k.sem(f"{tag}_{n}") for n in ("gate", "biased", "sig", "mul", "added", "turned", "copied", "stored")}
    s["ple"] = embedded
    base = k.slabs
    k.slabs += 4
    with nc.Block() as block:
        @block.sync
        def _(sp):
            for n in (2, 3):
                sp.wait_ge(s["ple" if n == 2 else "gate"], MT)
                load_slab(k, sp, n % 2, weights(n))
            for n, src in enumerate(nxt):
                sp.wait_ge(s["ple" if n == 0 else "gate"], 2 * MT)
                load_slab(k, sp, n, src)
            if not turn:
                for m in range(MT):
                    sp.wait_ge(s["added"], MT + m + 1)
                    sp.dma_start(io["out"][0, m * P:(m + 1) * P, :], X[:, m, :]).then_inc(s["stored"], 16)
                sp.wait_ge(s["stored"], 16 * MT)

        @block.tensor
        def _(pe):
            pe.wait_ge(k.rows, rows)
            for h in range(2):
                if h:
                    embed(k, pe, pT, base + 2, embedded, read=s["mul"])
                slab_wait(k, pe, base + 2 * h + 1)
                w = k.slab(1, KT, 512)
                for m in range(MT):
                    for kk in range(KT):
                        last = pe.matmul(k.bank[m][:, :], XT[:, kk, m * P:(m + 1) * P], w[:, kk, :],
                                         start=kk == 0, stop=kk == KT - 1)
                    last.then_inc(s["gate"], 1)
            if turn:
                for m in range(MT):
                    pe.wait_ge(s["added"], MT + m + 1)
                    if m >= 2:
                        pe.wait_ge(s["copied"], 2 * (m - 1))
                    else:
                        pe.wait_ge(s["mul"], 2 * MT)
                    pe.wait_ge(s["biased"], 2 * MT)
                    for b in range(2):
                        bank = k.bank[4 + 2 * (m % 2) + b]
                        for q in range(4):
                            last = pe.transpose(bank[:, q * P:(q + 1) * P], X[:, m, (4 * b + q) * P:(4 * b + q + 1) * P],
                                                k.c("ident"))
                        last.then_inc(s["turned"], 1)

        @block.scalar
        def _(act):
            for n in range(2 * MT):
                act.wait_ge(s["biased"], n + 1)
                act.activation(tmp[:, n % 4, :], tmp[:, n % 4, :], ACT.Sigmoid).then_inc(s["sig"], 1)
            if turn:
                for m in range(MT):
                    for b in range(2):
                        act.wait_ge(s["turned"], 2 * m + b + 1)
                        act.activation(XT[:, 4 * b:4 * b + 4, m * P:(m + 1) * P],
                                       k.bank[4 + 2 * (m % 2) + b][:, :].rearrange("p (q t) -> p q t", q=4),
                                       ACT.Copy).then_inc(s["copied"], 1)

        @block.vector
        def _(dve):
            dve.wait_ge(k.rows, rows)
            for n in range(2 * MT):
                h, m = n // MT, n % MT
                cols = slice(h * 512, (h + 1) * 512)
                dve.wait_ge(s["gate"], n + 1)
                if h:
                    dve.wait_ge(s["added"], m + 1)
                dve.tensor_tensor(tmp[:, m, :], k.bank[m][:, :], bias[:, cols], ALU.add).then_inc(s["biased"], 1)
                dve.wait_ge(s["sig"], n + 1)
                dve.wait_ge(s["ple"], n + 1)
                dve.tensor_tensor(tmp[:, m, :], tmp[:, m, :], k.bank[4 + m][:, :], ALU.mult).then_inc(s["mul"], 1)
                dve.wait_ge(s["mul"], n + 1)
                dve.tensor_tensor(X[:, m, cols], X[:, m, cols], tmp[:, m, :], ALU.add).then_inc(s["added"], 1)


SM_GATEW, SM_PHI2, SM_PHI2V, SM_B1, SM_POS, SM_ROUTER, SM_BR = 0, 384, 640, 768, 772, 804, 868
SM_GATES, SM_WEIGHTS = 876, 1108
R8_VS, R8_VW, R8_ROT, R8_CMPM, R8_RANK, R8_KC, R8_VC = 0, 1024, 2048, 3072, 3328, 3392, 3456


def phase_kv_q(k, XT, nxt):
    nc, io = k.nc, k.io
    s = {n: k.sem("kvq_" + n) for n in ("tables", "full", "free", "rot", "cos", "sin", "done", "twins")}
    base = k.slabs
    k.slabs += 8
    qn, qr = k.act(2), k.act(3)
    four = lambda r, a, n: k.region(r, a, n * T).rearrange("p (k t) -> p k t", t=T)
    z = [four(4, 0, 2), four(4, 2 * T, 2)]
    ks, kw = four(4, 4 * T, 2), four(4, 6 * T, 2)
    vs = k.region(8, R8_VS, 1024).rearrange("p (m c) -> p m c", m=MT)
    vw = k.region(8, R8_VW, 1024).rearrange("p (m c) -> p m c", m=MT)
    rot = k.region(8, R8_ROT, 1024).rearrange("p (i t) -> p i t", i=2)
    z2 = k.region(6).rearrange("p (j a e t) -> p j a e t", j=2, a=2, e=2)
    gw = k.small[:, SM_GATEW:SM_GATEW + 384].rearrange("p (k c) -> p k c", k=KT)
    gates = k.small[:, SM_GATES:SM_GATES + 192]
    tmp = four(5, 0, 2)
    dst = [z[0][:, a, :] for a in range(2)] + [z[1][:, a, :] for a in range(2)] + [ks[:, a, :] for a in range(2)]
    dst += [vs[:, m, :] for m in range(MT)] + [kw[:, a, :] for a in range(2)] + [vw[:, m, :] for m in range(MT)]
    dst += [qn[:, f, :] for f in range(KT)]
    first = [0, 2, 4, 6, 10, 12, 16, 20, 24]
    turns = [(4 + a, ks[:, a, :], ks[:, a, :]) for a in range(2)] + [(10 + a, kw[:, a, :], kw[:, a, :]) for a in range(2)]
    turns += [(16 + f, qn[:, f, :], qr[:, f, :]) for f in range(KT)]

    with nc.Block() as block:
        @block.sync
        def _(sp):
            sp.dma_start(k.region(8, R8_ROT, 1024 + 256 + 64), io["tables"]).then_inc(s["tables"], 16)
            sp.dma_start(k.small[:, 0:SM_BR], io["nsa_small"]).then_inc(s["tables"], 16)
            sp.dma_start(k.small[:, SM_BR:SM_BR + NE], io["router_b"].to_broadcast([P, NE])).then_inc(s["tables"], 16)
            for n in range(2, 8):
                sp.wait_ge(s["full"], first[n - 1])
                load_slab(k, sp, n % 2, io["w_kv"][n] if n < 6 else io["w_q"][n - 6])
            for n, src in enumerate(nxt):
                sp.wait_ge(s["full"], first[7 + n])
                load_slab(k, sp, n, src)
            for j in range(2):
                sp.wait_ge(s["free"], 2 * j + 2)
                for e in range(2):
                    part = z[j][64 * e:64 * e + 64, :, :]
                    sp.dma_start(z2[0:64, j, :, e, :], part).then_inc(s["twins"], 16)
                    sp.dma_start(z2[64:128, j, :, e, 0:T - 1], part[:, :, 1:T]).then_inc(s["twins"], 16)
            sp.wait_ge(s["twins"], 16 * 8)

        @block.tensor
        def _(pe):
            n = [0, 0]

            def room():
                if n[0] >= 4:
                    pe.wait_ge(s["free"], n[0] - 3)
                n[0] += 1
                return k.bank[(n[0] - 1) % 4]

            def rotate(count):
                for _ in range(count):
                    t = n[1]
                    n[1] += 1
                    pe.wait_ge(s["free"], turns[t][0] + 1)
                    if t >= 4:
                        pe.wait_ge(s["sin"], t - 3)
                    pe.matmul(k.bank[4 + t % 4][:, :], k.c("rmat"), turns[t][1], start=True,
                              stop=True).then_inc(s["rot"], 1)

            for i in range(8):
                slab_wait(k, pe, base + i)
                if i in (3, 5):
                    w = k.slab(i, KT, 256)
                    for m in range(MT):
                        bank = room()
                        for kk in range(KT):
                            last = pe.matmul(bank[:, 0:256], XT[:, kk, m * P:(m + 1) * P], w[:, kk, :],
                                             start=kk == 0, stop=kk == KT - 1)
                        last.then_inc(s["full"], 1)
                    rotate(2)
                    continue
                cols = 256 if i < 6 else 512
                w = k.slab(i, KT, cols)
                for o in range(cols // P):
                    bank = room()
                    for kk in range(KT):
                        last = pe.matmul(bank[:, :], w[:, kk, o * P:(o + 1) * P], XT[:, kk, :],
                                         start=kk == 0, stop=kk == KT - 1)
                    last.then_inc(s["full"], 1)
                if i == 7:
                    rotate(4)
            bank = room()
            pe.wait_ge(s["tables"], 48)
            for m in range(MT):
                for kk in range(KT):
                    last = pe.matmul(bank[:, m * 48:(m + 1) * 48], XT[:, kk, m * P:(m + 1) * P], gw[:, kk, :],
                                     start=kk == 0, stop=kk == KT - 1)
            last.then_inc(s["full"], 1)
            rotate(4)

        @block.scalar
        def _(act):
            for t, d in enumerate(dst):
                act.wait_ge(s["full"], t + 1)
                act.activation(d, k.bank[t % 4][:, 0:d.shape[1]], ACT.Copy).then_inc(s["free"], 1)
            act.wait_ge(s["full"], len(dst) + 1)
            act.wait_ge(s["tables"], 48)
            act.activation(gates, k.bank[len(dst) % 4][:, 0:192], ACT.Sigmoid).then_inc(s["free"], 1)

        @block.vector
        def _(dve):
            dve.wait_ge(s["tables"], 48)
            for t, (tile, src, out) in enumerate(turns):
                dve.wait_ge(s["rot"], t + 1)
                if t >= 2:
                    dve.wait_ge(s["done"], t - 1)
                dve.tensor_tensor(tmp[:, t % 2, :], k.bank[4 + t % 4][:, :], rot[:, 1, :], ALU.mult).then_inc(s["sin"], 1)
                dve.wait_ge(s["free"], tile + 1)
                dve.tensor_tensor(out, src, rot[:, 0, :], ALU.mult).then_inc(s["cos"], 1)
                dve.wait_ge(s["sin"], t + 1)
                dve.wait_ge(s["cos"], t + 1)
                dve.tensor_tensor(out, out, tmp[:, t % 2, :], ALU.add).then_inc(s["done"], 1)


def phase_compress(k, nxt):
    nc = k.nc
    s = {n: k.sem("cmp_" + n) for n in ("hidden", "placed", "u", "sq", "cube", "tanh", "half", "act", "keys",
                                        "values", "zero", "out")}
    base = k.slabs
    k.slabs += 2
    z2 = k.region(6).rearrange("p (j g t) -> p j g t", j=2, g=NKV)
    n_col = NKV * NCMP
    pos = k.small[:, SM_POS:SM_POS + 32].rearrange("p (j i) -> p j i", j=2)
    b1 = k.small[:, SM_B1:SM_B1 + 4]
    placed = k.region(0, 0, 2 * 16 * n_col).rearrange("p (j i g n) -> p j i g n", j=2, i=16, g=NKV)
    w2k = k.small[:, SM_PHI2:SM_PHI2 + 256].rearrange("p (h c) -> p h c", h=2)
    w2v = k.small[:, SM_PHI2V:SM_PHI2V + 128].rearrange("p (h c) -> p h c", h=2)
    buf = lambda i: k.region(4, i * 512, 4 * n_col).rearrange("p (i c) -> p i c", i=4)
    u, v = buf(0), buf(1)
    g = buf(2)
    kc = k.region(8, R8_KC, 64).rearrange("p (a n) -> p a n", a=2)
    vc = k.region(8, R8_VC, 256)[0:CMPW, :]

    with nc.Block() as block:
        @block.sync
        def _(sp):
            for n, src in enumerate(nxt):
                sp.wait_ge(s["hidden"], 2 * n + 2)
                load_slab(k, sp, n, src)

        @block.tensor
        def _(pe):
            for j in range(2):
                slab_wait(k, pe, base + j)
                w = k.slab(j, 16, HID)
                for h in range(2):
                    for i in range(16):
                        pe.wait_ge(s["placed"], 16 * j + i + 1)
                        last = pe.matmul(k.bank[2 * j + h][:, 0:n_col], w[:, i, h * P:(h + 1) * P],
                                         placed[:, j, i].rearrange("p g n -> p (g n)"), start=i == 0, stop=i == 15)
                    last.then_inc(s["hidden"], 1)
            pe.wait_ge(s["act"], 1)
            for h in range(2):
                last = pe.matmul(k.bank[5][:, 0:n_col], w2k[:, h, :], g[:, h, :], start=h == 0, stop=h == 1)
            last.then_inc(s["keys"], 1)
            for q in range(NKV):
                for h in range(2):
                    last = pe.matmul(k.bank[6][0:NCMP, q * DH:(q + 1) * DH], g[:, 2 + h, q * NCMP:(q + 1) * NCMP],
                                     w2v[:, h, :], start=h == 0, stop=h == 1)
            last.then_inc(s["values"], 1)

        @block.vector
        def _(dve):
            dve.memset(kc, 0.0).then_inc(s["zero"], 1)
            dve.memset(vc, 0.0).then_inc(s["zero"], 1)
            for j in range(2):
                for i in range(16):
                    span = z2[:, j, :, 2 * i:2 * i + CMP_STRIDE * (NCMP - 1) + 1:CMP_STRIDE]
                    dve.tensor_scalar(placed[:, j, i], span, pos[:, j, i:i + 1], None, ALU.add).then_inc(s["placed"], 1)
            for i in range(4):
                dve.wait_ge(s["hidden"], i + 1)
                dve.tensor_scalar(u[:, i, :], k.bank[i][:, 0:n_col], b1[:, i:i + 1], None, ALU.add).then_inc(s["u"], 1)
            dve.wait_ge(s["u"], 4)
            dve.tensor_tensor(v, u, u, ALU.mult).then_inc(s["sq"], 1)
            dve.wait_ge(s["sq"], 1)
            dve.tensor_scalar(v, v, 0.044715, 1.0, ALU.mult, ALU.add).then_inc(s["sq"], 1)
            dve.wait_ge(s["sq"], 2)
            dve.tensor_tensor(v, v, u, ALU.mult).then_inc(s["cube"], 1)
            dve.wait_ge(s["tanh"], 1)
            dve.tensor_scalar(v, v, 0.5, 0.5, ALU.mult, ALU.add).then_inc(s["half"], 1)
            dve.wait_ge(s["half"], 1)
            dve.tensor_tensor(g, v, u, ALU.mult).then_inc(s["act"], 1)
            dve.wait_ge(s["keys"], 1)
            dve.wait_ge(s["zero"], 2)
            keys = k.bank[5][:, 0:n_col].rearrange("p (a e n) -> p a e n", a=2, e=2)
            for e in range(2):
                dve.tensor_copy(kc[64 * e:64 * e + 64, :, 0:NCMP], keys[64 * e:64 * e + 64, :, e, :]).then_inc(s["out"], 1)
            dve.wait_ge(s["values"], 1)
            dve.tensor_copy(vc[0:NCMP, :], k.bank[6][0:NCMP, 0:256]).then_inc(s["out"], 1)

        @block.scalar
        def _(act):
            act.wait_ge(s["cube"], 1)
            act.activation(v, v, ACT.Tanh, scale=math.sqrt(2.0 / math.pi)).then_inc(s["tanh"], 1)


def phase_attend(k):
    assert T // 64 <= 8 and T <= 512
    nc = k.nc
    A = 17
    s = {n: k.sem("att_" + n) for n in (
        "keys_ok", "values_ok", "q_in", "cs", "cadd", "cmax", "csub", "cexp", "czero", "ctotal", "cguard", "crec", "ccoef", "cnorm",
        "cturn", "cevac", "cout", "scores", "masked", "max", "neg", "exp", "turn", "evac", "out",
        "rec", "coef", "norm", "stored")}
    keys_in, values_in = k.sem("att_keys_in"), k.sem("att_values_in")
    qn, qr = k.act(2), k.act(3)
    four = lambda r, a, n: k.region(r, a, n * T).rearrange("p (k t) -> p k t", t=T)
    keys = [four(4, 4 * T, 2), four(4, 6 * T, 2)]
    vals = [k.region(8, R8_VS, 1024).rearrange("p (m c) -> p m c", m=MT),
            k.region(8, R8_VW, 1024).rearrange("p (m c) -> p m c", m=MT)]
    cm = k.region(8, R8_CMPM, 256).rearrange("p (i m n) -> p i m n", i=2, m=MT)
    kc = k.region(8, R8_KC, 64).rearrange("p (a n) -> p a n", a=2)
    vc = k.region(8, R8_VC, 256)[0:CMPW, :]
    attT = k.act(5)
    gates = k.small[:, SM_GATES:SM_GATES + 192].rearrange("p (m c) -> p m c", m=MT)
    Qn, Qr, K2 = k.region(6, 0, T), k.region(6, T, T), [k.region(6, 3328 - T, T), k.region(4, 1536, T)]
    Kc = k.region(6, 3328, CMPW)
    Pc = k.region(6, 3392, 256).rearrange("p (e m n) -> p e m n", e=2, m=MT)
    Pc8 = k.region(6, 3392, 256).rearrange("p (i n) -> p i n", i=8)
    V2 = k.region(4, 0, 1024).rearrange("p (b e m c) -> p b e m c", b=2, e=2, m=MT)
    Vc = k.region(4, 1024, 2 * DH)[0:CMPW, :]
    prob = [k.region(6, 1024, 1280), k.slots[1][:, 4096:5376]]
    pcT = k.slots[0][0:CMPW, 4096:5120].rearrange("p (i t) -> p i t", i=8)
    PT = [k.region(0, 2048 * i, 2048).rearrange("p (m t) -> p m t", m=MT) for i in range(2)]
    stat = k.region(6, 3904, 64)
    c8 = [stat[:, 8 * i:8 * i + 8] for i in range(3)]
    mx, sm, cf = ([stat[:, 24 + 8 * i + 4 * b:28 + 8 * i + 4 * b] for b in range(2)] for i in range(3))
    width = [P * (m + 1) for m in range(MT)]
    at_p = [0, P, 3 * P, 6 * P]
    items = [(0, 1), (2,), (3,)]
    tiles_up_to = [2, 3, 4]
    units = [(e, b) for e in range(2) for b in range(2)]
    score_bank = lambda u, i: (3 * u + i) % 4
    score_col = lambda m: P if m == 1 else 0

    with nc.Block() as block:
        @block.sync
        def _(sp):
            for each in s.values():
                sp.sem_inc(each, A)
            flat = lambda x, i: x[:, ds(i, 1), :].rearrange("p a t -> p (a t)")
            with sp.Fori(0, 2) as a:
                sp.wait_ge(s["scores"], 48 * a + A)
                sp.wait_ge(s["cs"], 8 * a + A)
                for dst, src in ((Kc, flat(kc, a)), (K2[0], flat(keys[0], a)), (K2[1], flat(keys[1], a))):
                    sp.dma_start(dst, src).then_inc(keys_in, 16)
                sp.wait_ge(keys_in, 48 * a + 48)
                sp.sem_inc(s["keys_ok"], NQ)
                sp.wait_ge(s["out"], 16 * a + A)
                sp.wait_ge(s["cout"], 8 * a + A)
                for b in range(2):
                    for e in range(2):
                        sp.dma_start(V2[:, b, e], vals[b][:, :, ds((2 * a + e) * DH, DH)]).then_inc(values_in, 16)
                sp.dma_start(Vc, vc[:, ds(2 * a * DH, 2 * DH)]).then_inc(values_in, 16)
                sp.wait_ge(values_in, 80 * a + 80)
                sp.sem_inc(s["values_ok"], NQ)

        @block.gpsimd
        def _(pool):
            flat = lambda x, i: x[:, ds(i, 1), :].rearrange("p a t -> p (a t)")
            with pool.Fori(0, 2) as a:
                with pool.Fori(0, NQ) as r:
                    f = 4 * a + r
                    pool.wait_ge(s["cs"], 2 * f + A)
                    pool.wait_ge(s["scores"], 12 * f + A)
                    pool.nop(nofuse=True)
                    for dst, src in ((Qr, flat(qr, f)), (Qn, flat(qn, f))):
                        pool.tensor_copy(dst, src).then_inc(s["q_in"], 1)

        @block.tensor
        def _(pe):
            def scores(f, u):
                e, b = units[u]
                rows = slice(64 * e, 64 * e + 64)
                if u == 0:
                    pe.wait_ge(s["keys_ok"], f + 1 + A)
                    pe.wait_ge(s["q_in"], 2 * f + 1 + A)
                for i, tiles in enumerate(items):
                    j = 3 * u + i - 4
                    before = 4 * (j // 3) + tiles_up_to[j % 3]
                    pe.wait_ge(s["exp"], 16 * f + before + A)
                    for m in tiles:
                        col = score_col(m)
                        last = pe.matmul(k.bank[score_bank(u, i)][:, col:col + width[m]],
                                         Qr[rows, m * P:(m + 1) * P], K2[b][rows, 0:width[m]],
                                         start=True, stop=True)
                    last.then_inc(s["scores"], 1)

            def turn(f, u):
                for i, tiles in enumerate(items):
                    pe.wait_ge(s["norm"], 16 * f + 4 * u + tiles_up_to[i] + A)
                    pe.wait_ge(s["evac"], 16 * f + 4 * u - 4 + tiles_up_to[i] + A)
                    if u == 0 and i > 0:
                        pe.wait_ge(s["cadd"], 2 * f + 2 + A)
                    if u == 1 and i < 2:
                        pe.wait_ge(s["cevac"], 2 * f + i + 1 + A)
                    for kb in range(tiles[-1] + 1):
                        for m in tiles:
                            if m >= kb:
                                at = kb + m - tiles[0]
                                c = at_p[m] + kb * P
                                last = pe.transpose(k.bank[4 + i][:, at * P:(at + 1) * P],
                                                    prob[u % 2][:, c:c + P], k.c("ident"))
                    last.then_inc(s["turn"], 1)

            def values(f, u):
                e, b = units[u]
                if u == 0:
                    pe.wait_ge(s["values_ok"], f + 1 + A)
                    pe.wait_ge(s["stored"], 2 * f - 1 + A)
                pe.wait_ge(s["evac"], 16 * f + 4 * u + 4 + A)
                for kb in range(MT):
                    last = pe.matmul(k.bank[7][64 * e:64 * e + 64, kb * P:T], V2[:, b, e, kb, :],
                                     PT[u % 2][:, kb, kb * P:T], start=u == 0 and kb == 0,
                                     stop=b == 1 and kb == MT - 1)
                last.then_inc(s["out"], 1)

            def compressed_values(f, e):
                pe.wait_ge(s["cevac"], 2 * f + e + 1 + A)
                if e == 1:
                    pe.wait_ge(s["stored"], 2 * f + A)
                pe.matmul(k.bank[7][64 * e:64 * e + 64, :], Vc[:, e * DH:(e + 1) * DH],
                          pcT[:, 4 * e:4 * e + 4, :].rearrange("p m t -> p (m t)"),
                          start=e == 1, stop=False).then_inc(s["cout"], 1)

            def compressed_scores(f):
                pe.wait_ge(s["q_in"], 2 * f + 2 + A)
                pe.wait_ge(s["evac"], 16 * f + A)
                for e in range(2):
                    for m in range(MT):
                        last = pe.matmul(k.bank[6 - e][:, m * CMPW:(m + 1) * CMPW],
                                         Qn[64 * e:64 * e + 64, m * P:(m + 1) * P], Kc[64 * e:64 * e + 64, :],
                                         start=True, stop=True)
                    last.then_inc(s["cs"], 1)

            def turn_compressed(f):
                pe.wait_ge(s["cnorm"], f + 1 + A)
                for i in range(8):
                    last = pe.transpose(k.bank[4 + i // 4][0:CMPW, (i % 4) * P:(i % 4 + 1) * P], Pc8[:, i, :],
                                        k.c("ident"))
                    if i % 4 == 3:
                        last.then_inc(s["cturn"], 1)

            def pair(f, more):
                compressed_scores(f)
                scores(f, 1)
                turn(f, 0)
                scores(f, 2)
                values(f, 0)
                turn_compressed(f)
                scores(f, 3)
                turn(f, 1)
                compressed_values(f, 0)
                values(f, 1)
                turn(f, 2)
                compressed_values(f, 1)
                values(f, 2)
                if more:
                    scores(f + 1, 0)
                turn(f, 3)
                values(f, 3)

            scores(0, 0)
            with pe.Fori(0, KT - 1) as f:
                pair(f, True)
            pair(KT - 1, False)

        @block.scalar
        def _(act):
            with act.Fori(0, 2) as a:
                with act.Fori(0, NQ) as r:
                    f = 4 * a + r

                    def exps(u):
                        act.wait_ge(s["turn"], 12 * f + 3 * u - 3 + A)
                        act.wait_ge(s["rec"], 4 * f + u - 1 + A)
                        for i, tiles in enumerate(items):
                            act.wait_ge(s["neg"], 12 * f + 3 * u + i + 1 + A)
                            for m in tiles:
                                col = score_col(m)
                                act.activation(prob[u % 2][:, at_p[m]:at_p[m] + width[m]],
                                               k.bank[score_bank(u, i)][:, col:col + width[m]], ACT.Exp,
                                               bias=mx[u % 2][:, m:m + 1], scale=SCALE,
                                               accum_out=sm[u % 2][:, m:m + 1]).then_inc(s["exp"], 1)

                    def evacs(u):
                        act.wait_ge(s["out"], 4 * f + u - 1 + A)
                        for i, tiles in enumerate(items):
                            bank = k.bank[4 + i]
                            act.wait_ge(s["turn"], 12 * f + 3 * u + i + 1 + A)
                            if i == 0:
                                parts = [(PT[u % 2][:, 0, 0:2 * P], bank[:, 0:2 * P]),
                                         (PT[u % 2][:, 1, P:2 * P], bank[:, 2 * P:3 * P])]
                            else:
                                m = tiles[0]
                                parts = [(PT[u % 2][:, 0:m + 1, m * P:(m + 1) * P],
                                          bank[:, 0:width[m]].rearrange("p (k t) -> p k t", t=P))]
                            for dst, src in parts:
                                act.activation(dst, src, ACT.Copy).then_inc(s["evac"], 1)

                    def store(e):
                        act.wait_ge(s["out"], 4 * f + 2 * e + 2 + A)
                        rows = slice(64 * e, 64 * e + 64)
                        act.activation(attT[rows, ds(f, 1), :].rearrange("p a t -> p (a t)"), k.bank[7][rows, :],
                                       ACT.Copy).then_inc(s["stored"], 1)

                    exps(0)
                    act.wait_ge(s["csub"], f + 1 + A)
                    act.activation(Pc8, Pc8, ACT.Exp, scale=SCALE).then_inc(s["cexp"], 1)
                    evacs(0)
                    exps(1)
                    exps(2)
                    act.wait_ge(s["cout"], 2 * f + A)
                    for i in range(2):
                        act.wait_ge(s["cturn"], 2 * f + i + 1 + A)
                        act.activation(pcT[:, 4 * i:4 * i + 4, :],
                                       k.bank[4 + i][0:CMPW, :].rearrange("p (i t) -> p i t", i=4),
                                       ACT.Copy).then_inc(s["cevac"], 1)
                    evacs(1)
                    exps(3)
                    evacs(2)
                    store(0)
                    evacs(3)
                    store(1)

        @block.vector
        def _(dve):
            with dve.Fori(0, 2) as a:
                with dve.Fori(0, NQ) as r:
                    f = 4 * a + r
                    head = lambda e: 8 * a + 4 * e + r
                    spread8 = lambda x: x.rearrange("p (i n) -> p i n", n=1).to_broadcast([P, 8, CMPW])
                    n1 = f + 1

                    def maxima(u):
                        for i, tiles in enumerate(items):
                            n = 12 * f + 3 * u + i + 1 + A
                            bank = k.bank[score_bank(u, i)]
                            dve.wait_ge(s["scores"], n)
                            if i == 0:
                                diag = bank[:, :].rearrange("p (i c) -> p i c", c=2 * P)[:, :, 0:P]
                                causal = k.c("causal").rearrange("p (i c) -> p i c", i=1).to_broadcast([P, 2, P])
                            else:
                                diag, causal = bank[:, width[tiles[0]] - P:width[tiles[0]]], k.c("causal")
                            dve.tensor_tensor(diag, diag, causal, ALU.add).then_inc(s["masked"], 1)
                            dve.wait_ge(s["masked"], n)
                            for m in tiles:
                                col = score_col(m)
                                dve.tensor_reduce(mx[u % 2][:, m:m + 1], bank[:, col:col + width[m]], AX.X,
                                                  ALU.max).then_inc(s["max"], 1)
                            dve.wait_ge(s["max"], 16 * f + 4 * u + tiles_up_to[i] + A)
                            both = mx[u % 2][:, tiles[0]:tiles[-1] + 1]
                            dve.tensor_scalar(both, both, -SCALE, None, ALU.mult).then_inc(s["neg"], 1)

                    def normalise(u):
                        e, b = units[u]
                        n = 4 * f + u
                        dve.wait_ge(s["exp"], 16 * f + 4 * u + 4 + A)
                        dve.reciprocal(cf[u % 2], sm[u % 2]).then_inc(s["rec"], 1)
                        dve.wait_ge(s["rec"], n + 1 + A)
                        dve.tensor_tensor(cf[u % 2], cf[u % 2], gates[:, :, ds(head(e) * 3 + 1 + b, 1)].rearrange(
                            "p m o -> p (m o)"), ALU.mult).then_inc(s["coef"], 1)
                        dve.wait_ge(s["coef"], n + 1 + A)
                        for m in range(MT):
                            mine = prob[u % 2][:, at_p[m]:at_p[m] + width[m]]
                            dve.tensor_scalar(mine, mine, cf[u % 2][:, m:m + 1], None, ALU.mult).then_inc(s["norm"], 1)

                    maxima(0)
                    dve.wait_ge(s["cturn"], 2 * f + A)
                    for e in range(2):
                        dve.wait_ge(s["cs"], 2 * f + e + 1 + A)
                        dve.tensor_tensor(Pc[:, e], k.bank[6 - e][:, 0:P].rearrange("p (m n) -> p m n", m=MT),
                                          cm[:, 0], ALU.add).then_inc(s["cadd"], 1)
                    dve.wait_ge(s["cadd"], 2 * f + 2 + A)
                    dve.tensor_reduce(c8[0], Pc8, AX.X, ALU.max).then_inc(s["cmax"], 1)
                    dve.wait_ge(s["cmax"], n1 + A)
                    dve.tensor_tensor(Pc8, Pc8, spread8(c8[0]), ALU.subtract).then_inc(s["csub"], 1)
                    normalise(0)
                    maxima(1)
                    dve.wait_ge(s["cexp"], n1 + A)
                    for e in range(2):
                        dve.tensor_tensor(Pc[:, e], Pc[:, e], cm[:, 1], ALU.mult).then_inc(s["czero"], 1)
                    dve.wait_ge(s["czero"], 2 * f + 2 + A)
                    dve.tensor_reduce(c8[1], Pc8, AX.X, ALU.add).then_inc(s["ctotal"], 1)
                    dve.wait_ge(s["ctotal"], n1 + A)
                    dve.tensor_scalar(c8[1], c8[1], 1e-30, None, ALU.max).then_inc(s["cguard"], 1)
                    dve.wait_ge(s["cguard"], n1 + A)
                    dve.reciprocal(c8[2], c8[1]).then_inc(s["crec"], 1)
                    dve.wait_ge(s["crec"], n1 + A)
                    for e in range(2):
                        dve.tensor_tensor(c8[2][:, 4 * e:4 * e + 4], c8[2][:, 4 * e:4 * e + 4],
                                          gates[:, :, ds(head(e) * 3, 1)].rearrange("p m o -> p (m o)"),
                                          ALU.mult).then_inc(s["ccoef"], 1)
                    dve.wait_ge(s["ccoef"], 2 * f + 2 + A)
                    dve.tensor_tensor(Pc8, Pc8, spread8(c8[2]), ALU.mult).then_inc(s["cnorm"], 1)
                    maxima(2)
                    normalise(1)
                    normalise(2)
                    maxima(3)
                    normalise(3)


def phase_route(k, XT):
    nc, io = k.nc, k.io
    s = {n: k.sem("route_" + n) for n in ("full", "chain", "exp", "picks", "counted")}
    ids_made, zeroed, tokens_out, indexed = (k.sem("route_" + n) for n in ("ids_made", "zeroed", "tokens_out", "indexed"))
    k.scattered = k.sem("route_scattered")
    ids = k.token_ids
    wr = k.small[:, SM_ROUTER:SM_ROUTER + 64].rearrange("p (k e) -> p k e", k=KT)
    br = k.small[:, SM_BR:SM_BR + NE].rearrange("p (m e) -> p m e", m=1).to_broadcast([P, MT, NE])
    lower = k.region(8, R8_RANK, 64).rearrange("p (e g) -> p e g", e=NE)
    at = lambda a, n: k.region(6, a, n)
    L = at(0, 32).rearrange("p (m e) -> p m e", m=MT)
    big = [at(512 * (i + 1), 256).rearrange("p (m e g) -> p m e g", m=MT, e=NE) for i in range(3)]
    rank, sel0, sel1, t = (at(64 + 64 * i, 32).rearrange("p (m e) -> p m e", m=MT) for i in range(4))
    l0, l1, den = (at(384 + 16 * i, 4) for i in range(3))
    picks, before, dest, zero = (at(2304 + 64 * i, 32).rearrange("p (m e) -> p m e", m=MT) for i in range(4))
    total, count, nblk, bend = (at(2560 + 16 * i, NE) for i in range(4))
    be = at(2624, 16)
    w0, w1 = k.small[:, SM_WEIGHTS:SM_WEIGHTS + 4], k.small[:, SM_WEIGHTS + 4:SM_WEIGHTS + 8]
    rows = k.small[:, SM_WEIGHTS + 8:SM_WEIGHTS + 16]

    with nc.Block() as block:
        @block.sync
        def _(sp):
            for m in range(MT):
                sp.dma_start(io["tokens"][m * P:(m + 1) * P, :], k.tok(1)[:, m, :]).then_inc(tokens_out, 16)
            sp.wait_ge(ids_made, 2)
            sp.dma_start(io["slots"].rearrange("(p b) o -> p (b o)", p=P), k.slot_token[:, :]).then_inc(zeroed, 16)
            sp.wait_ge(zeroed, 16)
            sp.wait_ge(tokens_out, 16 * MT)

        @block.gpsimd
        def _(pool):
            pool.wait_ge(zeroed, 16)
            pool.wait_ge(indexed, 1)
            for n in range(2 * MT):
                at_rows = bass.IndirectOffsetOnAxis(ap=k.row_index[:, n:n + 1], axis=0)
                pool.indirect_dma_start(io["slots"], at_rows, ids[:, n % MT:n % MT + 1], None
                                        ).then_inc(k.scattered, 16)

        @block.tensor
        def _(pe):
            for m in range(MT):
                for kk in range(KT):
                    last = pe.matmul(k.bank[0][:, m * NE:(m + 1) * NE], XT[:, kk, m * P:(m + 1) * P], wr[:, kk, :],
                                     start=kk == 0, stop=kk == KT - 1)
            last.then_inc(s["full"], 1)
            pe.wait_ge(s["picks"], 1)
            for m in range(MT):
                pe.matmul(k.bank[1][:, m * NE:(m + 1) * NE], k.c("tri"), picks[:, m], start=True, stop=False)
                pe.matmul(k.bank[1][:, m * NE:(m + 1) * NE], k.c("ones"), before[:, m], start=False, stop=True)
            pe.matmul(k.bank[2][:, 0:NE], k.c("ones"), total, start=True, stop=True).then_inc(s["counted"], 1)

        @block.scalar
        def _(act):
            act.wait_ge(s["chain"], 11)
            act.activation(l1, l1, ACT.Exp).then_inc(s["exp"], 1)

        @block.vector
        def _(dve):
            n = [0]

            def link(op):
                n[0] += 1
                op.then_inc(s["chain"], 1)
                dve.wait_ge(s["chain"], n[0])

            dve.tensor_copy(ids[:, :], k.c("ids")).then_inc(ids_made, 1)
            dve.memset(k.slot_token[:, :], 0).then_inc(ids_made, 1)
            dve.wait_ge(s["full"], 1)
            dve.memset(at(2304, 256), 0.0)
            link(dve.tensor_tensor(L, k.bank[0][:, 0:32].rearrange("p (m e) -> p m e", m=MT), br, ALU.add))
            for m in range(MT):
                mine = L[:, m].rearrange("p (e g) -> p e g", g=1).to_broadcast([P, NE, NE])
                other = L[:, m].rearrange("p (e g) -> p e g", e=1).to_broadcast([P, NE, NE])
                dve.tensor_tensor(big[0][:, m], other, mine, ALU.is_gt)
                op = dve.tensor_tensor(big[1][:, m], other, mine, ALU.is_equal)
            link(op)
            low = lower.rearrange("p e (m g) -> p m e g", m=1).to_broadcast([P, MT, NE, NE])
            link(dve.tensor_tensor(big[1], big[1], low, ALU.mult))
            link(dve.tensor_tensor(big[2], big[1], big[0], ALU.add))
            link(dve.tensor_reduce(rank, big[2], AX.X, ALU.add))
            dve.tensor_scalar(sel0, rank, 0.0, None, ALU.is_equal)
            link(dve.tensor_scalar(sel1, rank, 1.0, None, ALU.is_equal))
            link(dve.tensor_tensor(t, L, sel0, ALU.mult))
            link(dve.tensor_reduce(l0, t, AX.X, ALU.add))
            link(dve.tensor_tensor(t, L, sel1, ALU.mult))
            link(dve.tensor_reduce(l1, t, AX.X, ALU.add))
            link(dve.tensor_tensor(l1, l1, l0, ALU.subtract))
            dve.wait_ge(s["exp"], 1)
            link(dve.tensor_scalar(den, l1, 1.0, None, ALU.add))
            link(dve.reciprocal(den, den))
            link(dve.tensor_tensor(l1, l1, den, ALU.mult))
            dve.tensor_copy(w0, den)
            dve.tensor_copy(w1, l1)
            link(dve.tensor_tensor(picks, sel0, sel1, ALU.add))
            link(dve.tensor_tensor(before, zero, picks, ALU.mult))
            for m in range(1, MT):
                link(dve.tensor_tensor(before[:, m], before[:, m - 1], picks[:, m - 1], ALU.add))
            link(dve.tensor_tensor(total, before[:, MT - 1], picks[:, MT - 1], ALU.add))
            dve.engine_nop().then_inc(s["picks"], 1)
            dve.wait_ge(s["counted"], 1)
            link(dve.tensor_copy(count, k.bank[2][:, 0:NE]))
            link(dve.tensor_scalar(nblk, count, 0.0, None, ALU.is_gt))
            for j in range(1, MT):
                link(dve.scalar_tensor_tensor(out=nblk, in0=count, scalar=float(P * j), in1=nblk, op0=ALU.is_gt,
                                              op1=ALU.add))
            link(dve.tensor_tensor_scan(bend, k.c("ones")[:, 0:NE], nblk, 0.0, ALU.mult, ALU.add))
            link(dve.tensor_tensor(nblk, bend, nblk, ALU.subtract))
            link(dve.tensor_scalar(nblk, nblk, float(P), None, ALU.mult))
            start = nblk.rearrange("p (m e) -> p m e", m=1).to_broadcast([P, MT, NE])
            link(dve.tensor_tensor(dest, k.bank[1][:, 0:32].rearrange("p (m e) -> p m e", m=MT), start, ALU.add))
            for sel, row in ((sel0, rows[:, 0:4]), (sel1, rows[:, 4:8])):
                link(dve.tensor_tensor(t, dest, sel, ALU.mult))
                link(dve.tensor_reduce(row, t, AX.X, ALU.add))
            link(dve.tensor_copy(k.row_index[:, :], rows))
            dve.engine_nop().then_inc(indexed, 1)
            blocks = k.c("iota")[:, 0:16].rearrange("p (b e) -> p b e", e=1).to_broadcast([P, 16, NE])
            ends = bend.rearrange("p (b e) -> p b e", b=1).to_broadcast([P, 16, NE])
            past = at(2048, 128).rearrange("p (b e) -> p b e", b=16)
            link(dve.tensor_tensor(past, ends, blocks, ALU.is_le))
            link(dve.tensor_reduce(be, past, AX.X, ALU.add))
            link(dve.tensor_scalar(be, be, float(NE - 1), None, ALU.min))
            link(dve.tensor_copy(k.block_expert[:, :], be))


def phase_experts(k):
    nc, io = k.nc, k.io
    n_f = D_FFE // P
    U = 3 * n_f
    RING = n_f
    A = RING + 1
    s = {n: k.sem("moe_" + n) for n in (
        "picked", "rows_free", "rows_turned", "gh", "gl", "hi", "lo", "used",
        "sig", "part", "h", "turn", "th", "tl", "y", "y_out")}
    raw_in = [k.sem(f"moe_raw{i}") for i in range(RING)]
    stored, rows_in, slots_in = (k.sem("moe_" + n) for n in ("stored", "rows_in", "slots_in"))
    scope = ExitStack()
    hold = lambda name, n, dt=F32: scope.enter_context(nc.sbuf_tensor("moe_" + name, [P, n], dt))
    f32 = lambda ap: ap.bitcast(F32)
    raw = [hold(f"raw{i}", D) for i in range(RING)]
    hi, lo = ([hold(f"{p}{i}", D, F32R) for i in range(RING)] for p in ("hi", "lo"))
    picked, rows = hold("picked", 1, I32), hold("rows", D)
    gh, gl = hold("gh", KT * P, F32R), hold("gl", KT * P, F32R)
    h, sg = hold("h", D_FFE), hold("sg", 2 * P)
    th, tl = hold("th", D_FFE, F32R), hold("tl", D_FFE, F32R)
    y = hold("y", D)
    slab_done = lambda x: 2 * x + 2

    def each_block(eng):
        return eng.Fori(0, NBLK)

    with nc.Block() as block:
        @block.sync
        def _(sp):
            for each in s.values():
                sp.sem_inc(each, A)

            def load(b, u, e):
                sp.wait_ge(s["lo"], U * b + u - RING + 1 + A)
                if u < 2 * n_f:
                    src = io["m_up"][ds(e * n_f + u // 2, 1), :, u % 2 * D:(u % 2 + 1) * D]
                else:
                    src = io["m_down"][ds(e * n_f + u - 2 * n_f, 1)]
                sp.dma_start(raw[u % RING][:, :], src.rearrange("a p c -> (a p) c")).then_inc(raw_in[u % RING], 16)

            e0 = sp.value_load(k.block_expert[0:1, 0:1], min_val=0, max_val=NE - 1)
            for u in range(RING):
                if u == 4:
                    sp.wait_ge(k.scattered, 16 * 2 * MT)
                load(0, u, e0)
            with each_block(sp) as b:
                e = sp.value_load(k.block_expert[0:1, ds(b, 1)], min_val=0, max_val=NE - 1)
                nxt = sp.value_load(k.block_expert[0:1, ds(b + 1, 1)], min_val=0, max_val=NE - 1)
                for u in range(RING, U):
                    load(b, u, e)
                for u in range(RING):
                    load(b + 1, u, nxt)
            for each in raw_in:
                sp.wait_ge(each, 16 * (U // RING * NBLK + 1))

        @block.gpsimd
        def _(pool):
            def gather(b):
                pool.wait_ge(s["rows_free"], b + A)
                pool.nop(nofuse=True)
                pool.tensor_copy(picked[:, :], k.slot_token[:, ds(b, 1)]).then_inc(s["picked"], 1)
                pool.wait_ge(s["picked"], b + 1 + A)
                pool.nop(nofuse=True)
                pool.indirect_dma_start(rows[:, :], None, io["tokens"],
                                        bass.IndirectOffsetOnAxis(ap=picked[:, 0:1], axis=0)).then_inc(rows_in, 16)

            pool.wait_ge(k.scattered, 16 * 2 * MT)
            pool.dma_start(k.slot_token[:, :], io["slots"].rearrange("(b p) o -> p (b o)", p=P),
                           allow_slow_non_contiguous=True).then_inc(slots_in, 16)
            pool.wait_ge(slots_in, 16)
            gather(0)
            with each_block(pool) as b:
                gather(b + 1)
                pool.wait_ge(s["y"], 2 * b + 2 + A)
                pool.nop(nofuse=True)
                pool.dma_start(io["rows_y"][ds(b * P, P), :], y[:, :]).then_inc(stored, 16)
                pool.wait_ge(stored, 16 * b + 16)
                pool.sem_inc(s["y_out"], 1)
            pool.wait_ge(rows_in, 16 * NBLK + 16)
            pool.wait_ge(stored, 16 * NBLK)

        @block.tensor
        def _(pe):
            def turn_rows(b):
                pe.wait_ge(rows_in, 16 * b + 16)
                pe.wait_ge(s["gl"], 2 * b + A)
                for i in range(2):
                    for q in range(4):
                        f = 4 * i + q
                        last = pe.transpose(k.bank[6 + i][:, q * P:(q + 1) * P], rows[:, f * P:(f + 1) * P],
                                            k.c("ident"))
                    last.then_inc(s["rows_turned"], 1)

            def turn(b, i):
                n = min(4, n_f - 4 * i)
                pe.wait_ge(s["h"], n_f * b + 4 * i + n + A)
                pe.wait_ge(s["tl"], 3 * b + (1 if i == 2 else 0) + A)
                for q in range(n):
                    last = pe.transpose(k.bank[4 + i % 2][:, q * P:(q + 1) * P],
                                        h[:, (4 * i + q) * P:(4 * i + q + 1) * P], k.c("ident"))
                last.then_inc(s["turn"], 1)

            turn_rows(0)
            with each_block(pe) as b:
                pe.wait_ge(s["gl"], 2 * b + 2 + A)
                for u in range(2 * n_f):
                    x = u // 2
                    pe.wait_ge(s["lo"], U * b + u + 1 + A)
                    if x >= 2 and u % 2 == 0:
                        pe.wait_ge(s["h"], n_f * b + x - 1 + A)
                    out = k.bank[x % 2][:, 0:2 * P]
                    wh, wl = hi[u % RING], lo[u % RING]
                    for kk in range(KT // 2):
                        first, end = u % 2 == 0 and kk == 0, u % 2 == 1 and kk == KT // 2 - 1
                        cols = slice((u % 2 * 4 + kk) * P, (u % 2 * 4 + kk + 1) * P)
                        w = slice(kk * 2 * P, (kk + 1) * 2 * P)
                        pe.matmul(out, gh[:, cols], wh[:, w], start=first, stop=False)
                        pe.matmul(out, gh[:, cols], wl[:, w], start=False, stop=False)
                        last = pe.matmul(out, gl[:, cols], wh[:, w], start=False, stop=end)
                    last.then_inc(s["used"], 1)
                    if u == 13:
                        turn(b, 0)
                turn(b, 1)
                turn_rows(b + 1)
                turn(b, 2)
                for x in range(n_f):
                    u = 2 * n_f + x
                    pe.wait_ge(s["lo"], U * b + u + 1 + A)
                    pe.wait_ge(s["tl"], 3 * b + x // 4 + 1 + A)
                    if x == 0:
                        pe.wait_ge(s["y"], 2 * b + A)
                    cols = slice(x * P, (x + 1) * P)
                    for a, w in ((th, hi), (th, lo), (tl, hi)):
                        for i in range(2):
                            last = pe.matmul(k.bank[2 + i][:, :], a[:, cols], w[u % RING][:, i * 512:(i + 1) * 512],
                                             start=x == 0 and a is th and w is hi, stop=x == n_f - 1 and a is tl)
                    last.then_inc(s["used"], 1)

        @block.scalar
        def _(act):
            def split(b, u):
                act.wait_ge(raw_in[u % RING], 16 * (U // RING * b + u // RING + 1))
                act.wait_ge(s["used"], U * b + u - RING + 1 + A)
                act.activation(hi[u % RING][:, :], raw[u % RING][:, :], ACT.Copy).then_inc(s["hi"], 1)

            def sigmoid(b, x):
                act.wait_ge(s["used"], U * b + slab_done(x) + A)
                act.wait_ge(s["h"], n_f * b + max(x - 1, 0) + A)
                act.activation(sg[:, x % 2 * P:(x % 2 + 1) * P], k.bank[x % 2][:, 0:P],
                               ACT.Sigmoid).then_inc(s["sig"], 1)

            def gathered(b, i):
                act.wait_ge(s["rows_turned"], 2 * b + i + 1 + A)
                if i == 1:
                    act.sem_inc(s["rows_free"], 1)
                act.activation(gh[:, i * 512:(i + 1) * 512], k.bank[6 + i][:, :], ACT.Copy).then_inc(s["gh"], 1)

            def turned(b, i):
                n = min(4, n_f - 4 * i) * P
                act.wait_ge(s["turn"], 3 * b + i + 1 + A)
                act.wait_ge(s["used"], U * b + A)
                act.activation(th[:, i * 512:i * 512 + n], k.bank[4 + i % 2][:, 0:n], ACT.Copy).then_inc(s["th"], 1)

            for u in range(RING):
                split(0, u)
            for i in range(2):
                gathered(0, i)
            with each_block(act) as b:
                for u in range(RING, U):
                    if (u - RING) % 2 == 1:
                        sigmoid(b, (u - RING) // 2)
                    split(b, u)
                    if u == 27:
                        turned(b, 0)
                turned(b, 1)
                for i in range(2):
                    gathered(b + 1, i)
                turned(b, 2)
                for u in range(RING):
                    split(b + 1, u)
                act.wait_ge(s["y_out"], b + A)
                for i in range(2):
                    act.wait_ge(s["used"], U * b + U + A)
                    act.activation(y[:, i * 512:(i + 1) * 512], k.bank[2 + i][:, :], ACT.Copy).then_inc(s["y"], 1)

        @block.vector
        def _(dve):
            def split(b, u):
                dve.wait_ge(s["hi"], U * b + u + 1 + A)
                dve.tensor_tensor(lo[u % RING][:, :], raw[u % RING][:, :], f32(hi[u % RING][:, :]),
                                  ALU.subtract).then_inc(s["lo"], 1)

            def hidden(b, x):
                mine = sg[:, x % 2 * P:(x % 2 + 1) * P]
                dve.wait_ge(s["sig"], n_f * b + x + 1 + A)
                dve.tensor_tensor(mine, mine, k.bank[x % 2][:, 0:P], ALU.mult).then_inc(s["part"], 1)
                dve.wait_ge(s["part"], n_f * b + x + 1 + A)
                dve.wait_ge(s["turn"], 3 * b + A)
                dve.tensor_tensor(h[:, x * P:(x + 1) * P], mine, k.bank[x % 2][:, P:2 * P],
                                  ALU.mult).then_inc(s["h"], 1)

            def gathered(b, i):
                dve.wait_ge(s["gh"], 2 * b + i + 1 + A)
                mine = slice(i * 512, (i + 1) * 512)
                dve.tensor_tensor(gl[:, mine], k.bank[6 + i][:, :], f32(gh[:, mine]), ALU.subtract).then_inc(s["gl"], 1)

            def turned(b, i):
                n = min(4, n_f - 4 * i) * P
                dve.wait_ge(s["th"], 3 * b + i + 1 + A)
                dve.tensor_tensor(tl[:, i * 512:i * 512 + n], k.bank[4 + i % 2][:, 0:n],
                                  f32(th[:, i * 512:i * 512 + n]), ALU.subtract).then_inc(s["tl"], 1)

            for u in range(RING):
                split(0, u)
            for i in range(2):
                gathered(0, i)
            with each_block(dve) as b:
                for u in range(RING, U):
                    if (u - RING) % 2 == 1:
                        hidden(b, (u - RING) // 2)
                    split(b, u)
                    if u == 27:
                        turned(b, 0)
                turned(b, 1)
                for i in range(2):
                    gathered(b + 1, i)
                turned(b, 2)
                for u in range(RING):
                    split(b + 1, u)
    scope.close()


def phase_collect(k, X, first, second, nxt):
    nc, io = k.nc, k.io
    scaled, one, both = (k.sem("collect_" + n) for n in ("scaled", "one", "both"))
    rows = [k.sem(f"collect_rows{m}") for m in range(MT)]
    w = k.small[:, SM_WEIGHTS:SM_WEIGHTS + 8]
    with nc.Block() as block:
        @block.gpsimd
        def _(pool):
            for m in range(MT):
                for j, dst in enumerate((first, second)):
                    at = bass.IndirectOffsetOnAxis(ap=k.row_index[:, 4 * j + m:4 * j + m + 1], axis=0)
                    pool.indirect_dma_start(dst[:, m, :], None, io["rows_y"], at).then_inc(rows[m], 16)

        @block.sync
        def _(sp):
            for each in rows:
                sp.wait_ge(each, 32)
            for n, src in enumerate(nxt):
                load_slab(k, sp, n, src)
            flat = io["rows"].rearrange("(o r) d -> o (r d)", o=1)
            sp.dma_start(k.region(7, 2 * D, 2 * D), flat[:, 6 * D:8 * D].to_broadcast([P, 2 * D])).then_inc(k.rows, 16)
            sp.dma_start(k.region(5, D, D), flat[:, 9 * D:10 * D].to_broadcast([P, D])).then_inc(k.rows, 16)
            sp.dma_start(k.region(5, 2 * D, 2 * T), io["pT"][1]).then_inc(k.rows, 16)

        @block.vector
        def _(dve):
            for m in range(MT):
                dve.wait_ge(rows[m], 32)
                dve.wait_ge(scaled, m + 1)
                dve.scalar_tensor_tensor(out=X[:, m, :], in0=first[:, m, :], scalar=w[:, m:m + 1], in1=X[:, m, :],
                                         op0=ALU.mult, op1=ALU.add).then_inc(one, 1)
                dve.wait_ge(one, m + 1)
                dve.scalar_tensor_tensor(out=X[:, m, :], in0=second[:, m, :], scalar=w[:, 4 + m:5 + m],
                                         in1=X[:, m, :], op0=ALU.mult, op1=ALU.add).then_inc(both, 1)

        @block.scalar
        def _(act):
            for m in range(MT):
                act.activation(X[:, m, :], X[:, m, :], ACT.Copy, scale=ALPHA).then_inc(scaled, 1)


def build(nc, io):
    with ExitStack() as ctx:
        k = Core(nc, ctx, io)
        k.open_arena("a")
        phase_project(k)
        phase_scale(k)
        phase_recurrence(k)
        phase_gate(k)
        X, XT = k.tok(1), k.act(0)
        row = lambda r, i: k.region(r, i * D, D)
        phase_out_norm(k, "mixa", k.act(3), io["w_o_a"], [KT], X, row(6, 0), row(6, 1), rows=2)
        k.close_arena()
        phase_ffn(k, X)
        k.clear_sems()
        k.open_arena("b")
        XT = k.act(0)
        pT = lambda r, a: k.region(r, a, 2 * T).rearrange("p (k t) -> p k t", k=2)
        embedded = [k.sem("ple0_embedded"), None]
        ple = lambda l: lambda n: io["ple_w"][l, n // 2] if n % 2 == 0 else io["ple_g"][l, n // 2]

        def second_rows(sp):
            flat = io["rows"].rearrange("(o r) d -> o (r d)", o=1)
            for dst, src in ((k.region(6, 2 * D, 2 * D), flat[:, 2 * D:4 * D].to_broadcast([P, 2 * D])),
                             (k.region(5, D, D), flat[:, 8 * D:9 * D].to_broadcast([P, D])),
                             (k.region(5, 2 * D, 2 * T), io["pT"][0]),
                             (k.region(7, 0, 2 * D), flat[:, 4 * D:6 * D].to_broadcast([P, 2 * D]))):
                sp.dma_start(dst, src).then_inc(k.rows, 16)

        phase_out_norm(k, "ffn_ln", None, None, [], X, row(6, 2), row(6, 3), XT, nxt=[ple(0)(n) for n in range(2)],
                       rows=6, load=second_rows, before=embed_first_half(k, pT(5, 2 * D), embedded[0], 16 * 6))
        phase_ple(k, "ple0", X, XT, pT(5, 2 * D), row(5, 1), k.region(8, 0, 2048).rearrange("p (m t) -> p m t", m=4),
                  ple(0), True, [io["w_kv"][n] for n in range(2)], 16 * 6, embedded[0])
        k.clear_sems()
        phase_kv_q(k, XT, nxt=[io["phi_w1"][n] for n in range(2)])
        phase_compress(k, nxt=[io["w_o_b"][n] for n in range(2)])
        phase_attend(k)
        phase_out_norm(k, "mixb", k.act(5), io["w_o_b"], [KT], X, row(7, 0), row(7, 1), XT, rows=6)
        phase_route(k, XT)
        k.close_arena()
        phase_experts(k)
        k.clear_sems()
        k.open_arena("c")
        XT = k.act(0)
        embedded[1] = k.sem("ple1_embedded")
        phase_collect(k, X, k.tok(4), k.tok(3), nxt=[ple(1)(n) for n in range(2)])
        phase_out_norm(k, "moe", None, None, [], X, row(7, 2), row(7, 3), XT, rows=9,
                       before=embed_first_half(k, pT(5, 2 * D), embedded[1], 16 * 9))
        phase_ple(k, "ple1", X, XT, pT(5, 2 * D), row(5, 1), k.region(8, 0, 2048).rearrange("p (m t) -> p m t", m=4),
                  ple(1), False, [], 16 * 9, embedded[1])
        k.close_arena()


def constants():
    c = np.zeros((P, NCONST), np.float32)
    i, j = np.arange(P)[:, None], np.arange(P)[None, :]
    same = i // CH == j // CH
    put = lambda name, a: c.__setitem__((slice(None), slice(CONST[name][0], CONST[name][0] + CONST[name][1])), a)
    put("ident", i == j)
    put("bones", same)
    put("strict", same & (i < j))
    levels = []
    for m in (1, 2, 4, 8, 16, 32):
        levels.append((i // (2 * m) == j // (2 * m)) & (i // m % 2 == 0) & (j // m % 2 == 1))
    put("lev", np.concatenate(levels, 1))
    put("incl", i % CH <= np.arange(CH)[None, :])
    half = DH // 2
    rm = np.zeros((P, P), np.float32)
    for o in range(P):
        b, r = o // DH * DH, o % DH
        rm[b + (r + half) % DH, o] = -1.0 if r < half else 1.0
    put("rmat", rm)
    put("causal", np.where(j <= i, 0.0, NEG))
    put("mhalf", -0.5)
    put("tri", i < j)
    put("ones", 1.0)
    head = 2 * np.arange(KT)[None, :] + i // DH
    pick = head[:, :, None] == np.arange(NH)
    put("pick", pick.reshape(P, -1))
    put("spread", np.concatenate([pick.transpose(2, 1, 0).reshape(NH, -1), np.zeros((P - NH, KT * P))]))
    put("ids", P * np.arange(MT)[None, :] + i)
    put("iota", np.broadcast_to(np.arange(P, dtype=np.float32), (P, P)))
    put("reset", np.broadcast_to((np.arange(T) % CH != 0).astype(np.float32), (P, T)))
    return c


def tables():
    half = DH // 2
    inv = np.float32(10000.0) ** (-np.arange(half, dtype=np.float32) / np.float32(half))
    ang = np.arange(T, dtype=np.float32)[None, :] * inv[np.arange(P) % half][:, None]
    rot = np.stack([np.cos(ang), np.sin(ang)], 1).astype(np.float32)
    t = (np.arange(MT)[None, :, None] * P + np.arange(P)[:, None, None])
    ok = (np.arange(CMPW) * CMP_STRIDE + CMP_LEN - 1 <= t) & (np.arange(CMPW) < NCMP)
    cmp = np.stack([np.where(ok, 0.0, NEG), ok], 1).astype(np.float32)
    rank = np.broadcast_to((np.arange(NE)[None, :] < np.arange(NE)[:, None]).astype(np.float32).reshape(1, -1), (P, 64))
    return np.ascontiguousarray(np.concatenate([rot.reshape(P, -1), cmp.reshape(P, -1), rank], 1))


def slabs(w, kt, cols):
    w = np.asarray(w)
    return np.ascontiguousarray(w.reshape(kt, P, -1, cols).transpose(2, 1, 0, 3))


def layout(i):
    g = {n: np.asarray(a) for n, a in i.items()}
    feat = lambda v: v.reshape(KT, P).T
    o = {"const": constants(), "tables": tables()}
    mu = g["a_mu"][0]
    o["vec"] = np.ascontiguousarray(np.concatenate(
        [feat(mu[m]) for m in range(6)] + [feat(g[n][0]) for n in
         ("a_w0", "a_a0", "a_k_k", "a_k_a", "a_r_k", "a_gn_g", "a_gn_b")], 1))
    x = g["x"][0]
    o["x"] = x
    o["xT"] = np.ascontiguousarray(x.T.reshape(KT, P, T).transpose(1, 0, 2).reshape(P, -1))
    o["lora_in"] = slabs(np.concatenate([g["a_w1"][0], g["a_a1"][0], g["a_g1"][0]], 1), KT, 256).reshape(P, -1)
    o["lora_out"] = np.ascontiguousarray(np.concatenate([g["a_w2"][0], g["a_a2"][0]], 1))
    o["g2"] = g["a_g2"][0]
    o["w_rkv"] = np.concatenate([slabs(g["a_w_rkv"][0, m], KT, 512) for m in range(3)])
    o["w_o_a"] = slabs(g["a_w_o"][0], KT, 512)
    o["rows"] = np.ascontiguousarray(np.concatenate(
        [np.stack([g["ln_g"][l, j], g["ln_b"][l, j]]) for l in range(DEPTH) for j in range(2)] + [g["ple_gate_b"]]))
    o["pT"] = np.ascontiguousarray(g["p"][:, 0].transpose(0, 2, 1).reshape(DEPTH, 2, P, T).transpose(0, 2, 1, 3)
                                   .reshape(DEPTH, P, 2 * T))
    gu = lambda w, f: np.stack([w[:, :f].reshape(D, f // P, P), w[:, f:].reshape(D, f // P, P)], 2).reshape(D, -1)
    o["w_up"] = slabs(gu(g["f_w_gu"][0], D_FF), KT, 256).reshape(-1, P, UPW)
    o["w_down"] = g["f_w_down"][0].reshape(-1, P, D)
    o["ple_w"] = np.stack([slabs(g["ple_w"][l], 2, 512) for l in range(DEPTH)])
    o["ple_g"] = np.stack([slabs(g["ple_gate_w"][l], KT, 512) for l in range(DEPTH)])
    o["w_kv"] = slabs(g["b_w_kv"], KT, 256)
    order = [(2 * a + e) * NQ + r for a in range(2) for r in range(NQ) for e in range(2)]
    wq = g["b_w_in"][0][:, :D].reshape(D, 2 * KT, DH)[:, order].reshape(D, D)
    o["w_q"] = slabs(wq, KT, 512)
    o["phi_w1"] = slabs(np.concatenate([g["b_phi_w1"][0], g["b_phi_w1"][1]], 1), 16, HID)
    tile = lambda w: w.reshape(-1, P, w.shape[-1]).transpose(1, 0, 2).reshape(P, -1)
    w2 = g["b_phi_w2"]
    o["nsa_small"] = np.ascontiguousarray(np.concatenate(
        [tile(g["b_w_in"][0][:, D:]), tile(np.concatenate([w2[0], w2[0]], 1)), tile(w2[1]),
         g["b_phi_b1"].reshape(4, P).T, g["b_cmp_pos"].reshape(32, P).T, tile(g["m_w_router"][0])], 1))
    o["router_b"] = g["m_b_router"]
    pairs = g["b_w_o"][0].reshape(2, 2, NQ, DH, D).transpose(0, 2, 1, 3, 4).reshape(D, D)
    o["w_o_b"] = slabs(pairs, KT, 512)
    o["m_up"] = np.concatenate([slabs(gu(g["m_w_gu"][0, e], D_FFE), KT, 256) for e in range(NE)]).reshape(-1, P, UPW)
    o["m_down"] = g["m_w_down"][0].reshape(-1, P, D)
    return o


def kernel(**inputs):
    import concourse.bacc as bacc
    from concourse.bass_utils import run_bass_kernel_spmd

    nc = bacc.Bacc("TRN2", target_bir_lowering=False, num_devices=1)
    arrays = layout(inputs)
    io = {n: nc.dram_tensor("in_" + n, a.shape, F32, kind="ExternalInput").ap() for n, a in arrays.items()}
    io["out"] = nc.dram_tensor("out", (1, T, D), F32, kind="ExternalOutput").ap()
    io["tokens"] = nc.dram_tensor("tokens", (T, D), F32).ap()
    io["slots"] = nc.dram_tensor("slots", (16 * P, 1), I32).ap()
    io["rows_y"] = nc.dram_tensor("rows_y", (NBLK * P, D), F32).ap()
    build(nc, io)
    r = run_bass_kernel_spmd(nc, [{"in_" + n: a for n, a in arrays.items()}], core_ids=[0])
    return np.asarray(r.results[0]["out"])
```
